# Optimizing a Trainium2 kernel written in Bass

```python
import jax, jax.numpy as jnp
from jax import lax
import numpy as np

D_MODEL = 1024
BATCH = 1
SEQ = 1024
DEPTH = 1

GRID_W = 64
CTX_LEN = 256
EPS = 1e-6
POS_BASE = 10000.0
ML_WIDTH = D_MODEL // 2
N_ML_HEADS = 4
ML_HEAD_DIM = ML_WIDTH // N_ML_HEADS
ML_CHUNK = 64
CONV_W = 3
N_ML_GATES = 4 * N_ML_HEADS
GLA_V_WIDTH = D_MODEL - ML_WIDTH
GLA_K_WIDTH = GLA_V_WIDTH // 2
N_GLA_HEADS = 4
GLA_KEY_DIM = GLA_K_WIDTH // N_GLA_HEADS
GLA_VAL_DIM = GLA_V_WIDTH // N_GLA_HEADS
GLA_RANK = 16
GLA_GATE_TAU = 16.0
GLA_CHUNK = 16
N_EXPERTS = 16
EC_FACTOR = 2
D_EXPERT = D_MODEL
OFF_ML_Q = 0
OFF_ML_K = OFF_ML_Q + ML_WIDTH
OFF_ML_V = OFF_ML_K + ML_WIDTH
OFF_ML_O = OFF_ML_V + ML_WIDTH
OFF_ML_G = OFF_ML_O + ML_WIDTH
OFF_GLA_Q = OFF_ML_G + N_ML_GATES
OFF_GLA_K = OFF_GLA_Q + GLA_K_WIDTH
OFF_GLA_V = OFF_GLA_K + GLA_K_WIDTH
OFF_GLA_R = OFF_GLA_V + GLA_V_WIDTH
OFF_GLA_A = OFF_GLA_R + GLA_V_WIDTH
PROJ_WIDTH = OFF_GLA_A + 2 * GLA_RANK

kernel_name = "hybrid_mlstm_gla_ec_moe_prefix_dit"

def rms_norm(x, g):
    x32 = x.astype(jnp.float32)
    y = x32 * lax.rsqrt(jnp.mean(x32 * x32, axis=-1, keepdims=True) + EPS)
    return y.astype(x.dtype) * g

def head_rms_norm(h, g, n_heads):
    b, t, w = h.shape
    return rms_norm(h.reshape(b, t, n_heads, w // n_heads), g.reshape(n_heads, w // n_heads)).reshape(b, t, w)

def modulate(h, shift, scale):
    return h * (1 + scale) + shift

def dw_conv(x, w):
    pad = CONV_W // 2
    t = x.shape[1]
    xp = jnp.pad(x, ((0, 0), (pad, pad), (0, 0)))
    return sum(xp[:, j:j + t] * w[j] for j in range(CONV_W))

def to_heads(x, n_heads):
    b, t, w = x.shape
    return x.reshape(b, t, n_heads, w // n_heads).transpose(0, 2, 1, 3).astype(jnp.float32)

def from_heads(x, dtype):
    b, h, t, d = x.shape
    return x.transpose(0, 2, 1, 3).reshape(b, t, h * d).astype(dtype)

def chunk(x, size):
    return x.reshape(x.shape[:2] + (x.shape[2] // size, size) + x.shape[3:])

def flip_time(xs):
    return tuple(None if t is None else jnp.flip(t, axis=2) for t in xs)

def mlstm_states(k, v, log_i, log_f, state):
    kc, vc = chunk(k, ML_CHUNK), chunk(v, ML_CHUNK)
    b = jnp.cumsum(chunk(log_f, ML_CHUNK), axis=-1)
    b_end = b[..., -1]
    w_end = b_end[..., None] - b + chunk(log_i, ML_CHUNK)
    m_kv = jnp.max(w_end, axis=-1)
    e = jnp.exp(w_end - m_kv[..., None])
    c_kv = jnp.einsum('bhnl,bhnlv,bhnlk->bhnvk', e, vc, kc)
    n_kv = jnp.einsum('bhnl,bhnlk->bhnk', e, kc)

    def step(carry, inp):
        c_st, n_st, m_st = carry
        be, mk, ck, nk = inp
        m_new = jnp.maximum(be + m_st, mk)
        a_old = jnp.exp(be + m_st - m_new)
        a_new = jnp.exp(mk - m_new)
        c_new = a_old[..., None, None] * c_st + a_new[..., None, None] * ck
        n_new = a_old[..., None] * n_st + a_new[..., None] * nk
        return (c_new, n_new, m_new), carry

    xs = tuple(jnp.moveaxis(t, 2, 0) for t in (b_end, m_kv, c_kv, n_kv))
    final, pre = lax.scan(step, state, xs)
    pre = tuple(jnp.moveaxis(t, 0, 2) for t in pre)
    return pre, final

def mlstm_outputs(q, k, v, log_i, log_f, pre):
    c_prev, n_prev, m_prev = pre
    bsz, nh, t, dv = v.shape
    qc = chunk(q, ML_CHUNK) * (q.shape[-1] ** -0.5)
    kc, vc = chunk(k, ML_CHUNK), chunk(v, ML_CHUNK)
    b = jnp.cumsum(chunk(log_f, ML_CHUNK), axis=-1)
    li = chunk(log_i, ML_CHUNK)
    causal = jnp.tril(jnp.ones((ML_CHUNK, ML_CHUNK), dtype=bool))
    d = jnp.where(causal, b[..., :, None] - b[..., None, :] + li[..., None, :], -jnp.inf)
    m_intra = jnp.max(d, axis=-1)
    m_inter = b + m_prev[..., None]
    m = jnp.maximum(m_inter, m_intra)
    s = jnp.einsum('bhntk,bhnsk->bhnts', qc, kc) * jnp.exp(d - m[..., None])
    a = jnp.exp(m_inter - m)
    num = jnp.einsum('bhnts,bhnsv->bhntv', s, vc) + a[..., None] * jnp.einsum('bhntk,bhnvk->bhntv', qc, c_prev)
    den = jnp.sum(s, axis=-1) + a * jnp.einsum('bhntk,bhnk->bhnt', qc, n_prev)
    h = num / jnp.maximum(jnp.abs(den), jnp.exp(-m))[..., None]
    return h.reshape(bsz, nh, t, dv)

def gla_states(k, v, log_a, state):
    kc, vc = chunk(k, GLA_CHUNK), chunk(v, GLA_CHUNK)
    b = jnp.cumsum(chunk(log_a, GLA_CHUNK), axis=3)
    b_end = b[:, :, :, -1]
    kv = jnp.einsum('bhnsk,bhnsv->bhnkv', kc * jnp.exp(b_end[:, :, :, None] - b), vc)

    def step(s_st, inp):
        be, kvc = inp
        return jnp.exp(be)[..., None] * s_st + kvc, s_st

    final, pre = lax.scan(step, state, (jnp.moveaxis(b_end, 2, 0), jnp.moveaxis(kv, 2, 0)))
    return jnp.moveaxis(pre, 0, 2), final

def gla_outputs(q, k, v, log_a, pre):
    bsz, nh, t, dv = v.shape
    qc = chunk(q, GLA_CHUNK) * (q.shape[-1] ** -0.5)
    kc, vc = chunk(k, GLA_CHUNK), chunk(v, GLA_CHUNK)
    b = jnp.cumsum(chunk(log_a, GLA_CHUNK), axis=3)
    inter = jnp.einsum('bhntk,bhnkv->bhntv', qc * jnp.exp(b), pre)
    causal = jnp.tril(jnp.ones((GLA_CHUNK, GLA_CHUNK), dtype=bool))
    diff = b[:, :, :, :, None, :] - b[:, :, :, None, :, :]
    decay = jnp.exp(jnp.where(causal[:, :, None], diff, -jnp.inf))
    att = jnp.einsum('bhntk,bhnsk,bhntsk->bhnts', qc, kc, decay)
    o = jnp.einsum('bhnts,bhnsv->bhntv', att, vc) + inter
    return o.reshape(bsz, nh, t, dv)

def bidirectional(state_fn, out_fn, ctx_f, ctx_b, lat_f, lat_b, init, ctx_out):
    cb, lb = flip_time(ctx_b), flip_time(lat_b)
    pre_cf, s_f = state_fn(*ctx_f[1:], init)
    pre_cb, s_b = state_fn(*cb[1:], init)
    pre_lf, _ = state_fn(*lat_f[1:], s_f)
    pre_lb, _ = state_fn(*lb[1:], s_b)
    y_lat = out_fn(*lat_f, pre_lf) + jnp.flip(out_fn(*lb, pre_lb), axis=2)
    y_ctx = (out_fn(*ctx_f, pre_cf) + jnp.flip(out_fn(*cb, pre_cb), axis=2)) if ctx_out else None
    return y_ctx, y_lat

def mlstm_prep(p, conv_w, b_gates, with_q):
    bsz, t, _ = p.shape
    k = to_heads(jax.nn.silu(dw_conv(p[..., OFF_ML_K:OFF_ML_V], conv_w[:, ML_WIDTH:])), N_ML_HEADS)
    q = to_heads(jax.nn.silu(dw_conv(p[..., OFF_ML_Q:OFF_ML_K], conv_w[:, :ML_WIDTH])), N_ML_HEADS) if with_q else None
    v = to_heads(p[..., OFF_ML_V:OFF_ML_O], N_ML_HEADS)
    g = (p[..., OFF_ML_G:OFF_GLA_Q] + b_gates).astype(jnp.float32)
    g = g.reshape(bsz, t, 4, N_ML_HEADS).transpose(2, 0, 3, 1)
    fwd = (q, k, v, g[0], jax.nn.log_sigmoid(g[1]))
    bwd = (q, k, v, g[2], jax.nn.log_sigmoid(g[3]))
    return fwd, bwd

def gla_prep(p, w_a2, b_a, with_q):
    q = to_heads(p[..., OFF_GLA_Q:OFF_GLA_K], N_GLA_HEADS) if with_q else None
    k = to_heads(p[..., OFF_GLA_K:OFF_GLA_V], N_GLA_HEADS)
    v = to_heads(p[..., OFF_GLA_V:OFF_GLA_R], N_GLA_HEADS)
    a_lr = p[..., OFF_GLA_A:PROJ_WIDTH]
    la_f = to_heads(jax.nn.log_sigmoid((a_lr[..., :GLA_RANK] @ w_a2[0] + b_a[0]).astype(jnp.float32)) / GLA_GATE_TAU, N_GLA_HEADS)
    la_b = to_heads(jax.nn.log_sigmoid((a_lr[..., GLA_RANK:] @ w_a2[1] + b_a[1]).astype(jnp.float32)) / GLA_GATE_TAU, N_GLA_HEADS)
    return (q, k, v, la_f), (q, k, v, la_b)

def merge_groups(h_ml, o_gla, p, g_ml, g_gla):
    y_ml = head_rms_norm(from_heads(h_ml, p.dtype), g_ml, N_ML_HEADS) * jax.nn.sigmoid(p[..., OFF_ML_O:OFF_ML_G])
    y_gla = head_rms_norm(from_heads(o_gla, p.dtype), g_gla, N_GLA_HEADS) * jax.nn.silu(p[..., OFF_GLA_R:OFF_GLA_A])
    return jnp.concatenate([y_ml, y_gla], axis=-1)

def token_mixers(hc, hl, w_in, conv_w, b_gates, w_a2, b_a, g_ml, g_gla, w_out, ctx_out):
    bsz = hl.shape[0]
    pc = hc @ w_in
    pl = hl @ w_in
    f32 = jnp.float32
    ml_init = (jnp.zeros((bsz, N_ML_HEADS, ML_HEAD_DIM, ML_HEAD_DIM), f32),
               jnp.zeros((bsz, N_ML_HEADS, ML_HEAD_DIM), f32),
               jnp.zeros((bsz, N_ML_HEADS), f32))
    gla_init = jnp.zeros((bsz, N_GLA_HEADS, GLA_KEY_DIM, GLA_VAL_DIM), f32)
    mc_f, mc_b = mlstm_prep(pc, conv_w, b_gates, ctx_out)
    ml_f, ml_b = mlstm_prep(pl, conv_w, b_gates, True)
    hm_c, hm_l = bidirectional(mlstm_states, mlstm_outputs, mc_f, mc_b, ml_f, ml_b, ml_init, ctx_out)
    gc_f, gc_b = gla_prep(pc, w_a2, b_a, ctx_out)
    gl_f, gl_b = gla_prep(pl, w_a2, b_a, True)
    go_c, go_l = bidirectional(gla_states, gla_outputs, gc_f, gc_b, gl_f, gl_b, gla_init, ctx_out)
    y_l = merge_groups(hm_l, go_l, pl, g_ml, g_gla) @ w_out
    y_c = (merge_groups(hm_c, go_c, pc, g_ml, g_gla) @ w_out) if ctx_out else None
    return y_c, y_l

def expert_choice_ffn(h, w_router, w_gate, w_up, w_down):
    n, d = h.shape[1], h.shape[2]
    cap = EC_FACTOR * n // N_EXPERTS
    aff = jax.nn.softmax(jnp.einsum('bnd,de->bne', h, w_router).astype(jnp.float32), axis=-1)
    g, idx = lax.top_k(jnp.swapaxes(aff, 1, 2), cap)
    xin = jax.vmap(lambda hb, ib: hb[ib])(h, idx)
    hid = jax.nn.silu(jnp.einsum('becd,edf->becf', xin, w_gate)) * jnp.einsum('becd,edf->becf', xin, w_up)
    y = jnp.einsum('becf,efd->becd', hid, w_down) * g[..., None].astype(h.dtype)
    return jax.vmap(lambda yb, ib: jnp.zeros((n, d), h.dtype).at[ib.reshape(-1)].add(yb.reshape(-1, d)))(y, idx)

def grid_pos_embedding(rows, d, dtype):
    r = jnp.broadcast_to(jnp.arange(rows, dtype=jnp.float32)[:, None], (rows, GRID_W)).reshape(-1)
    col = jnp.broadcast_to(jnp.arange(GRID_W, dtype=jnp.float32)[None, :], (rows, GRID_W)).reshape(-1)
    quarter = d // 4
    freq = jnp.power(POS_BASE, -jnp.arange(quarter, dtype=jnp.float32) / quarter)
    ar, ac = r[:, None] * freq, col[:, None] * freq
    return jnp.concatenate([jnp.sin(ar), jnp.cos(ar), jnp.sin(ac), jnp.cos(ac)], axis=-1).astype(dtype)

def setup_inputs(seed: int = 0) -> dict:
    key = jax.random.key(seed)
    ks = jax.random.split(key, 24)
    D, E, F = D_MODEL, N_EXPERTS, D_EXPERT

    def nrm(k, shape, scale):
        return scale * jax.random.normal(k, shape, jnp.float32)

    gate_base = jnp.repeat(jnp.array([0.0, 3.0, 0.0, 3.0], jnp.float32), N_ML_HEADS)
    return {
        "x": nrm(ks[0], (BATCH, SEQ, D), 1.0),
        "c": nrm(ks[1], (BATCH, D), 1.0),
        "ctx": nrm(ks[2], (BATCH, CTX_LEN, D), 1.0),
        "c_ctx": nrm(ks[3], (D,), 1.0),
        "w_ada": nrm(ks[4], (DEPTH, D, 6 * D), 0.5 * D ** -0.5),
        "b_ada": nrm(ks[5], (DEPTH, 6 * D), 0.02),
        "g_mix_pre": 1.0 + nrm(ks[6], (DEPTH, D), 0.05),
        "g_mix_post": 1.0 + nrm(ks[7], (DEPTH, D), 0.05),
        "g_ffn_pre": 1.0 + nrm(ks[8], (DEPTH, D), 0.05),
        "g_ffn_post": 1.0 + nrm(ks[9], (DEPTH, D), 0.05),
        "w_in": nrm(ks[10], (DEPTH, D, PROJ_WIDTH), D ** -0.5),
        "conv_qk": nrm(ks[11], (DEPTH, CONV_W, 2 * ML_WIDTH), 0.5),
        "b_ml_gates": gate_base + nrm(ks[12], (DEPTH, N_ML_GATES), 0.1),
        "w_gla_a2": nrm(ks[13], (DEPTH, 2, GLA_RANK, GLA_K_WIDTH), GLA_RANK ** -0.5),
        "b_gla_a": nrm(ks[14], (DEPTH, 2, GLA_K_WIDTH), 0.1),
        "g_ml_norm": 1.0 + nrm(ks[15], (DEPTH, ML_WIDTH), 0.05),
        "g_gla_norm": 1.0 + nrm(ks[16], (DEPTH, GLA_V_WIDTH), 0.05),
        "w_out": nrm(ks[17], (DEPTH, D, D), D ** -0.5),
        "w_router": nrm(ks[18], (DEPTH, D, E), D ** -0.5),
        "w_e_gate": nrm(ks[19], (DEPTH, E, D, F), D ** -0.5),
        "w_e_up": nrm(ks[20], (DEPTH, E, D, F), D ** -0.5),
        "w_e_down": nrm(ks[21], (DEPTH, E, F, D), F ** -0.5),
    }

def reference(x, c, ctx, c_ctx, w_ada, b_ada, g_mix_pre, g_mix_post, g_ffn_pre, g_ffn_post,
              w_in, conv_qk, b_ml_gates, w_gla_a2, b_gla_a, g_ml_norm, g_gla_norm, w_out,
              w_router, w_e_gate, w_e_up, w_e_down):
    n_tok = x.shape[1]
    rows = n_tok // GRID_W
    x = x + grid_pos_embedding(rows, x.shape[-1], x.dtype)[None]
    xc = ctx
    for l in range(DEPTH):
        last = l == DEPTH - 1
        mod = jax.nn.silu(c) @ w_ada[l] + b_ada[l]
        mod_c = jax.nn.silu(c_ctx) @ w_ada[l] + b_ada[l]
        sh1, sc1, ga1, sh2, sc2, ga2 = jnp.split(mod[:, None, :], 6, axis=-1)
        csh1, csc1, cga1, csh2, csc2, cga2 = jnp.split(mod_c, 6)
        hl = modulate(rms_norm(x, g_mix_pre[l]), sh1, sc1)
        hc = modulate(rms_norm(xc, g_mix_pre[l]), csh1, csc1)
        y_c, y_l = token_mixers(hc, hl, w_in[l], conv_qk[l], b_ml_gates[l], w_gla_a2[l], b_gla_a[l],
                                g_ml_norm[l], g_gla_norm[l], w_out[l], not last)
        x = x + ga1 * rms_norm(y_l, g_mix_post[l])
        hl2 = modulate(rms_norm(x, g_ffn_pre[l]), sh2, sc2)
        x = x + ga2 * rms_norm(expert_choice_ffn(hl2, w_router[l], w_e_gate[l], w_e_up[l], w_e_down[l]), g_ffn_post[l])
        if not last:
            xc = xc + cga1 * rms_norm(y_c, g_mix_post[l])
            hc2 = modulate(rms_norm(xc, g_ffn_pre[l]), csh2, csc2)
            xc = xc + cga2 * rms_norm(expert_choice_ffn(hc2, w_router[l], w_e_gate[l], w_e_up[l], w_e_down[l]), g_ffn_post[l])
    return x


_drawn_inputs = setup_inputs


def setup_inputs(seed=0):
    import zlib

    import numpy as np

    out = dict(_drawn_inputs(seed))
    spreads = {}
    factors = {'g_ffn_post': 4.588, 'g_ml_norm': 3.217}
    for name, (base, spread) in spreads.items():
        noise = np.random.default_rng([zlib.crc32(name.encode()), seed]).standard_normal(out[name].shape)
        drawn = base * np.exp(spread * noise) if base else spread * noise
        out[name] = __import__('jax').numpy.asarray(drawn.astype(out[name].dtype))
    for name, factor in factors.items():
        out[name] = (out[name] * factor).astype(out[name].dtype)
    return out
```

```python
from contextlib import ExitStack

import numpy as np

import concourse.bass as bass
from concourse import mybir

F32 = mybir.dt.float32
F32R = mybir.dt.float32r
U32 = mybir.dt.uint32
ALU = mybir.AluOpType
ACT = mybir.ActivationFunctionType
AX = mybir.AxisListType
ds = bass.ds

P = 128
D = 1024
SEQ = 1024
CTX = 256
ALL = CTX + SEQ
EPS = 1e-6
GRID_W = 64
POS_BASE = 10000.0
ML_W = 512
NH = 4
HD = 128
GK_W = 256
GV_W = 512
RANK = 16
TAU = 16.0
N_EXP = 16
CAP = 2 * SEQ // N_EXP
F = D
KC = D // P
TC = CTX // P
TL = SEQ // P
TA = TC + TL
UW = 256
OFF_Q, OFF_K, OFF_V, OFF_O, OFF_G = 0, 512, 1024, 1536, 2048
OFF_GQ = OFF_G + 4 * NH
OFF_GK = OFF_GQ + GK_W
OFF_GV = OFF_GK + GK_W
OFF_R = OFF_GV + GV_W
OFF_A = OFF_R + GV_W

_cols = {}
_n = 0
for _name, _w in (("c", 2 * KC), ("b_ada", 6 * KC), ("g_mix_pre", KC), ("g_mix_post", KC), ("g_ffn_pre", KC),
                  ("g_ffn_post", KC), ("g_heads", KC), ("conv", 3 * 2 * NH), ("b_gates", 2), ("b_gla", 4),
                  ("w_gla2", 2 * GK_W), ("w_router", KC * N_EXP)):
    _cols[_name] = (_n, _n + _w)
    _n += _w
NSMALL = _n
COLS = dict(_cols)

ADA_FIRST = list(range(8))
ADA_REST = list(range(8, 24))
IN_UNITS = ["G", "k0", "k1", "q0", "q1", "v0", "v1", "gk", "gq", "gv0", "gv1", "o0", "o1", "r0", "r1"]
STREAM = [("ada", j) for j in ADA_FIRST]
_rest = list(ADA_REST)
for _u in IN_UNITS:
    STREAM.append(("in", IN_UNITS.index(_u)))
    if _u in ("gv0", "gv1", "o0", "o1", "r0", "r1"):
        STREAM += [("ada", j) for j in _rest[:3]]
        _rest = _rest[3:]
STREAM += [("out", j) for j in range(4)]
assert not _rest
AT = {("in", n): STREAM.index(("in", IN_UNITS.index(n))) for n in IN_UNITS}
AT |= {("ada", j): STREAM.index(("ada", j)) for j in range(24)}
AT |= {("out", j): STREAM.index(("out", j)) for j in range(4)}

PAIRS = {}
for _u, _k in (("v0", 5), ("v1", 5), ("gv0", 5), ("gv1", 5), ("o0", 4), ("o1", 4), ("r0", 4), ("r1", 4),
               ("out0", 4), ("out1", 4), ("out2", 4), ("out3", 4)):
    PAIRS[_u] = (sum(v[1] for v in PAIRS.values()), _k)
TOK_BANKS = 6

BASE = 16512
KB = 1024
AT_SMALL, AT_HT, AT_RING, AT_OUT = BASE, BASE + 13 * KB, BASE + 93 * KB, BASE + 141 * KB

BANK = 512
EV_C0 = 15
ML_T0 = 4
GLA_SCALE = float(GK_W // NH) ** -0.5
LN_HD = 0.5 * float(np.log(HD))

EU = 12


def build(nc, I, out):
    ctx = ExitStack()
    with ctx:
        def at(name, offset, shape, dt=F32):
            return nc.alloc_sbuf_tensor_at(name, shape, dt, offset=offset)

        def sem(name):
            return ctx.enter_context(nc.semaphore(name))

        xn2_dram = nc.dram_tensor("xn2_dram", [SEQ, D], F32).ap()
        acc_dram = nc.dram_tensor("acc_dram", [SEQ, D], F32).ap()

        psum = ctx.enter_context(nc.psum_tensor("psum", [P, 8 * BANK], F32))

        off = [AT_SMALL]

        def small(name, shape, dt=F32):
            t = at(name, off[0], shape, dt)
            off[0] += (int(np.prod(shape[1:])) * 4 + 31) // 32 * 32
            assert off[0] <= AT_HT, off[0] - AT_SMALL
            return t

        sm = small("sm", [P, NSMALL])
        ident = small("ident", [P, P])
        gate_rows = small("gate_rows", [P, ALL])
        mask_add = small("mask_add", [P, 2, P])
        modc = small("modc", [P, 6 * KC, 2])
        amix = small("amix", [P, 2, KC])
        cst = small("cst", [P, 3, TA, 2 * NH])
        ssq = small("ssq", [P, 16])
        rstd = small("rstd", [P, 16])
        decm = small("decm", [P, 2, NH])
        den = small("den", [P, 2, NH])
        gcol = small("gcol", [P, 5, 4, TA])
        hstat = small("hstat", [P, TL * NH])
        mprev = small("mprev", [P, TA])
        sel_s = small("sel_s", [P, 2 * NH])
        one_s = small("one_s", [P, 2])
        zero_r = small("zero_r", [P, P])
        ln_hd = small("ln_hd", [P, 1])

        def col(name):
            a, b = COLS[name]
            return sm[:, a:b]

        h_hi = at("h_hi", AT_HT, [P, KC, ALL], F32R)
        h_lo = at("h_lo", AT_HT + 40 * KB, [P, KC, ALL], F32R)
        raw = [at(f"raw{s}", AT_RING + 8 * KB * s, [P, KC, UW]) for s in range(2)]
        w_hi = [at(f"w_hi{s}", AT_RING + 16 * KB + 8 * KB * s, [P, KC, UW], F32R) for s in range(2)]
        w_lo = [at(f"w_lo{s}", AT_RING + 32 * KB + 8 * KB * s, [P, KC, UW], F32R) for s in range(2)]
        xs = at("xs", AT_OUT, [P, TA, D])
        pos_l = at("pos_l", AT_OUT + 40 * KB, [P, TL, D // 2])
        h32 = at("h32", AT_OUT + 40 * KB, [P, 2, ALL])
        c_st = at("c_st", AT_OUT + 58 * KB, [P, KC, P], F32R)
        c32 = at("c32", AT_OUT + 62 * KB, [P, 2, KC, 2])
        mod_rows = at("mod_rows", AT_OUT + 63 * KB, [P, 2, UW])
        pos_c = at("pos_c", AT_OUT + 56 * KB, [P, D // 2])
        kT = at("kT", AT_OUT, [P, NH, ALL])
        qT = at("qT", AT_OUT + 20 * KB, [P, NH, SEQ])
        rows_na = at("rows_na", AT_OUT + 36 * KB, [P, 2, ALL])
        v_ext = at("v_ext", AT_OUT + 46 * KB, [P, TA, NH, HD + 1])
        row_f = at("row_f", AT_OUT + 46 * KB, [P, ALL])
        row_b = at("row_b", AT_OUT + 51 * KB, [P, ALL])
        row_m = at("row_m", AT_OUT + 56 * KB, [P, ALL])
        row_a = at("row_a", AT_OUT + 61 * KB, [P, ALL])

        def ml(name, n):
            return [at(f"{name}{d}", AT_RING + 2 * KB * (2 * n + d), [P, NH, P]) for d in range(2)]

        ml_w, ml_sw, ml_qs, ml_kh, ml_ks = ml("ml_w", 0), ml("ml_sw", 1), ml("ml_qs", 2), ml("ml_kh", 3), ml("ml_ks", 4)
        ml_c = at("ml_c", AT_RING + 20 * KB, [P, 2, NH, HD + 1])
        h_ml = at("h_ml", AT_RING + 25 * KB, [P, TL, ML_W])
        sel_r = at("sel_r", AT_RING + 41 * KB, [P, 2 * NH, P])
        h_sq = at("h_sq", AT_RING, [P, TL, ML_W])
        y_ml = at("y_ml", AT_OUT, [P, TL, ML_W])
        ht_f = at("ht_f", AT_HT, [P, 2 * KC, ALL])
        gk = at("gk", AT_OUT + 16 * KB, [P, 2, ALL])
        gq = at("gq", AT_OUT + 26 * KB, [P, 2, SEQ])
        gv = at("gv", AT_OUT + 34 * KB, [P, TA, GV_W])
        b_ctx = at("b_ctx", AT_OUT + 54 * KB, [P, 4, CTX])
        l_ctx = at("l_ctx", AT_OUT + 65 * KB, [P, CTX])
        g_s = at("g_s", AT_OUT + 58 * KB, [P, 2, 2, 2 * HD])
        g_ps = at("g_ps", AT_OUT + 62 * KB, [P, 2, 2, 2 * HD])

        def stage(j):
            return ht_f[:, KC + j, CTX + 512:ALL]

        qz = [stage(d).rearrange("p (i h t) -> p i h t", i=2, h=2) for d in range(2)]
        g_a = [stage(2 + d).rearrange("p (h t) -> p h t", h=NH) for d in range(2)]
        kx = [stage(4 + d)[:, 0:2 * P].rearrange("p (i t) -> p i t", i=2) for d in range(2)]
        k_tok = [stage(4 + d)[:, 2 * P:4 * P].rearrange("p (i t) -> p i t", i=2) for d in range(2)]
        e_q = [stage(6 + d)[:, 0:2 * P].rearrange("p (i t) -> p i t", i=2) for d in range(2)]
        e_k = [stage(6 + d)[:, 2 * P:4 * P].rearrange("p (i t) -> p i t", i=2) for d in range(2)]

        def og(t):
            return ht_f[:, KC + t, CTX:CTX + GV_W]

        def gla_bank(d, j, n):
            return psum[:, BANK * (4 * d + j):BANK * (4 * d + j) + n]

        bc_ps = psum[:, 0:2 * BANK].rearrange("p (h q t) -> p h q t", h=NH, q=2)
        st_ps = psum[:, 2 * BANK:3 * BANK].rearrange("p (h t) -> p h t", h=NH)
        kt_ps = psum[:, 3 * BANK:4 * BANK].rearrange("p (h t) -> p h t", h=NH)

        def two_banks(b):
            v = psum[:, b * BANK:(b + 2) * BANK].rearrange("p (b n) -> p b n", b=2)
            return v[:, :, 0:2 * (HD + 1)].rearrange("p b (j e) -> p b j e", j=2)

        kv_ps, num_ps = two_banks(4), two_banks(6)
        modps = psum[:, 7 * BANK:7 * BANK + 12 * KC].rearrange("p (j r) -> p j r", r=2)

        s_small, s_x, s_pos = sem("s_small"), sem("s_x"), sem("s_pos")
        raw_full = [sem("raw_full0"), sem("raw_full1")]
        hi_ready, lo_ready = sem("hi_ready"), sem("lo_ready")
        konst, ones_set = sem("konst"), sem("ones_set")
        dve_seq, act_seq = sem("dve_seq"), sem("act_seq")
        sem_out = sem("sem_out")
        c_silu, c_ready = sem("c_silu"), sem("c_ready")
        ada_rows, ada_evac, ada_cols = sem("ada_rows"), sem("ada_evac"), sem("ada_cols")
        mod1_ready = sem("mod1_ready")
        ssq_done, std_done, xn_ready = sem("ssq_done"), sem("std_done"), sem("xn_ready")
        xt_ready, h32_ready, h_ready, hhi_ready = sem("xt_ready"), sem("h32_ready"), sem("h_ready"), sem("hhi_ready")
        tile_mm, g_free, conv_mid, conv_free, conv_act = (sem("tile_mm"), sem("g_free"), sem("conv_mid"),
                                                          sem("conv_free"), sem("conv_act"))
        tok_mm, tok_act, tok_dve = sem("tok_mm"), sem("tok_act"), sem("tok_dve")
        row_act, row_dve, stat_mm, stat_ready = sem("row_act"), sem("row_dve"), sem("stat_mm"), sem("stat_ready")

        def wait_used(eng, n):
            kind, j = STREAM[n]
            if kind == "ada" and n < 8:
                eng.wait_ge(ada_rows, n + 1)
            elif n <= AT["in", "q1"]:
                eng.wait_ge(tile_mm, 2 * (n - 8) + 2)
            elif kind == "ada":
                eng.wait_ge(ada_rows, j + 1)
            elif kind == "in" and IN_UNITS[j] in ("gk", "gq"):
                eng.wait_ge(tile_mm, 12 if IN_UNITS[j] == "gk" else 14)
            else:
                name = IN_UNITS[j] if kind == "in" else f"out{j}"
                eng.wait_ge(tok_mm, PAIRS[name][0] + PAIRS[name][1])

        def pair_out(eng, p):
            if p < PAIRS["o0"][0]:
                eng.wait_ge(tok_dve if p % 2 else tok_act, p // 2 + 1 if p % 2 == 0 else (p + 1) // 2)
            elif p < PAIRS["r0"][0]:
                eng.wait_ge(tok_dve, 10 + p - PAIRS["o0"][0] + 1)
            elif p < PAIRS["out0"][0]:
                eng.wait_ge(tok_act, 10 + p - PAIRS["r0"][0] + 1)
            else:
                q = p - PAIRS["out0"][0]
                eng.wait_ge(tok_dve if q % 2 else tok_act, 18 + q // 2 + 1)

        def tok_ps(p, r):
            return psum[:, BANK * (p % TOK_BANKS) + UW * r:BANK * (p % TOK_BANKS) + UW * (r + 1)]

        def tokv(p, r):
            return tok_ps(p, r).rearrange("p (h n) -> p h n", n=HD)

        kst_ready, bc_mm, st_mm, kt_mm = sem("kst_ready"), sem("bc_mm"), sem("st_mm"), sem("kt_mm")
        d_ready, w_ready, sw_ready, bc_read = sem("d_ready"), sem("w_ready"), sem("sw_ready"), sem("bc_read")
        kh_ready, kv_mm, num_mm, c_done = sem("kh_ready"), sem("kv_mm"), sem("num_mm"), sem("c_done")
        h_done, den_seq, ml_zero, ml_norm = sem("h_done"), sem("den_seq"), sem("ml_zero"), sem("ml_norm")

        def at_least(eng, s, v):
            if not isinstance(v, int) or v > 0:
                eng.wait_ge(s, v)

        def scan_steps(eng, front, back):
            def args(t):
                i, d = t // 2, t % 2
                if t < ML_T0:
                    return t, None, d, (i if d == 0 else TC - 1 - i)
                return t, t - ML_T0, d, (i if d == 0 else TC + TA - 1 - i)

            peel, last = ML_T0 + 2, 2 * TA
            front(*args(0))
            for t in range(peel):
                front(*args(t + 1))
                back(*args(t))
            with eng.Fori(TC + 1 + 0, TA - 1) as i:
                t = 2 * i
                mirrored = i * -1 + (TC + TA - 1)
                front(t + 1, t + 1 - ML_T0, 1, mirrored)
                back(t, t - ML_T0, 0, i)
                front(t + 2, t + 2 - ML_T0, 0, i + 1)
                back(t + 1, t + 1 - ML_T0, 1, mirrored)
            front(*args(last - 1))
            back(*args(last - 2))
            back(*args(last - 1))

        def chunk_cols(c):
            return ds(P * c, P)

        y_dve, zero_g = sem("y_dve"), sem("zero_g")
        z_out, la_tmp, la_seq, b_ready, cols_dve, cols_act = (sem("z_out"), sem("la_tmp"), sem("la_seq"),
                                                              sem("b_ready"), sem("cols_dve"), sem("cols_act"))
        e_ready, gx_ready, gst_mm, gkt_mm = sem("e_ready"), sem("gx_ready"), sem("gst_mm"), sem("gkt_mm")
        gkh_ready, a_ready, gkv_mm, go_mm = sem("gkh_ready"), sem("a_ready"), sem("gkv_mm"), sem("go_mm")
        ps_ready, kvs_ready, s_done, og_done = sem("ps_ready"), sem("kvs_ready"), sem("s_done"), sem("og_done")
        c_again, mask_exp = sem("c_again"), sem("mask_exp")
        sig_done = sem("sig_done")

        y_gla = at("y_gla", AT_OUT + 16 * KB, [P, TL, GV_W])
        yt_hi = at("yt_hi", AT_HT, [P, KC, SEQ], F32R)
        yt_lo = at("yt_lo", AT_HT + 32 * KB, [P, KC, SEQ], F32R)
        rowb = at("rowb", AT_HT + 64 * KB, [P, 3, D])
        diag = at("diag", AT_HT + 76 * KB, [P, KC, P])
        y_out = at("y_out", AT_OUT + 32 * KB, [P, TL, D])
        x_res = at("x_res", AT_OUT, [P, TL, D])
        pos_r2 = at("pos_r2", AT_RING, [P, TL, D // 2])
        pos_c2 = at("pos_c2", AT_OUT + 64 * KB, [P, D // 2])
        h2 = at("h2", AT_HT, [P, TL, D])
        h2t = at("h2t", AT_HT + 32 * KB, [P, KC, SEQ])
        aff_t = at("aff_t", AT_OUT + 44 * KB, [P, SEQ])
        vals = at("vals", AT_OUT + 48 * KB, [P, CAP])
        idx_u = at("idx_u", AT_OUT + 48 * KB + 512, [P, CAP], U32)
        idx_f = at("idx_f", AT_OUT + 49 * KB, [P, CAP])
        e_lg = at("e_lg", AT_OUT + 50 * KB, [P, TL, N_EXP])
        diag2 = at("diag2", AT_OUT + 52 * KB, [P, KC, P])
        zeros = at("zeros", AT_OUT + 56 * KB, [P, D])
        e_raw = [at(f"e_raw{u}", (AT_RING if u < 6 else AT_HT + 32 * KB) + 8 * KB * (u % 6), [P, 2 * D]) for u in range(EU)]
        e_hi = [at(f"e_hi{s}", AT_HT + 16 * KB * s, [P, 2 * D], F32R) for s in range(2)]
        e_lo = [at(f"e_lo{s}", AT_HT + 16 * KB * s + 8 * KB, [P, 2 * D], F32R) for s in range(2)]
        x_tok = at("x_tok", AT_OUT + 32 * KB, [P, D])
        xt_hi = at("xt_hi", AT_OUT + 36 * KB, [P, KC, CAP], F32R)
        xt_lo = at("xt_lo", AT_OUT + 40 * KB, [P, KC, CAP], F32R)
        hid = at("hid", AT_OUT + 44 * KB, [P, F])
        hd_hi = at("hd_hi", AT_OUT + 48 * KB, [P, F // P, CAP], F32R)
        hd_lo = at("hd_lo", AT_OUT + 52 * KB, [P, F // P, CAP], F32R)
        y_exp = at("y_exp", AT_OUT + 56 * KB, [P, D])
        row_g2 = at("row_g2", AT_OUT + 60 * KB, [P, D])
        gates = at("gates", AT_OUT + 66 * KB, [P, N_EXP])
        tokens = at("tokens", AT_OUT + 66 * KB + 64, [P, N_EXP], U32)
        tok_g = at("tok_g", AT_OUT + 66 * KB + 128, [P, 1], U32)
        tok_s = at("tok_s", AT_OUT + 66 * KB + 160, [P, 1], U32)
        acc = at("acc", AT_HT, [P, TL, D])
        ones_m = zero_r
        vec_c = cst[:, 0, 0:4, :]

        gla_sq, yt_mm, yt_hi_ok, yt_lo_ok = sem("gla_sq"), sem("yt_mm"), sem("yt_hi_ok"), sem("yt_lo_ok")
        diag_ready, row_mm, rowb_ready = sem("diag_ready"), sem("row_mm"), sem("rowb_ready")
        s_xr, s_pr, pos_added = sem("s_xr"), sem("s_pr"), sem("pos_added")
        y_ssq, y_scaled, x1_ready, x_ssq = sem("y_ssq"), sem("y_scaled"), sem("x1_ready"), sem("x_ssq")
        h2_mid, h2_ready, h2t_mm, h2t_ready, lg_mm = (sem("h2_mid"), sem("h2_ready"), sem("h2t_mm"), sem("h2t_ready"),
                                                      sem("lg_mm"))
        h2_stored, acc_zeroed, zeros_set = sem("h2_stored"), sem("acc_zeroed"), sem("zeros_set")
        soft, aff_mm, topk, sel_mm, route_ready = sem("soft"), sem("aff_mm"), sem("topk"), sem("sel_mm"), sem("route_ready")
        e_full = [sem(f"e_full{u}") for u in range(EU)]
        e_hi_ok, e_lo_ok, w_used = sem("e_hi_ok"), sem("e_lo_ok"), sem("w_used")
        gathered, xt_mm, xt_hi_ok, xt_ok = sem("gathered"), sem("xt_mm"), sem("xt_hi_ok"), sem("xt_ok")
        tok_0_ok, tok_g_ok, tok_s_ok = sem("tok_0_ok"), sem("tok_g_ok"), sem("tok_s_ok")
        sg_ok, hid_ok, hd_mm, hd_hi_ok, hd_ok = sem("sg_ok"), sem("hid_ok"), sem("hd_mm"), sem("hd_hi_ok"), sem("hd_ok")
        y_free, y_taken, scattered = sem("y_free"), sem("y_taken"), sem("scattered")
        acc_full = [sem(f"acc_full{j}") for j in range(4)]
        a_ssq, o_mid, o_ready = sem("a_ssq"), sem("o_mid"), sem("o_ready")

        def e_ps(b):
            return psum[:, b * BANK:(b + 2) * BANK]

        def quarter(b, q):
            o = BANK * (b + q % 2) + UW * (q // 2)
            return psum[:, o:o + UW]

        block = ctx.enter_context(nc.Block())

        def t_lat(s):
            return psum[:, 2048 * s:2048 * s + SEQ]

        def t_ctx(s):
            return psum[:, 2048 * s + SEQ:2048 * s + ALL]

        def unit_src(kind, j):
            if kind == "ada":
                return I["w_ada"].rearrange("(k p) n -> p k n", p=P)[:, :, UW * j:UW * (j + 1)]
            return I["w_in_units" if kind == "in" else "w_out_units"][j].rearrange("p (k n) -> p k n", k=KC)

        @block.sync
        def _(sp):
            sp.dma_start(sm[:], I["small"]).then_inc(s_small, 16)
            sp.dma_start(xs[:, 0:TC, :], I["ctx"].rearrange("(t p) d -> p t d", p=P)).then_inc(s_x, 16)
            sp.dma_start(xs[:, TC:TA, :], I["x"].rearrange("(t p) d -> p t d", p=P)).then_inc(s_x, 16)
            for half in range(2):
                sp.dma_start(pos_c[64 * half:64 * half + 64, :], I["pos_col"]).then_inc(s_pos, 16)
                sp.dma_start(pos_l[64 * half:64 * half + 64, :, :],
                             I["pos_row"].rearrange("(t h) n -> h t n", h=2)[half].partition_broadcast(64)).then_inc(s_pos, 16)

            def load_unit(n):
                if n >= 2:
                    sp.wait_ge(hi_ready, n - 1)
                    sp.wait_ge(lo_ready, n - 1)
                sp.dma_start(raw[n % 2][:], unit_src(*STREAM[n])).then_inc(raw_full[n % 2], 16)

            for n in range(EV_C0):
                load_unit(n)
            sp.wait_ge(ml_norm, 4)
            for n in range(EV_C0, AT["out", 0]):
                load_unit(n)
            for n in range(AT["out", 0], len(STREAM)):
                load_unit(n)
            sp.wait_ge(og_done, 2 * TL)
            for half in range(2):
                sp.dma_start(pos_c2[64 * half:64 * half + 64, :], I["pos_col"]).then_inc(s_pr, 16)
            sp.wait_ge(yt_mm, KC)
            sp.dma_start(x_res[:], I["x"].rearrange("(t p) d -> p t d", p=P)).then_inc(s_xr, 16)
            sp.wait_ge(hi_ready, len(STREAM))
            sp.wait_ge(lo_ready, len(STREAM))
            for half in range(2):
                sp.dma_start(pos_r2[64 * half:64 * half + 64, :, :],
                             I["pos_row"].rearrange("(t h) n -> h t n", h=2)[half].partition_broadcast(64)).then_inc(s_pr, 16)

            def expert_src(e, u):
                if 4 <= u < 8:
                    c = slice(UW * (u - 4), UW * (u - 3))
                    return I["w_e_up"][ds(e, 1), :, c].rearrange("o (k p) n -> p (o k) n", p=P)
                w = I["w_e_gate"] if u < 4 else I["w_e_down"]
                r = 2 * P * (u % 4)
                return w[ds(e, 1), r:r + 2 * P, :].rearrange("o (k p) n -> p (o k) n", p=P)

            def load_expert_unit(e, u):
                dst = e_raw[u][:].rearrange("p (k n) -> p k n", k=KC if 4 <= u < 8 else 2)
                sp.dma_start(dst, expert_src(e, u)).then_inc(e_full[u], 16)

            sp.wait_ge(pos_added, 2)
            sp.wait_ge(tok_mm, 52)
            for u in range(6):
                load_expert_unit(0, u)
            for t in range(TL):
                sp.wait_ge(h2_ready, t + 1)
                sp.dma_start(xn2_dram[P * t:P * (t + 1), :], h2[:, t, :]).then_inc(h2_stored, 16)
            sp.wait_ge(zeros_set, 1)
            sp.dma_start(acc_dram.rearrange("(t p) d -> p t d", p=P), zeros[:].unsqueeze(1).to_broadcast([P, TL, D])).then_inc(acc_zeroed, 16)
            sp.wait_ge(lg_mm, TL)
            for u in range(6, EU):
                load_expert_unit(0, u)
            with sp.Fori(0, N_EXP - 1) as e:
                for u in range(EU):
                    sp.wait_ge(e_hi_ok, EU * e + u + 1)
                    sp.wait_ge(e_lo_ok, EU * e + u + 1)
                    load_expert_unit(e + 1, u)
            sp.wait_ge(scattered, 16 * N_EXP)
            sp.wait_ge(w_used, EU * N_EXP + 2)
            sp.wait_ge(e_lo_ok, EU * N_EXP)
            for j in range(4):
                sp.dma_start(acc[:, 2 * j:2 * j + 2, :],
                             acc_dram[2 * P * j:2 * P * (j + 1), :].rearrange("(t p) d -> p t d", p=P)).then_inc(acc_full[j], 16)
            for t in range(TL):
                sp.wait_ge(o_ready, t + 1)
                sp.dma_start(out[P * t:P * (t + 1), :], x_res[:, t, :]).then_inc(sem_out, 16)
            sp.wait_ge(sem_out, 16 * TL)

        @block.gpsimd
        def _(pool):
            pool.memset(ident[:], 0.0).then_inc(konst, 1)
            pool.memset(mask_add[:], 0.0).then_inc(konst, 1)
            pool.memset(sel_s[:], 0.0).then_inc(konst, 1)
            pool.memset(one_s[:], 0.0).then_inc(konst, 1)
            pool.wait_ge(konst, 4)
            pool.affine_select(out=ident[:], in_=ident[:], compare_op=ALU.not_equal, fill=1.0, base=0,
                               pattern=[[-1, P]], channel_multiplier=1).then_inc(konst, 1)
            pool.affine_select(out=mask_add[:, 0, :], in_=mask_add[:, 0, :], compare_op=ALU.is_ge, fill=-1e30,
                               base=0, pattern=[[1, P]], channel_multiplier=-1).then_inc(konst, 1)
            pool.affine_select(out=mask_add[:, 1, :], in_=mask_add[:, 1, :], compare_op=ALU.is_ge, fill=-1e30,
                               base=0, pattern=[[-1, P]], channel_multiplier=1).then_inc(konst, 1)
            for d in range(2):
                v = sel_s[:, NH * d:NH * d + NH]
                pool.affine_select(out=v, in_=v, compare_op=ALU.not_equal, fill=1.0, base=-32 * d,
                                   pattern=[[-1, NH]], channel_multiplier=1).then_inc(konst, 1)
            v = one_s[:, :]
            pool.affine_select(out=v, in_=v, compare_op=ALU.not_equal, fill=1.0, base=0,
                               pattern=[[-1, 2]], channel_multiplier=1).then_inc(konst, 1)
            pool.wait_ge(konst, 10)
            pool.affine_select(out=v, in_=v, compare_op=ALU.not_equal, fill=1.0, base=-2,
                               pattern=[[-1, 2]], channel_multiplier=1).then_inc(konst, 1)

            pool.wait_ge(stat_ready, 1)
            pool.wait_ge(tok_mm, 10)
            pool.wait_ge(konst, 11)
            pool.memset(ml_c[:], 0.0).then_inc(ml_zero, 1)
            pool.memset(h_ml[:], 0.0).then_inc(ml_zero, 1)
            pool.memset(sel_r[:], 0.0).then_inc(ml_zero, 1)
            pool.wait_ge(ml_zero, 3)
            for d in range(2):
                v = sel_r[:, NH * d:NH * d + NH, :]
                pool.affine_select(out=v, in_=v, compare_op=ALU.not_equal, fill=1.0, base=-32 * d,
                                   pattern=[[-1, NH], [0, P]], channel_multiplier=1).then_inc(ml_zero, 1)
            pool.wait_ge(conv_act, 8)

            def stage_k(t, l, d, c):
                at_least(pool, kt_mm, t - 1)
                pool.tensor_copy(ml_ks[d][:], kT[:, :, chunk_cols(c)]).then_inc(kst_ready, 1)

            scan_steps(pool, stage_k, lambda t, l, d, c: None)
            pool.wait_ge(z_out, 4)
            pool.memset(g_s[:], 0.0)
            pool.memset(ht_f[:, KC:2 * KC, CTX:CTX + GV_W], 0.0)
            pool.memset(ht_f[:, KC:KC + 2, CTX + 512:ALL], 0.0).then_inc(zero_g, 1)
            pool.wait_ge(s_xr, 16)
            pool.wait_ge(s_pr, 64)
            pool.tensor_tensor(x_res[:, :, 0:D // 2], x_res[:, :, 0:D // 2], pos_r2[:], ALU.add).then_inc(pos_added, 1)
            pool.tensor_tensor(x_res[:, :, D // 2:D], x_res[:, :, D // 2:D],
                               pos_c2[:].unsqueeze(1).to_broadcast([P, TL, D // 2]), ALU.add).then_inc(pos_added, 1)
            pool.wait_ge(x1_ready, TL)
            pool.memset(zeros[:], 0.0).then_inc(zeros_set, 1)
            def gather(e, copied, n):
                pool.tensor_copy(tok_g[:], tokens[:, ds(e, 1)]).then_inc(copied, 1)
                pool.wait_ge(h2_stored, 16 * TL)
                pool.wait_ge(copied, n)
                pool.indirect_dma_start(x_tok[:], None, xn2_dram, bass.IndirectOffsetOnAxis(ap=tok_g[:, 0:1], axis=0)).then_inc(gathered, 16)

            def scatter(e):
                pool.wait_ge(y_free, e + 2)
                pool.tensor_copy(tok_s[:], tokens[:, ds(e, 1)]).then_inc(tok_s_ok, 1)
                pool.wait_ge(acc_zeroed, 16)
                pool.wait_ge(tok_s_ok, e + 1)
                pool.indirect_dma_start(acc_dram, bass.IndirectOffsetOnAxis(ap=tok_s[:, 0:1], axis=0), y_exp[:], None,
                                        compute_op=ALU.add).then_inc(scattered, 16)
                pool.wait_ge(scattered, 16 * e + 16)
                pool.nop().then_inc(y_taken, 1)

            pool.wait_ge(route_ready, 1)
            gather(0, tok_0_ok, 1)
            pool.nop().then_inc(y_taken, 1)
            with pool.Fori(1, N_EXP) as e:
                pool.wait_ge(xt_mm, e)
                gather(e, tok_g_ok, e)
                scatter(e - 1)
            scatter(N_EXP - 1)

        @block.scalar
        def _(act):
            n_act = [0]

            def act_link(ins):
                n_act[0] += 1
                ins.then_inc(act_seq, 1)
                act.wait_ge(act_seq, n_act[0])

            def split_hi(n):
                act.wait_ge(raw_full[n % 2], 16 * (n // 2 + 1))
                if n >= 2:
                    wait_used(act, n - 2)
                act.activation(w_hi[n % 2][:], raw[n % 2][:], ACT.Copy).then_inc(hi_ready, 1)

            act.wait_ge(s_small, 16)
            cc = col("c").rearrange("p (k r) -> p k r", k=KC)
            act.activation(c32[:, 0, :, :], cc, ACT.Silu).then_inc(c_silu, 1)
            act.wait_ge(s_x, 32)
            act.wait_ge(xn_ready, 1)
            for t in range(TA):
                if t >= 2:
                    act.wait_ge(ssq_done, t - 1)
                act.activation(psum[:, 2048 + D * (t % 2):2048 + D * (t % 2 + 1)], xs[:, t, :], ACT.Square,
                               accum_out=ssq[:, t:t + 1]).then_inc(ssq_done, 1)
            act.wait_ge(ssq_done, TA + 1)
            act.activation(rstd[:, 0:TA], ssq[:, 0:TA], ACT.Sqrt).then_inc(std_done, 1)

            def ada_evac_rows(n):
                act.wait_ge(ada_rows, n + 1)
                if n >= 2:
                    act.wait_ge(ada_cols, n - 1)
                act.activation(mod_rows[:, n % 2, :], psum[:, BANK * (n % 2):BANK * (n % 2) + UW], ACT.Copy).then_inc(ada_evac, 1)

            for n in range(8):
                split_hi(n)
                if n:
                    ada_evac_rows(n - 1)
            ada_evac_rows(7)
            split_hi(8)
            act.wait_ge(mod1_ready, 1)
            for k in range(KC):
                act.wait_ge(xt_ready, k + 1)
                if k >= 2:
                    act.wait_ge(h_ready, k - 1)
                s = k % 2
                act.activation(h32[:, s, 0:CTX], t_ctx(s), ACT.Identity, bias=modc[:, k, 1:2],
                               scale=amix[:, 1, k:k + 1])
                act.activation(h32[:, s, CTX:ALL], t_lat(s), ACT.Identity, bias=modc[:, k, 0:1],
                               scale=amix[:, 0, k:k + 1]).then_inc(h32_ready, 1)
                act.wait_ge(h32_ready, k + 1)
                act.activation(h_hi[:, k, :], h32[:, s, :], ACT.Copy).then_inc(hhi_ready, 1)

            def conv_first(i, part, h, has_ctx):
                dst, j = (kT, NH + h) if part else (qT, h)
                act.wait_ge(tile_mm, i + 1)
                w = col("conv")[:, 2 * NH + j:2 * NH + j + 1]
                s = i % 2
                if part:
                    act.activation(dst[:, h, 0:CTX], t_ctx(s), ACT.Copy, scale=w)
                    act.activation(dst[:, h, CTX:ALL], t_lat(s), ACT.Copy, scale=w).then_inc(conv_mid, 1)
                else:
                    act.activation(dst[:, h, :], t_lat(s), ACT.Copy, scale=w).then_inc(conv_mid, 1)

            def conv_silu(i, part, h):
                act.wait_ge(conv_free, i - 1)
                v = (kT if part else qT)[:, h, :]
                act.activation(v, v, ACT.Silu).then_inc(conv_act, 1)

            split_hi(9)
            for t in range(2):
                act.wait_ge(tile_mm, t + 1)
                dst = gate_rows if t == 0 else row_f
                act.activation(dst[:, 0:CTX], t_ctx(t), ACT.Identity, bias=col("b_gates")[:, t:t + 1])
                act.activation(dst[:, CTX:ALL], t_lat(t), ACT.Identity, bias=col("b_gates")[:, t:t + 1]).then_inc(g_free, 1)
            split_hi(10)
            act.wait_ge(g_free, 2)
            act_link(act.activation(row_a[:], row_f[:], ACT.Abs))
            act_link(act.activation(row_a[:], row_a[:], ACT.Exp, scale=-1.0))
            act.activation(row_a[:], row_a[:], ACT.Ln, bias=1.0).then_inc(row_act, 1)
            conv_first(2, 1, 0, True)
            conv_first(3, 1, 1, True)
            act.wait_ge(row_dve, 1)
            act.activation(rows_na[:, 1, :], rows_na[:, 1, :], ACT.Exp).then_inc(row_act, 1)
            act.activation(row_f[:], row_f[:], ACT.Exp).then_inc(row_act, 1)
            act.activation(row_m[:], row_m[:], ACT.Exp, scale=-1.0, bias=ln_hd[:, 0:1]).then_inc(row_act, 1)
            split_hi(11)
            conv_silu(2, 1, 0)
            conv_silu(3, 1, 1)
            conv_first(4, 1, 2, True)
            conv_first(5, 1, 3, True)
            split_hi(12)
            conv_silu(4, 1, 2)
            conv_silu(5, 1, 3)
            conv_first(6, 0, 0, False)
            conv_first(7, 0, 1, False)
            split_hi(13)
            conv_silu(6, 0, 0)
            conv_silu(7, 0, 1)
            conv_first(8, 0, 2, False)
            conv_first(9, 0, 3, False)
            split_hi(14)
            conv_silu(8, 0, 2)
            conv_silu(9, 0, 3)
            act.wait_ge(stat_ready, 1)
            for u in range(2):
                for j in range(5):
                    p = 5 * u + j
                    if p % 2 == 0:
                        act.wait_ge(tok_mm, p + 1)
                        for r in range(2):
                            i = act.activation(v_ext[:, 2 * j + r, 2 * u:2 * u + 2, 0:HD], tokv(p, r), ACT.Copy)
                        i.then_inc(tok_act, 1)
            def ml_front(t, l, d, c):
                act.wait_ge(kt_mm, t + 1)
                at_least(act, kv_mm, t - 1)
                for h in range(NH):
                    i = act.activation(ml_kh[d][:, h, :], kt_ps[:, h, :], ACT.Copy,
                                       scale=cst[:, 1, ds(c, 1), NH * d + h])
                i.then_inc(kh_ready, 1)
                if l is not None:
                    act.wait_ge(d_ready, l + 1)
                    act.activation(ml_w[d][:], ml_w[d][:], ACT.Exp).then_inc(w_ready, 1)

            scan_steps(act, ml_front, lambda t, l, d, c: None)
            act.wait_ge(h_done, 2 * TL)
            act.activation(h_sq[:], h_ml[:], ACT.Square).then_inc(ml_norm, 1)
            act.wait_ge(ml_norm, 2)
            act.activation(hstat[:], hstat[:], ACT.Sqrt).then_inc(ml_norm, 1)
            act.wait_ge(num_mm, 2 * TL)
            act.activation(c32[:, 0, :, :], cc, ACT.Silu).then_inc(c_again, 1)

            def small_ada(n):
                kind, j = STREAM[n]
                if kind == "ada":
                    act.wait_ge(ada_rows, j + 1)
                    act.wait_ge(ada_cols, j - 1)
                    act.activation(mod_rows[:, j % 2, :], psum[:, 6 * BANK:6 * BANK + UW], ACT.Copy).then_inc(ada_evac, 1)

            split_hi(15)
            split_hi(16)
            for i in range(10, 14):
                act.wait_ge(tile_mm, i + 1)
                if i < 12:
                    act.activation(gk[:, i - 10, 0:CTX], t_ctx(i % 2), ACT.Copy)
                    act.activation(gk[:, i - 10, CTX:ALL], t_lat(i % 2), ACT.Copy).then_inc(g_free, 1)
                else:
                    act.activation(gq[:, i - 12, :], t_lat(i % 2), ACT.Copy, scale=GLA_SCALE).then_inc(g_free, 1)
                if i == 11:
                    split_hi(17)
            for n in range(17, AT["out", 0]):
                if n + 1 < AT["out", 0]:
                    split_hi(n + 1)
                kind, j = STREAM[n]
                if kind == "ada":
                    small_ada(n)
                    continue
                name = IN_UNITS[j]
                p0, pairs = PAIRS[name]
                u = int(name[-1])
                for q in range(pairs):
                    p = p0 + q
                    if name[:2] == "gv" and p % 2:
                        continue
                    act.wait_ge(tok_mm, p + 1)
                    src = psum[:, BANK * (p % TOK_BANKS):BANK * (p % TOK_BANKS + 1)].rearrange("p (r n) -> p r n", r=2)
                    if name[:2] == "gv":
                        act.activation(gv[:, 2 * q:2 * q + 2, UW * u:UW * (u + 1)], src, ACT.Copy).then_inc(tok_act, 1)
                    elif name[0] == "o":
                        act.activation(src, src, ACT.Sigmoid).then_inc(sig_done, 1)
                    else:
                        act.activation(ht_f[:, KC * u + 2 * q:KC * u + 2 * q + 2, 0:UW], src, ACT.Silu).then_inc(tok_act, 1)
            for i in range(4):
                act.wait_ge(tile_mm, 15 + i)
                act.activation(b_ctx[:, i, :], t_ctx(i % 2), ACT.Identity, bias=col("b_gla")[:, i:i + 1])
                act.activation(ht_f[:, i, CTX:ALL], t_lat(i % 2), ACT.Identity, bias=col("b_gla")[:, i:i + 1]).then_inc(z_out, 1)
            for i in range(4):
                act.wait_ge(z_out, i + 1)
                at_least(act, b_ready, i)
                pieces = ((l_ctx[:], b_ctx[:, i, :]), (ht_f[:, 4 + i, CTX:ALL], ht_f[:, i, CTX:ALL]))
                for tmp, z in pieces:
                    x = act.activation(tmp, z, ACT.Abs)
                x.then_inc(la_seq, 1)
                act.wait_ge(la_seq, 2 * i + 1)
                for tmp, z in pieces:
                    x = act.activation(tmp, tmp, ACT.Exp, scale=-1.0)
                x.then_inc(la_seq, 1)
                act.wait_ge(la_seq, 2 * i + 2)
                for tmp, z in pieces:
                    x = act.activation(tmp, tmp, ACT.Ln, bias=1.0)
                x.then_inc(la_tmp, 1)
            act.activation(mask_add[:], mask_add[:], ACT.Exp).then_inc(mask_exp, 1)
            act.wait_ge(cols_dve, 1)
            act.activation(gcol[:, 2:5, :, :], gcol[:, 2:5, :, :], ACT.Exp, scale=1.0 / TAU).then_inc(cols_act, 1)
            act.wait_ge(cols_act, 1)
            act.wait_ge(zero_g, 1)

            def b_of(dp, l, c):
                return b_ctx[:, dp, chunk_cols(c)] if l is None else ht_f[:, dp, chunk_cols(c)]

            def gla_front(t, l, d, c):
                at_least(act, gx_ready, t - 1)
                for i in range(2):
                    dp = 2 * d + i
                    x = act.activation(e_k[d][:, i, :], b_of(dp, l, c), ACT.Exp, scale=-1.0 / TAU, bias=gcol[:, 1, dp, ds(c, 1)])
                    if l is not None:
                        x = act.activation(e_q[d][:, i, :], b_of(dp, l, c), ACT.Exp, scale=1.0 / TAU, bias=gcol[:, 0, dp, ds(c, 1)])
                x.then_inc(e_ready, 1)
                if l is not None:
                    at_least(act, s_done, t - 1)
                    at_least(act, go_mm, l - 1)
                    for i in range(2):
                        x = act.activation(g_ps[:, d, i, :], g_s[:, d, i, :], ACT.Copy, scale=gcol[:, 2, 2 * d + i, ds(c, 1)])
                    x.then_inc(ps_ready, 1)
                act.wait_ge(gkt_mm, t + 1)
                at_least(act, gkv_mm, t - 1)
                act.activation(k_tok[d], gla_bank(d, 1, 2 * P).rearrange("p (i t) -> p i t", i=2), ACT.Copy).then_inc(gkh_ready, 1)

            def gla_back(t, l, d, c):
                act.wait_ge(gkv_mm, t + 1)
                for i in range(2):
                    v = gla_bank(d, 2, 4 * HD)[:, 2 * HD * i:2 * HD * (i + 1)]
                    x = act.activation(v, v, ACT.Copy, scale=gcol[:, 4, 2 * d + i, ds(c, 1)])
                x.then_inc(kvs_ready, 1)

            scan_steps(act, gla_front, gla_back)
            act.wait_ge(og_done, 2 * TL)
            act.wait_ge(s_done, 2 * TA)
            act.activation(y_gla[:], ht_f[:, KC:2 * KC, CTX:CTX + GV_W], ACT.Square).then_inc(gla_sq, 1)
            split_hi(AT["out", 0])
            split_hi(AT["out", 1])
            act.wait_ge(gla_sq, 2)
            act.activation(hstat[:], hstat[:], ACT.Sqrt).then_inc(gla_sq, 1)
            act.wait_ge(gla_sq, 4)
            for k in range(KC):
                act.wait_ge(yt_mm, k + 1)
                act.activation(yt_hi[:, k, :], t_lat(k % 2), ACT.Copy, scale=col("g_heads")[:, k:k + 1]).then_inc(yt_hi_ok, 1)

            def y_pair(u, q):
                p = PAIRS["out0"][0] + 4 * u + q
                src = psum[:, BANK * (p % TOK_BANKS):BANK * (p % TOK_BANKS + 1)].rearrange("p (r n) -> p r n", r=2)
                return p, src, y_out[:, 2 * q:2 * q + 2, UW * u:UW * (u + 1)]

            for u in range(4):
                for q in (0, 2):
                    p, src, dst = y_pair(u, q)
                    act.wait_ge(tok_mm, p + 1)
                    act.activation(dst, src, ACT.Copy).then_inc(tok_act, 1)
                if u < 2:
                    split_hi(AT["out", u + 2])
                if u < 3:
                    act.wait_ge(row_mm, u + 1)
                    act.activation(rowb[:, u, :], e_ps(6), ACT.Copy).then_inc(rowb_ready, 1)
            act.wait_ge(tok_act, 26)
            act.wait_ge(tok_dve, 26)
            act.wait_ge(rowb_ready, 3)
            for t in range(TL):
                at_least(act, y_ssq, t - 1)
                act.activation(e_ps(4 + 2 * (t % 2)), y_out[:, t, :], ACT.Square, accum_out=ssq[:, t:t + 1]).then_inc(y_ssq, 1)
            act.wait_ge(y_ssq, TL + 1)
            act.activation(rstd[:, 0:TL], ssq[:, 0:TL], ACT.Sqrt).then_inc(y_ssq, 1)
            for t in range(TL):
                act.wait_ge(x1_ready, t + 1)
                at_least(act, x_ssq, t - 1)
                act.activation(e_ps(4 + 2 * (t % 2)), x_res[:, t, :], ACT.Square, accum_out=ssq[:, TL + t:TL + t + 1]).then_inc(x_ssq, 1)
            act.wait_ge(x_ssq, TL + 1)
            act.activation(rstd[:, TL:2 * TL], ssq[:, TL:2 * TL], ACT.Sqrt).then_inc(x_ssq, 1)
            for t in range(TL):
                act.wait_ge(h2t_mm, t + 1)
                act.activation(h2t[:, :, P * t:P * (t + 1)], t_lat(t % 2).rearrange("p (k n) -> p k n", k=KC), ACT.Copy).then_inc(h2t_ready, 1)
            act.wait_ge(row_mm, 4)
            act.activation(row_g2[:], e_ps(6), ACT.Copy).then_inc(rowb_ready, 1)
            act.wait_ge(soft, 1)
            act.activation(e_lg[:], e_lg[:], ACT.Exp).then_inc(soft, 1)

            def e_split_hi(e, u):
                act.wait_ge(e_full[u], 16 * e + 16)
                act.wait_ge(w_used, EU * e + u + 1)
                act.activation(e_hi[u % 2][:], e_raw[u][:], ACT.Copy).then_inc(e_hi_ok, 1)

            def xt_hi_part(e):
                act.wait_ge(xt_mm, e + 1)
                act.activation(xt_hi[:].rearrange("p k n -> p (k n)"), e_ps(6), ACT.Copy).then_inc(xt_hi_ok, 1)

            def hd_hi_part(e, q):
                act.wait_ge(hd_mm, 4 * e + q + 1)
                act.activation(hd_hi[:, 2 * q:2 * q + 2, :], quarter(0, q).rearrange("p (k n) -> p k n", k=2), ACT.Copy).then_inc(hd_hi_ok, 1)

            def expert_act(e, last):
                for u in range(2, 6):
                    e_split_hi(e, u)
                act.wait_ge(w_used, EU * e + 4 + 2)
                act.activation(hid[:], e_ps(0), ACT.Silu).then_inc(sg_ok, 1)
                e_split_hi(e, 6)
                e_split_hi(e, 7)
                hd_hi_part(e, 0)
                e_split_hi(e, 8)
                hd_hi_part(e, 1)
                e_split_hi(e, 9)
                hd_hi_part(e, 2)
                if not last:
                    xt_hi_part(e + 1)
                hd_hi_part(e, 3)
                e_split_hi(e, 10)
                e_split_hi(e, 11)
                if not last:
                    e_split_hi(e + 1, 0)
                    e_split_hi(e + 1, 1)
                act.wait_ge(w_used, EU * e + EU + 2)
                act.wait_ge(y_taken, e + 1)
                act.activation(y_exp[:], e_ps(4), ACT.Copy, scale=gates[:, ds(e, 1)]).then_inc(y_free, 1)

            act.wait_ge(h2_stored, 16 * TL)
            act.nop().then_inc(y_free, 1)
            act.wait_ge(route_ready, 1)
            e_split_hi(0, 0)
            e_split_hi(0, 1)
            xt_hi_part(0)
            with act.Fori(0, N_EXP - 1) as e:
                expert_act(e, False)
            expert_act(N_EXP - 1, True)
            for j in range(4):
                act.wait_ge(acc_full[j], 16)
                for t in (2 * j, 2 * j + 1):
                    at_least(act, a_ssq, 4 * (j - 1) + 4)
                    act.activation(e_ps(4 + 2 * (t % 2)), acc[:, t, :], ACT.Square, accum_out=ssq[:, t:t + 1]).then_inc(a_ssq, 1)
                act.wait_ge(a_ssq, 4 * j + 3)
                act.activation(rstd[:, 2 * j:2 * j + 2], ssq[:, 2 * j:2 * j + 2], ACT.Sqrt).then_inc(a_ssq, 1)

        @block.vector
        def _(dve):
            n_dve = [0]

            def link(ins):
                n_dve[0] += 1
                ins.then_inc(dve_seq, 1)
                dve.wait_ge(dve_seq, n_dve[0])

            def split_lo(n):
                dve.wait_ge(hi_ready, n + 1)
                dve.tensor_tensor(w_lo[n % 2][:], raw[n % 2][:], w_hi[n % 2][:], ALU.subtract).then_inc(lo_ready, 1)

            link(dve.memset(c_st[:].bitcast(F32), 0.0))
            link(dve.memset(zero_r[:], 0.0))
            dve.wait_ge(c_silu, 1)
            link(dve.tensor_copy(c_st[:, :, 0:2], c32[:, 0, :, :]))
            dve.tensor_tensor(c_st[:, :, 2:4], c32[:, 0, :, :], c_st[:, :, 0:2], ALU.subtract).then_inc(c_ready, 1)
            dve.wait_ge(s_x, 32)
            dve.wait_ge(s_pos, 64)
            dve.tensor_tensor(xs[:, TC:TA, 0:D // 2], xs[:, TC:TA, 0:D // 2], pos_l[:], ALU.add)
            dve.tensor_tensor(xs[:, TC:TA, D // 2:D], xs[:, TC:TA, D // 2:D],
                              pos_c[:].unsqueeze(1).to_broadcast([P, TL, D // 2]), ALU.add).then_inc(xn_ready, 1)
            dve.memset(ln_hd[:], LN_HD).then_inc(ones_set, 1)
            dve.wait_ge(ssq_done, TA)
            dve.tensor_scalar(ssq[:, 0:TA], ssq[:, 0:TA], 1.0 / D, EPS, ALU.mult, ALU.add).then_inc(ssq_done, 1)
            dve.wait_ge(std_done, 1)
            link(dve.reciprocal(rstd[:, 0:TA], rstd[:, 0:TA]))
            for t in range(TA):
                dve.tensor_scalar(xs[:, t, :], xs[:, t, :], rstd[:, t:t + 1], None, ALU.mult).then_inc(xn_ready, 1)
            for n in range(8):
                split_lo(n)
            dve.wait_ge(ada_cols, 8)
            b = col("b_ada")[:, 0:2 * KC].unsqueeze(2).to_broadcast([P, 2 * KC, 2])
            link(dve.tensor_tensor(modc[:, 0:2 * KC, :], modps[:, 0:2 * KC, :], b, ALU.add))
            for r in range(2):
                i = dve.scalar_tensor_tensor(amix[:, r, :], modc[:, KC:2 * KC, r], 1.0, col("g_mix_pre"), ALU.add, ALU.mult)
            i.then_inc(mod1_ready, 1)
            split_lo(8)
            for k in range(KC):
                dve.wait_ge(hhi_ready, k + 1)
                dve.tensor_tensor(h_lo[:, k, :], h32[:, k % 2, :], h_hi[:, k, :], ALU.subtract).then_inc(h_ready, 1)
            split_lo(9)
            link(dve.memset(row_b[:], 0.0))
            link(dve.memset(row_m[:], 0.0))
            split_lo(10)

            dve.wait_ge(row_act, 1)
            link(dve.scalar_tensor_tensor(row_f[:], row_f[:], 0.0, row_a[:], ALU.min, ALU.subtract))
            for c in range(TA):
                a, z = P * c, P * (c + 1)
                dve.tensor_tensor_scan(row_b[0:NH, a:z], row_f[0:NH, a:z], zero_r[0:NH, :], 0.0, ALU.add, ALU.add)
                rb = row_b[32:32 + NH, a:z][:, ::-1]
                dve.tensor_tensor_scan(rb, row_f[32:32 + NH, a:z][:, ::-1], zero_r[32:32 + NH, :], 0.0, ALU.add, ALU.add)
            dve.tensor_tensor_scan(row_m[0:NH, :], row_f[0:NH, :], gate_rows[0:NH, :], 0.0, ALU.add, ALU.max)
            link(dve.tensor_tensor_scan(row_m[32:32 + NH, 0:CTX][:, ::-1], row_f[32:32 + NH, 0:CTX][:, ::-1],
                                        gate_rows[32:32 + NH, 0:CTX][:, ::-1], 0.0, ALU.add, ALU.max))
            link(dve.tensor_tensor_scan(row_m[32:32 + NH, CTX:ALL][:, ::-1], row_f[32:32 + NH, CTX:ALL][:, ::-1],
                                        gate_rows[32:32 + NH, CTX:ALL][:, ::-1], row_m[32:32 + NH, 0:1], ALU.add, ALU.max))
            link(dve.tensor_tensor(rows_na[:, 0, :], row_b[:], row_m[:], ALU.subtract))
            link(dve.memset(mprev[:], 0.0))
            dve.tensor_copy(mprev[0:NH, 1:TA], row_m[0:NH, P - 1:ALL - 1:P])
            dve.tensor_copy(mprev[32:32 + NH, TC:TA - 1], row_m[32:32 + NH, CTX + P:ALL:P])
            dve.tensor_copy(mprev[32:32 + NH, TA - 1:TA], row_m[32:32 + NH, 0:1])
            link(dve.tensor_copy(mprev[32:32 + NH, 0:1], row_m[32:32 + NH, P:P + 1]))
            r3 = lambda v: v.rearrange("p (c t) -> p c t", t=P)
            dve.tensor_tensor(r3(rows_na[:, 1, :]), r3(rows_na[:, 0, :]), mprev[:].unsqueeze(2).to_broadcast([P, TA, P]), ALU.add)
            link(dve.tensor_tensor(row_a[:], gate_rows[:], row_b[:], ALU.subtract))
            link(dve.memset(row_f[:], 0.0))
            for d in range(2):
                q = slice(32 * d, 32 * d + NH)
                end = r3(rows_na[q, 0, :])[:, :, (P - 1) * (1 - d):(P - 1) * (1 - d) + 1]
                i = dve.tensor_tensor(r3(row_f[q, :]), r3(row_a[q, :]), end.to_broadcast([NH, TA, P]), ALU.add)
            i.then_inc(row_dve, 1)

            def conv_taps(i, part, h):
                dst, j = (kT, NH + h) if part else (qT, h)
                wts = [col("conv")[:, 2 * NH * t + j:2 * NH * t + j + 1] for t in (0, 2)]
                dve.wait_ge(conv_mid, i - 1)
                s = i % 2
                segs = [(t_lat(s), dst[:, h, CTX:ALL] if part else dst[:, h, :], SEQ)]
                if part:
                    segs.append((t_ctx(s), dst[:, h, 0:CTX], CTX))
                for src, o, n in segs:
                    last = dve.scalar_tensor_tensor(o[:, 1:n], src[:, 0:n - 1], wts[0], o[:, 1:n], ALU.mult, ALU.add)
                link(last)
                for src, o, n in segs:
                    last = dve.scalar_tensor_tensor(o[:, 0:n - 1], src[:, 1:n], wts[1], o[:, 0:n - 1], ALU.mult, ALU.add)
                last.then_inc(conv_free, 1)

            conv_taps(2, 1, 0)
            conv_taps(3, 1, 1)
            split_lo(11)
            conv_taps(4, 1, 2)
            conv_taps(5, 1, 3)
            split_lo(12)
            conv_taps(6, 0, 0)
            conv_taps(7, 0, 1)
            split_lo(13)
            conv_taps(8, 0, 2)
            conv_taps(9, 0, 3)
            dve.wait_ge(stat_mm, 1)
            dve.tensor_copy(cst[:].rearrange("p q c s -> p (q c s)"), psum[:, 7 * BANK:7 * BANK + 3 * TA * 2 * NH]).then_inc(stat_ready, 1)
            split_lo(14)
            dve.memset(v_ext[:, :, :, HD:HD + 1], 1.0).then_inc(ones_set, 1)
            for u in range(2):
                for j in range(5):
                    p = 5 * u + j
                    if p % 2 == 1:
                        dve.wait_ge(tok_mm, p + 1)
                        for r in range(2):
                            i = dve.tensor_copy(v_ext[:, 2 * j + r, 2 * u:2 * u + 2, 0:HD], tokv(p, r))
                        i.then_inc(tok_dve, 1)
            def ml_front(t, l, d, c):
                dve.wait_ge(bc_mm, t + 1)
                at_least(dve, c_done, t - 1)
                if l is None:
                    dve.tensor_copy(decm[:, d, :], bc_ps[:, :, 1, (P - 1) * (1 - d)]).then_inc(bc_read, 1)
                    return
                dve.tensor_copy(decm[:, d, :], bc_ps[:, :, 1, (P - 1) * (1 - d)])
                at_least(dve, sw_ready, l - 1)
                for h in range(NH):
                    i = dve.scalar_tensor_tensor(ml_w[d][:, h, :], mask_add[:, d, :], cst[:, 0, ds(c, 1), NH * d + h],
                                                 bc_ps[:, h, 0, :], ALU.add, ALU.add)
                i.then_inc(d_ready, 1)
                at_least(dve, num_mm, l - 1)
                dve.tensor_tensor(ml_qs[d][:], qT[:, :, ds(P * (c - TC), P)], bc_ps[:, :, 1, :], ALU.mult).then_inc(bc_read, 1)
                dve.wait_ge(w_ready, l + 1)
                dve.wait_ge(st_mm, l + 1)
                dve.tensor_tensor(ml_sw[d][:], st_ps[:], ml_w[d][:], ALU.mult).then_inc(sw_ready, 1)

            def ml_back(t, l, d, c):
                dve.wait_ge(kv_mm, t + 1)
                dve.wait_ge(bc_read, t + 1)
                if l is not None:
                    dve.wait_ge(num_mm, l + 1)
                at_least(dve, c_done, t)
                for h in range(NH):
                    i = dve.scalar_tensor_tensor(ml_c[:, d, h, :], ml_c[:, d, h, :], decm[:, d, h:h + 1],
                                                 kv_ps[:, h // 2, h % 2, :], ALU.mult, ALU.add)
                i.then_inc(c_done, 1)
                if l is None:
                    return
                dn = den[:, d, :].rearrange("p (b j) -> p b j", b=2)
                fl = cst[:, 2, ds(c, 1), NH * d:NH * d + NH].rearrange("p o (b j) -> p (o b) j", b=2)
                dve.tensor_tensor(dn, num_ps[:, :, :, HD], fl, ALU.max).then_inc(den_seq, 1)
                dve.wait_ge(den_seq, 3 * l + 1)
                dve.scalar_tensor_tensor(dn, num_ps[:, :, :, HD], -1.0, dn, ALU.mult, ALU.max).then_inc(den_seq, 1)
                dve.wait_ge(den_seq, 3 * l + 2)
                dve.reciprocal(den[:, d, :], den[:, d, :]).then_inc(den_seq, 1)
                dve.wait_ge(den_seq, 3 * l + 3)
                at_least(dve, h_done, l)
                for h in range(NH):
                    o = h_ml[:, ds(c - TC, 1), HD * h:HD * (h + 1)].rearrange("p o n -> p (o n)")
                    i = dve.scalar_tensor_tensor(o, num_ps[:, h // 2, h % 2, 0:HD], den[:, d, h:h + 1], o, ALU.mult, ALU.add)
                i.then_inc(h_done, 1)

            dve.wait_ge(ml_zero, 5)
            scan_steps(dve, ml_front, ml_back)
            dve.wait_ge(ml_norm, 1)
            link(dve.tensor_reduce(hstat[:], h_sq[:].rearrange("p t (h n) -> p (t h) n", h=NH), AX.X, ALU.add))
            dve.tensor_scalar(hstat[:], hstat[:], 1.0 / HD, EPS, ALU.mult, ALU.add).then_inc(ml_norm, 1)
            dve.wait_ge(ml_norm, 3)
            link(dve.reciprocal(hstat[:], hstat[:]))
            v4 = lambda v: v.rearrange("p t (h n) -> p (t h) n", h=NH)
            dve.tensor_tensor(v4(y_ml[:]), v4(h_ml[:]), hstat[:].unsqueeze(2).to_broadcast([P, TL * NH, HD]),
                              ALU.mult).then_inc(ml_norm, 1)
            dve.wait_ge(c_again, 1)
            link(dve.memset(c_st[:].bitcast(F32), 0.0))
            link(dve.tensor_copy(c_st[:, :, 0:2], c32[:, 0, :, :]))
            dve.tensor_tensor(c_st[:, :, 2:4], c32[:, 0, :, :], c_st[:, :, 0:2], ALU.subtract).then_inc(c_ready, 1)
            dve.wait_ge(ml_norm, 4)
            split_lo(15)
            split_lo(16)
            split_lo(17)
            for n in range(17, AT["out", 0]):
                if n + 1 < AT["out", 0]:
                    split_lo(n + 1)
                kind, j = STREAM[n]
                if kind == "ada" or IN_UNITS[j][0] == "r":
                    continue
                name = IN_UNITS[j]
                p0, pairs = PAIRS[name]
                u = int(name[-1])
                for q in range(pairs):
                    p = p0 + q
                    src = psum[:, BANK * (p % TOK_BANKS):BANK * (p % TOK_BANKS + 1)].rearrange("p (r n) -> p r n", r=2)
                    if name[:2] == "gv":
                        if p % 2:
                            dve.wait_ge(tok_mm, p + 1)
                            dve.tensor_copy(gv[:, 2 * q:2 * q + 2, UW * u:UW * (u + 1)], src).then_inc(tok_dve, 1)
                    else:
                        dve.wait_ge(sig_done, p - PAIRS["o0"][0] + 1)
                        y = y_ml[:, 2 * q:2 * q + 2, UW * u:UW * (u + 1)]
                        dve.tensor_tensor(y, y, src, ALU.mult).then_inc(tok_dve, 1)
            dve.wait_ge(ada_cols, 24)
            b2 = col("b_ada")[:, 2 * KC:].unsqueeze(2).to_broadcast([P, 4 * KC, 2])
            link(dve.tensor_tensor(modc[:, 2 * KC:, :], modps[:, 2 * KC:, :], b2, ALU.add))
            for i in range(4):
                dve.wait_ge(la_tmp, i + 1)
                dve.scalar_tensor_tensor(b_ctx[:, i, :], b_ctx[:, i, :], 0.0, l_ctx[:], ALU.min, ALU.subtract)
                link(dve.scalar_tensor_tensor(ht_f[:, i, CTX:ALL], ht_f[:, i, CTX:ALL], 0.0, ht_f[:, 4 + i, CTX:ALL],
                                              ALU.min, ALU.subtract))
                for c in range(TA):
                    v = b_ctx[:, i, P * c:P * (c + 1)] if c < TC else ht_f[:, i, P * c:P * (c + 1)]
                    if i >= 2:
                        v = v[:, ::-1]
                    x = dve.tensor_tensor_scan(v, v, zero_r[:], 0.0, ALU.add, ALU.add)
                link(x)
                for q, pos in ((2, P // 2 - 1 if i < 2 else P // 2), (3, P - 1 if i < 2 else 0)):
                    dve.tensor_copy(gcol[:, q, i, 0:TC], b_ctx[:, i, pos::P])
                    x = dve.tensor_copy(gcol[:, q, i, TC:TA], ht_f[:, i, CTX + pos::P])
                x.then_inc(b_ready, 1)
            dve.wait_ge(b_ready, 4)
            dve.tensor_scalar(gcol[:, 0, :, :], gcol[:, 2, :, :], -1.0 / TAU, None, ALU.mult)
            dve.tensor_scalar(gcol[:, 1, :, :], gcol[:, 2, :, :], 1.0 / TAU, None, ALU.mult)
            dve.tensor_tensor(gcol[:, 4, :, :], gcol[:, 3, :, :], gcol[:, 2, :, :], ALU.subtract).then_inc(cols_dve, 1)

            def gla_front(t, l, d, c):
                dve.wait_ge(e_ready, t + 1)
                at_least(dve, gkt_mm, t - 1)
                if l is not None:
                    at_least(dve, go_mm, l - 1)
                    for h in range(2):
                        q = slice(64 * h, 64 * h + 64)
                        dve.tensor_tensor(qz[d][q, :, h, :], gq[q, :, ds(P * (c - TC), P)], e_q[d][q, :, :], ALU.mult)
                dve.tensor_tensor(kx[d], gk[:, :, chunk_cols(c)], e_k[d], ALU.mult).then_inc(gx_ready, 1)
                if l is not None:
                    dve.wait_ge(gst_mm, l + 1)
                    dve.tensor_tensor(g_a[d], gla_bank(d, 0, 512).rearrange("p (h t) -> p h t", h=NH),
                                      mask_add[:, d, :].unsqueeze(1).to_broadcast([P, NH, P]), ALU.mult).then_inc(a_ready, 1)

            def gla_back(t, l, d, c):
                dve.wait_ge(kvs_ready, t + 1)
                if l is not None:
                    dve.wait_ge(ps_ready, l + 1)
                at_least(dve, s_done, t - 1)
                for i in range(2):
                    x = dve.scalar_tensor_tensor(g_s[:, d, i, :], g_s[:, d, i, :], gcol[:, 3, 2 * d + i, ds(c, 1)],
                                                 gla_bank(d, 2, 4 * HD)[:, 2 * HD * i:2 * HD * (i + 1)], ALU.mult, ALU.add)
                x.then_inc(s_done, 1)
                if l is not None:
                    dve.wait_ge(go_mm, l + 1)
                    at_least(dve, og_done, l)
                    o = ht_f[:, ds(KC + c - TC, 1), CTX:CTX + GV_W]
                    dve.tensor_tensor(o, o, gla_bank(d, 3, 512).unsqueeze(1), ALU.add).then_inc(og_done, 1)

            dve.wait_ge(mask_exp, 1)
            dve.wait_ge(cols_act, 1)
            dve.wait_ge(zero_g, 1)
            scan_steps(dve, gla_front, gla_back)
            v4g = lambda v: v.rearrange("p t (h n) -> p (t h) n", h=NH)
            dve.wait_ge(gla_sq, 1)
            link(dve.tensor_reduce(hstat[:], v4g(y_gla[:]), AX.X, ALU.add))
            dve.tensor_scalar(hstat[:], hstat[:], 1.0 / HD, EPS, ALU.mult, ALU.add).then_inc(gla_sq, 1)
            split_lo(AT["out", 0])
            split_lo(AT["out", 1])
            dve.wait_ge(gla_sq, 3)
            link(dve.reciprocal(hstat[:], hstat[:]))
            for h in range(NH):
                o = slice(HD * h, HD * (h + 1))
                i = dve.tensor_tensor(y_gla[:, :, o], ht_f[:, KC:2 * KC, CTX + HD * h:CTX + HD * (h + 1)],
                                      hstat[:, h::NH].unsqueeze(2).to_broadcast([P, TL, HD]), ALU.mult)
            link(i)
            for u in range(2):
                y = y_gla[:, :, UW * u:UW * (u + 1)]
                i = dve.tensor_tensor(y, y, ht_f[:, KC * u:KC * (u + 1), 0:UW], ALU.mult)
            i.then_inc(gla_sq, 1)
            dve.memset(ones_m[:], 1.0)
            part = lambda j: modc[:, KC * j:KC * (j + 1), 0]
            dve.tensor_tensor(vec_c[:, 0, :], part(2), col("g_mix_post"), ALU.mult)
            dve.scalar_tensor_tensor(vec_c[:, 1, :], part(4), 1.0, col("g_ffn_pre"), ALU.add, ALU.mult)
            dve.tensor_copy(vec_c[:, 2, :], part(3))
            link(dve.tensor_tensor(vec_c[:, 3, :], part(5), col("g_ffn_post"), ALU.mult))

            def make_diag(dst, q):
                dve.tensor_tensor(dst[:], ident[:].unsqueeze(1).to_broadcast([P, KC, P]),
                                  vec_c[:, q, :].unsqueeze(2).to_broadcast([P, KC, P]), ALU.mult).then_inc(diag_ready, 1)

            dve.wait_ge(gla_sq, 4)
            make_diag(diag, 0)
            for k in range(KC):
                dve.wait_ge(yt_hi_ok, k + 1)
                dve.scalar_tensor_tensor(yt_lo[:, k, :], t_lat(k % 2), col("g_heads")[:, k:k + 1], yt_hi[:, k, :],
                                         ALU.mult, ALU.subtract).then_inc(yt_lo_ok, 1)
            for u in range(4):
                for q in (1, 3):
                    p = PAIRS["out0"][0] + 4 * u + q
                    src = psum[:, BANK * (p % TOK_BANKS):BANK * (p % TOK_BANKS + 1)].rearrange("p (r n) -> p r n", r=2)
                    dve.wait_ge(tok_mm, p + 1)
                    dve.tensor_copy(y_out[:, 2 * q:2 * q + 2, UW * u:UW * (u + 1)], src).then_inc(tok_dve, 1)
                if u < 2:
                    split_lo(AT["out", u + 2])
                    dve.wait_ge(row_mm, u + 1)
                    make_diag(diag, u + 1)
            dve.wait_ge(y_ssq, TL)
            dve.tensor_scalar(ssq[:, 0:TL], ssq[:, 0:TL], 1.0 / D, EPS, ALU.mult, ALU.add).then_inc(y_ssq, 1)
            dve.wait_ge(y_ssq, TL + 2)
            link(dve.reciprocal(rstd[:, 0:TL], rstd[:, 0:TL]))
            dve.wait_ge(rowb_ready, 3)
            dve.wait_ge(pos_added, 2)
            for t in range(TL + 1):
                if t < TL:
                    dve.scalar_tensor_tensor(y_out[:, t, :], y_out[:, t, :], rstd[:, t:t + 1], rowb[:, 0, :], ALU.mult, ALU.mult).then_inc(y_scaled, 1)
                if t:
                    dve.wait_ge(y_scaled, t)
                    dve.tensor_tensor(x_res[:, t - 1, :], x_res[:, t - 1, :], y_out[:, t - 1, :], ALU.add).then_inc(x1_ready, 1)
            dve.wait_ge(x1_ready, TL)
            make_diag(diag2, 3)
            dve.wait_ge(x_ssq, TL)
            dve.tensor_scalar(ssq[:, TL:2 * TL], ssq[:, TL:2 * TL], 1.0 / D, EPS, ALU.mult, ALU.add).then_inc(x_ssq, 1)
            dve.wait_ge(x_ssq, TL + 2)
            link(dve.reciprocal(rstd[:, TL:2 * TL], rstd[:, TL:2 * TL]))
            for t in range(TL + 1):
                if t < TL:
                    dve.scalar_tensor_tensor(h2[:, t, :], x_res[:, t, :], rstd[:, TL + t:TL + t + 1], rowb[:, 1, :], ALU.mult, ALU.mult).then_inc(h2_mid, 1)
                if t:
                    dve.wait_ge(h2_mid, t)
                    dve.tensor_tensor(h2[:, t - 1, :], h2[:, t - 1, :], rowb[:, 2, :], ALU.add).then_inc(h2_ready, 1)
            link(dve.memset(vals[:], 0.0))
            link(dve.memset(idx_f[:], 0.0))
            dve.wait_ge(lg_mm, TL)
            lg = psum[:, 2 * BANK:2 * BANK + TL * N_EXP].rearrange("p (t e) -> p t e", t=TL)
            wide = lambda v: v.unsqueeze(2).to_broadcast([P, TL, N_EXP])
            link(dve.tensor_reduce(ssq[:, 0:TL], lg, AX.X, ALU.max))
            dve.tensor_tensor(e_lg[:], lg, wide(ssq[:, 0:TL]), ALU.subtract).then_inc(soft, 1)
            dve.wait_ge(soft, 2)
            link(dve.tensor_reduce(ssq[:, 0:TL], e_lg[:], AX.X, ALU.add))
            link(dve.reciprocal(ssq[:, 0:TL], ssq[:, 0:TL]))
            dve.tensor_tensor(e_lg[:], e_lg[:], wide(ssq[:, 0:TL]), ALU.mult).then_inc(soft, 1)
            dve.wait_ge(aff_mm, 1)
            dve.tensor_copy(aff_t[0:N_EXP, :], psum[0:N_EXP, 0:SEQ]).then_inc(topk, 1)
            got = slice(0, N_EXP)
            for r in range(CAP // 8):
                best, where = vals[got, 8 * r:8 * r + 8], idx_u[got, 8 * r:8 * r + 8]
                dve.wait_ge(topk, 3 * r + 1)
                dve.max(best, aff_t[got, :]).then_inc(topk, 1)
                dve.wait_ge(topk, 3 * r + 2)
                dve.max_index(where, best, aff_t[got, :]).then_inc(topk, 1)
                dve.wait_ge(topk, 3 * r + 3)
                dve.match_replace(aff_t[got, :], best, aff_t[got, :], -1.0).then_inc(topk, 1)
            dve.wait_ge(topk, 3 * (CAP // 8) + 1)
            dve.tensor_copy(idx_f[got, :], idx_u[got, :]).then_inc(topk, 1)
            dve.wait_ge(sel_mm, 1)
            dve.tensor_copy(gates[:], psum[:, 0:N_EXP])
            dve.tensor_copy(tokens[:], psum[:, P:P + N_EXP]).then_inc(route_ready, 1)

            def e_split_lo(e, u):
                dve.wait_ge(e_hi_ok, EU * e + u + 1)
                dve.tensor_tensor(e_lo[u % 2][:], e_raw[u][:], e_hi[u % 2][:], ALU.subtract).then_inc(e_lo_ok, 1)

            def xt_lo_part(e):
                dve.wait_ge(xt_hi_ok, e + 1)
                dve.tensor_tensor(xt_lo[:].rearrange("p k n -> p (k n)"), e_ps(6), xt_hi[:].rearrange("p k n -> p (k n)"),
                                  ALU.subtract).then_inc(xt_ok, 1)

            def hid_part(e, q):
                if q == 0:
                    dve.wait_ge(sg_ok, e + 1)
                dve.wait_ge(w_used, EU * e + 4 + q + 1 + 2)
                h = hid[:, UW * q:UW * (q + 1)]
                dve.tensor_tensor(h, h, quarter(2, q), ALU.mult).then_inc(hid_ok, 1)

            def hd_lo_part(e, q):
                dve.wait_ge(hd_hi_ok, 4 * e + q + 1)
                dve.tensor_tensor(hd_lo[:, 2 * q:2 * q + 2, :], quarter(0, q).rearrange("p (k n) -> p k n", k=2),
                                  hd_hi[:, 2 * q:2 * q + 2, :], ALU.subtract).then_inc(hd_ok, 1)

            def expert_dve(e, last):
                for u in range(2, 6):
                    e_split_lo(e, u)
                hid_part(e, 0)
                e_split_lo(e, 6)
                hid_part(e, 1)
                hd_lo_part(e, 0)
                e_split_lo(e, 7)
                hid_part(e, 2)
                hd_lo_part(e, 1)
                e_split_lo(e, 8)
                hid_part(e, 3)
                hd_lo_part(e, 2)
                e_split_lo(e, 9)
                if not last:
                    xt_lo_part(e + 1)
                hd_lo_part(e, 3)
                e_split_lo(e, 10)
                e_split_lo(e, 11)
                if not last:
                    e_split_lo(e + 1, 0)
                    e_split_lo(e + 1, 1)

            e_split_lo(0, 0)
            e_split_lo(0, 1)
            xt_lo_part(0)
            with dve.Fori(0, N_EXP - 1) as e:
                expert_dve(e, False)
            expert_dve(N_EXP - 1, True)
            for j in range(4):
                pr = slice(2 * j, 2 * j + 2)
                dve.wait_ge(a_ssq, 4 * j + 2)
                dve.tensor_scalar(ssq[:, pr], ssq[:, pr], 1.0 / D, EPS, ALU.mult, ALU.add).then_inc(a_ssq, 1)
                dve.wait_ge(a_ssq, 4 * j + 4)
                link(dve.reciprocal(rstd[:, pr], rstd[:, pr]))
                for t in (2 * j, 2 * j + 1):
                    dve.scalar_tensor_tensor(acc[:, t, :], acc[:, t, :], rstd[:, t:t + 1], row_g2[:], ALU.mult, ALU.mult).then_inc(o_mid, 1)
                for t in (2 * j, 2 * j + 1):
                    dve.wait_ge(o_mid, t + 1)
                    dve.tensor_tensor(x_res[:, t, :], x_res[:, t, :], acc[:, t, :], ALU.add).then_inc(o_ready, 1)

        @block.tensor
        def _(pe):
            def unit_ready(n):
                pe.wait_ge(hi_ready, n + 1)
                pe.wait_ge(lo_ready, n + 1)

            pe.wait_ge(c_ready, 1)

            def ada_to_cols(n):
                pe.wait_ge(ada_evac, n + 1)
                for j in range(2):
                    i = pe.matmul(modps[:, 2 * n + j, :], mod_rows[:, n % 2, P * j:P * (j + 1)], one_s[:],
                                  start=True, stop=True)
                i.then_inc(ada_cols, 1)

            pe.wait_ge(konst, 11)
            for n in range(8):
                unit_ready(n)
                if n >= 2:
                    pe.wait_ge(ada_evac, n - 1)
                o = psum[:, BANK * (n % 2):BANK * (n % 2) + UW]
                for k in range(KC):
                    pe.matmul(o, c_st[:, k, :], w_hi[n % 2][:, k, :], start=k == 0, stop=False)
                for k in range(KC):
                    i = pe.matmul(o, c_st[:, k, :], w_lo[n % 2][:, k, :], start=False, stop=k == KC - 1)
                i.then_inc(ada_rows, 1)
                if n:
                    ada_to_cols(n - 1)
            ada_to_cols(7)
            pe.wait_ge(xn_ready, 1 + TA)
            for k in range(KC):
                if k >= 2:
                    pe.wait_ge(h32_ready, k - 1)
                s = k % 2
                for t in range(TA):
                    o = t_ctx(s)[:, P * t:P * (t + 1)] if t < TC else t_lat(s)[:, P * (t - TC):P * (t - TC + 1)]
                    i = pe.transpose(o, xs[:, t, P * k:P * (k + 1)], ident[:])
                i.then_inc(xt_ready, 1)
            pe.wait_ge(h_ready, KC)

            def t_tile(i, n, j, has_ctx):
                s, m = i % 2, n % 2
                c = slice(P * j, P * (j + 1))
                for k in range(KC):
                    for w, h in ((w_hi, h_hi), (w_hi, h_lo), (w_lo, h_hi)):
                        a, z = k == 0 and w is w_hi and h is h_hi, k == KC - 1 and w is w_lo
                        for q in range(2):
                            last = pe.matmul(t_lat(s)[:, BANK * q:BANK * (q + 1)], w[m][:, k, c],
                                             h[:, k, CTX + BANK * q:CTX + BANK * (q + 1)], start=a, stop=z)
                        if has_ctx:
                            last = pe.matmul(t_ctx(s), w[m][:, k, c], h[:, k, 0:CTX], start=a, stop=z)
                return last

            def t_unit(n, i0, has_ctx, free):
                unit_ready(n)
                for j in range(2):
                    if free is not None:
                        pe.wait_ge(free, i0 + j - 1 - (2 if free is conv_free else 0))
                    last = t_tile(i0 + j, n, j, has_ctx)
                    if j == 0:
                        last.then_inc(tile_mm, 1)
                last.then_inc(tile_mm, 1)

            t_unit(8, 0, True, None)
            t_unit(9, 2, True, g_free)
            t_unit(10, 4, True, conv_free)
            t_unit(11, 6, False, conv_free)
            t_unit(12, 8, False, conv_free)
            pe.wait_ge(row_act, 4)
            for q, src in enumerate((row_a, row_f, row_m)):
                for c in range(TA):
                    o = 7 * BANK + (q * TA + c) * 2 * NH
                    last = pe.matmul(psum[:, o:o + 2 * NH], src[:, P * c:P * (c + 1)], sel_s[:], start=True, stop=True)
            last.then_inc(stat_mm, 1)

            def tok_unit(name, n, x_hi, x_lo, t0):
                unit_ready(n)
                p0, pairs = PAIRS[name]
                for j in range(pairs):
                    p = p0 + j
                    if p >= TOK_BANKS:
                        pair_out(pe, p - TOK_BANKS)
                    for r in range(2):
                        c = slice(P * (t0 + 2 * j + r), P * (t0 + 2 * j + r + 1))
                        o = tok_ps(p, r)
                        for k in range(KC):
                            pe.matmul(o, x_hi[:, k, c], w_hi[n % 2][:, k, :], start=k == 0, stop=False)
                            pe.matmul(o, x_lo[:, k, c], w_hi[n % 2][:, k, :], start=False, stop=False)
                            last = pe.matmul(o, x_hi[:, k, c], w_lo[n % 2][:, k, :], start=False, stop=k == KC - 1)
                    last.then_inc(tok_mm, 1)

            pe.wait_ge(conv_free, 8)
            pe.wait_ge(stat_ready, 1)
            tok_unit("v0", 13, h_hi, h_lo, 0)
            tok_unit("v1", 14, h_hi, h_lo, 0)
            def ml_front(t, l, d, c):
                pe.wait_ge(kst_ready, t + 1)
                at_least(pe, bc_read, t)
                for h in range(NH):
                    i = pe.matmul(bc_ps[:, h, :, :], sel_r[:, NH * d + h, :], rows_na[:, :, chunk_cols(c)], start=True, stop=True)
                i.then_inc(bc_mm, 1)
                if l is not None:
                    at_least(pe, sw_ready, l)
                    for h in range(NH):
                        i = pe.matmul(st_ps[:, h, :], ml_ks[d][:, h, :], qT[:, h, ds(P * (c - TC), P)], start=True, stop=True)
                    i.then_inc(st_mm, 1)
                at_least(pe, kh_ready, t)
                for h in range(NH):
                    i = pe.transpose(kt_ps[:, h, :], ml_ks[d][:, h, :], ident[:])
                i.then_inc(kt_mm, 1)

            def ml_back(t, l, d, c):
                pe.wait_ge(kh_ready, t + 1)
                at_least(pe, c_done, t)
                vc = lambda h: v_ext[:, ds(c, 1), h, :]
                for h in range(NH):
                    i = pe.matmul(kv_ps[:, h // 2, h % 2, :], ml_kh[d][:, h, :], vc(h), start=True, stop=True)
                i.then_inc(kv_mm, 1)
                if l is None:
                    return
                pe.wait_ge(sw_ready, l + 1)
                at_least(pe, h_done, l)
                for h in range(NH):
                    o = num_ps[:, h // 2, h % 2, :]
                    pe.matmul(o, ml_sw[d][:, h, :], vc(h), start=True, stop=False)
                    i = pe.matmul(o, ml_qs[d][:, h, :], ml_c[:, d, h, :], start=False, stop=True)
                i.then_inc(num_mm, 1)

            pe.wait_ge(ml_zero, 5)
            pe.wait_ge(conv_act, 8)
            pe.wait_ge(tok_act, 5)
            pe.wait_ge(tok_dve, 5)
            pe.wait_ge(ones_set, 2)
            scan_steps(pe, ml_front, ml_back)
            pe.wait_ge(h_done, 2 * TL)
            pe.wait_ge(c_done, 2 * TA)
            t_unit(15, 10, True, None)
            unit_ready(16)
            for i in (12, 13):
                pe.wait_ge(g_free, i - 9)
                t_tile(i, 16, i - 12, False).then_inc(tile_mm, 1)
            pe.wait_ge(g_free, 6)
            pe.wait_ge(c_ready, 2)
            for n in range(17, AT["out", 0]):
                kind, j = STREAM[n]
                if kind == "in":
                    name = IN_UNITS[j]
                    tok_unit(name, n, h_hi, h_lo, 0 if name[:2] == "gv" else TC)
                    continue
                unit_ready(n)
                pe.wait_ge(ada_evac, j)
                o = psum[:, 6 * BANK:6 * BANK + UW]
                for k in range(KC):
                    pe.matmul(o, c_st[:, k, :], w_hi[n % 2][:, k, :], start=k == 0, stop=False)
                for k in range(KC):
                    i = pe.matmul(o, c_st[:, k, :], w_lo[n % 2][:, k, :], start=False, stop=k == KC - 1)
                i.then_inc(ada_rows, 1)
                if j > 8:
                    ada_to_cols(j - 1)
            ada_to_cols(23)
            pair_out(pe, PAIRS["r1"][0] + 3)
            for i in range(4):
                if i >= 2:
                    pe.wait_ge(z_out, i - 1)
                w = col("w_gla2")[:, P * i:P * (i + 1)]
                for q in range(2):
                    pe.matmul(t_lat(i % 2)[:, BANK * q:BANK * (q + 1)], w, gate_rows[:, CTX + BANK * q:CTX + BANK * (q + 1)],
                              start=True, stop=True)
                pe.matmul(t_ctx(i % 2), w, gate_rows[:, 0:CTX], start=True, stop=True).then_inc(tile_mm, 1)

            def gla_front(t, l, d, c):
                pe.wait_ge(gx_ready, t + 1)
                if l is not None:
                    at_least(pe, a_ready, l - 1)
                    for i in range(2):
                        x = pe.matmul(gla_bank(d, 0, 512)[:, 2 * P * i:2 * P * (i + 1)], kx[d][:, i, :],
                                      qz[d][:, i, :, :], start=True, stop=True)
                    x.then_inc(gst_mm, 1)
                at_least(pe, gkh_ready, t - 1)
                for i in range(2):
                    x = pe.transpose(gla_bank(d, 1, 2 * P)[:, P * i:P * (i + 1)], kx[d][:, i, :], ident[:])
                x.then_inc(gkt_mm, 1)

            def gla_back(t, l, d, c):
                pe.wait_ge(gkh_ready, t + 1)
                at_least(pe, s_done, t - 1)
                for i in range(2):
                    x = pe.matmul(gla_bank(d, 2, 4 * HD)[:, 2 * HD * i:2 * HD * (i + 1)], k_tok[d][:, i, :],
                                  gv[:, ds(c, 1), 2 * HD * i:2 * HD * (i + 1)], start=True, stop=True)
                x.then_inc(gkv_mm, 1)
                if l is None:
                    return
                pe.wait_ge(a_ready, l + 1)
                pe.wait_ge(ps_ready, l + 1)
                at_least(pe, og_done, l - 1)
                for h in range(NH):
                    o = gla_bank(d, 3, 512)[:, HD * h:HD * (h + 1)]
                    pe.matmul(o, g_a[d][:, h, :], gv[:, ds(c, 1), HD * h:HD * (h + 1)], start=True, stop=False)
                    x = pe.matmul(o, qz[d][:, h // 2, h % 2, :], g_ps[:, d, h // 2, HD * (h % 2):HD * (h % 2 + 1)],
                                  start=False, stop=True)
                x.then_inc(go_mm, 1)

            pe.wait_ge(z_out, 4)
            pe.wait_ge(tok_dve, 18)
            pe.wait_ge(zero_g, 1)
            scan_steps(pe, gla_front, gla_back)
            pe.wait_ge(og_done, 2 * TL)
            pe.wait_ge(s_done, 2 * TA)
            for k in range(KC):
                if k == KC // 2:
                    pe.wait_ge(gla_sq, 4)
                at_least(pe, yt_lo_ok, k - 1)
                y = y_ml if k < KC // 2 else y_gla
                for t in range(TL):
                    i = pe.transpose(t_lat(k % 2)[:, P * t:P * (t + 1)], y[:, t, P * (k % 4):P * (k % 4 + 1)], ident[:])
                i.then_inc(yt_mm, 1)

            def row_product(q, d):
                pe.wait_ge(diag_ready, q + 1)
                at_least(pe, rowb_ready, q)
                for b in range(2):
                    i = pe.matmul(psum[:, (6 + b) * BANK:(7 + b) * BANK], ones_m[:], d[:, 4 * b:4 * b + 4, :], start=True, stop=True)
                i.then_inc(row_mm, 1)

            pe.wait_ge(yt_lo_ok, KC)
            for u in range(4):
                tok_unit(f"out{u}", AT["out", u], yt_hi, yt_lo, 0)
                if u < 3:
                    row_product(u, diag)
            pe.wait_ge(x_ssq, TL)
            row_product(3, diag2)
            w_r = col("w_router").rearrange("p (k e) -> p k e", k=KC)

            def logits(t):
                pe.wait_ge(h2t_ready, t + 1)
                for k in range(KC):
                    i = pe.matmul(psum[:, 2 * BANK + N_EXP * t:2 * BANK + N_EXP * (t + 1)], h2t[:, k, P * t:P * (t + 1)], w_r[:, k, :],
                                  start=k == 0, stop=k == KC - 1)
                i.then_inc(lg_mm, 1)

            for t in range(TL):
                pe.wait_ge(h2_ready, t + 1)
                at_least(pe, h2t_ready, t - 1)
                for k in range(KC):
                    i = pe.transpose(t_lat(t % 2)[:, P * k:P * (k + 1)], h2[:, t, P * k:P * (k + 1)], ident[:])
                i.then_inc(h2t_mm, 1)
                if t:
                    logits(t - 1)
            logits(TL - 1)
            pe.wait_ge(soft, 3)
            for t in range(TL):
                i = pe.transpose(psum[0:N_EXP, P * t:P * (t + 1)], e_lg[:, t, :], ident[:])
            i.then_inc(aff_mm, 1)
            pe.wait_ge(topk, 3 * (CAP // 8) + 2)
            pe.transpose(psum[:, 0:P], vals[:], ident[:])
            pe.transpose(psum[:, P:2 * P], idx_f[:], ident[:]).then_inc(sel_mm, 1)

            def e_unit(e, u, x_hi, x_lo, o):
                pe.wait_ge(e_lo_ok, EU * e + u + 1)
                hi, lo = e_hi[u % 2], e_lo[u % 2]
                if 4 <= u < 8:
                    for k in range(KC):
                        c = slice(UW * k, UW * (k + 1))
                        pe.matmul(o, x_hi[:, k, :], hi[:, c], start=k == 0, stop=False)
                        pe.matmul(o, x_lo[:, k, :], hi[:, c], start=False, stop=False)
                        i = pe.matmul(o, x_hi[:, k, :], lo[:, c], start=False, stop=k == KC - 1)
                else:
                    for j in range(2):
                        k = 2 * (u % 4) + j
                        for x, w in ((x_hi, hi), (x_hi, lo), (x_lo, hi)):
                            a, z = k == 0 and x is x_hi and w is hi, k == KC - 1 and x is x_lo
                            for b in range(2):
                                i = pe.matmul(o[:, BANK * b:BANK * (b + 1)], x[:, k, :], w[:, D * j + BANK * b:D * j + BANK * (b + 1)],
                                              start=a, stop=z)
                i.then_inc(w_used, 1)

            def x_transposes(e):
                pe.wait_ge(gathered, 16 * e + 16)
                for k in range(KC):
                    i = pe.transpose(e_ps(6)[:, P * k:P * (k + 1)], x_tok[:, P * k:P * (k + 1)], ident[:])
                i.then_inc(xt_mm, 1)

            def hid_transposes(e, q):
                pe.wait_ge(hid_ok, 4 * e + q + 1)
                for j in range(2):
                    c = UW * q + P * j
                    i = pe.transpose(quarter(0, q)[:, P * j:P * (j + 1)], hid[:, c:c + P], ident[:])
                i.then_inc(hd_mm, 1)

            def expert_pe(e, last):
                pe.wait_ge(xt_ok, e + 1)
                for u in range(4):
                    e_unit(e, u, xt_hi, xt_lo, e_ps(0))
                for q in range(4):
                    e_unit(e, 4 + q, xt_hi, xt_lo, quarter(2, q))
                    if q:
                        hid_transposes(e, q - 1)
                if not last:
                    x_transposes(e + 1)
                hid_transposes(e, 3)
                pe.wait_ge(y_free, e + 1)
                for u in range(8, EU):
                    pe.wait_ge(hd_ok, 4 * e + u - 8 + 1)
                    e_unit(e, u, hd_hi, hd_lo, e_ps(4))

            pe.wait_ge(rowb_ready, 4)
            pe.wait_ge(route_ready, 1)
            pe.nop().then_inc(w_used, 2)
            x_transposes(0)
            with pe.Fori(0, N_EXP - 1) as e:
                expert_pe(e, False)
            expert_pe(N_EXP - 1, True)


def small_array(a):
    def cols(v):
        return v.reshape(-1, P).T

    c2 = np.stack([a["c"][0], a["c_ctx"]], -1).reshape(KC, P, 2).transpose(1, 0, 2).reshape(P, -1)
    bg = np.zeros((P, 2), np.float32)
    g = a["b_ml_gates"][0].reshape(4, NH)
    for kind in range(2):
        bg[0:NH, kind], bg[32:32 + NH, kind] = g[kind], g[2 + kind]
    w2 = np.zeros((P, 2 * GK_W), np.float32)
    for d in range(2):
        w2[64 + RANK * d:64 + RANK * (d + 1), GK_W * d:GK_W * (d + 1)] = a["w_gla_a2"][0, d]
    parts = {
        "c": c2, "b_ada": cols(a["b_ada"][0]), "g_mix_pre": cols(a["g_mix_pre"][0]),
        "g_mix_post": cols(a["g_mix_post"][0]), "g_ffn_pre": cols(a["g_ffn_pre"][0]),
        "g_ffn_post": cols(a["g_ffn_post"][0]),
        "g_heads": cols(np.concatenate([a["g_ml_norm"][0], a["g_gla_norm"][0]])),
        "conv": a["conv_qk"][0].reshape(3 * 2 * NH, P).T, "b_gates": bg, "b_gla": cols(a["b_gla_a"][0].reshape(-1)),
        "w_gla2": w2,
        "w_router": a["w_router"][0].reshape(KC, P, N_EXP).transpose(1, 0, 2).reshape(P, -1),
    }
    return np.ascontiguousarray(np.concatenate([parts[n] for n in COLS], 1))


def unit_arrays(a):
    w = a["w_in"][0]
    g = np.zeros((D, UW), np.float32)
    for d in range(2):
        for kind in range(2):
            o = OFF_G + NH * (2 * d + kind)
            g[:, P * kind + 32 * d:P * kind + 32 * d + NH] = w[:, o:o + NH]
    g[:, 64:64 + 2 * RANK] = w[:, OFF_A:OFF_A + 2 * RANK]
    starts = [OFF_K, OFF_K + UW, OFF_Q, OFF_Q + UW, OFF_V, OFF_V + UW, OFF_GK, OFF_GQ, OFF_GV, OFF_GV + UW,
              OFF_O, OFF_O + UW, OFF_R, OFF_R + UW]
    units = [g] + [w[:, o:o + UW] for o in starts]
    pack = lambda u: u.reshape(KC, P, UW).transpose(1, 0, 2).reshape(P, KC * UW)
    wo = a["w_out"][0]
    return (np.ascontiguousarray(np.stack([pack(u) for u in units])),
            np.ascontiguousarray(np.stack([pack(wo[:, UW * j:UW * (j + 1)]) for j in range(D // UW)])))


def pos_tables():
    quarter = D // 4
    freq = np.power(np.float32(POS_BASE), -np.arange(quarter, dtype=np.float32) / np.float32(quarter)).astype(np.float32)
    r = np.arange(SEQ // GRID_W, dtype=np.float32)[:, None] * freq
    c = np.arange(GRID_W, dtype=np.float32)[:, None] * freq
    return (np.concatenate([np.sin(r), np.cos(r)], -1).astype(np.float32),
            np.concatenate([np.sin(c), np.cos(c)], -1).astype(np.float32))


def arrays_of(inputs):
    a = {k: np.asarray(v) for k, v in inputs.items()}
    w_in_units, w_out_units = unit_arrays(a)
    pos_row, pos_col = pos_tables()
    return {
        "x": np.ascontiguousarray(a["x"][0]), "ctx": np.ascontiguousarray(a["ctx"][0]),
        "small": small_array(a), "w_ada": np.ascontiguousarray(a["w_ada"][0]),
        "w_in_units": w_in_units, "w_out_units": w_out_units, "pos_row": pos_row, "pos_col": pos_col,
        "w_e_gate": np.ascontiguousarray(a["w_e_gate"][0]), "w_e_up": np.ascontiguousarray(a["w_e_up"][0]),
        "w_e_down": np.ascontiguousarray(a["w_e_down"][0]),
    }


def kernel(**inputs):
    import concourse.bacc as bacc
    from concourse.bass_utils import run_bass_kernel_spmd

    nc = bacc.Bacc("TRN2", target_bir_lowering=False, num_devices=1)
    arrays = arrays_of(inputs)
    I = {n: nc.dram_tensor(n, a.shape, mybir.dt.from_np(a.dtype), kind="ExternalInput").ap() for n, a in arrays.items()}
    out = nc.dram_tensor("out", [SEQ, D], F32, kind="ExternalOutput").ap()
    build(nc, I, out)
    r = run_bass_kernel_spmd(nc, [arrays], core_ids=[0])
    return r.results[0]["out"].reshape(1, SEQ, D)
```

```python
from contextlib import ExitStack

import numpy as np

import concourse.bass as bass
from concourse import mybir

F32 = mybir.dt.float32
F32R = mybir.dt.float32r
U32 = mybir.dt.uint32
ALU = mybir.AluOpType
ACT = mybir.ActivationFunctionType
AX = mybir.AxisListType
ds = bass.ds

P = 128
D = 1024
SEQ = 1024
CTX = 256
ALL = CTX + SEQ
EPS = 1e-6
GRID_W = 64
POS_BASE = 10000.0
ML_W = 512
NH = 4
HD = 128
GK_W = 256
GV_W = 512
RANK = 16
TAU = 16.0
N_EXP = 16
CAP = 2 * SEQ // N_EXP
F = D
KC = D // P
TC = CTX // P
TL = SEQ // P
TA = TC + TL
UW = 256
OFF_Q, OFF_K, OFF_V, OFF_O, OFF_G = 0, 512, 1024, 1536, 2048
OFF_GQ = OFF_G + 4 * NH
OFF_GK = OFF_GQ + GK_W
OFF_GV = OFF_GK + GK_W
OFF_R = OFF_GV + GV_W
OFF_A = OFF_R + GV_W

_cols = {}
_n = 0
for _name, _w in (("c", 2 * KC), ("b_ada", 6 * KC), ("g_mix_pre", KC), ("g_mix_post", KC), ("g_ffn_pre", KC),
                  ("g_ffn_post", KC), ("g_heads", KC), ("conv", 3 * 2 * NH), ("b_gates", 2), ("b_gla", 4),
                  ("w_gla2", 2 * GK_W), ("w_router", KC * N_EXP)):
    _cols[_name] = (_n, _n + _w)
    _n += _w
NSMALL = _n
COLS = dict(_cols)

ADA_FIRST = list(range(8))
ADA_REST = list(range(8, 24))
IN_UNITS = ["G", "k0", "k1", "q0", "q1", "v0", "v1", "gk", "gq", "gv0", "gv1", "o0", "o1", "r0", "r1"]
ADA_BEHIND = {"gq": 2, "gv0": 4, "gv1": 4, "o0": 2, "o1": 2, "r0": 2}
STREAM = [("ada", j) for j in ADA_FIRST]
_rest = list(ADA_REST)
for _u in IN_UNITS:
    STREAM.append(("in", IN_UNITS.index(_u)))
    _k = ADA_BEHIND.get(_u, 0)
    STREAM += [("ada", j) for j in _rest[:_k]]
    _rest = _rest[_k:]
STREAM += [("out", j) for j in range(4)]
assert not _rest
AT = {("in", n): STREAM.index(("in", IN_UNITS.index(n))) for n in IN_UNITS}
AT |= {("ada", j): STREAM.index(("ada", j)) for j in range(24)}
AT |= {("out", j): STREAM.index(("out", j)) for j in range(4)}

PAIRS = {}
for _u, _k in (("v0", 5), ("v1", 5), ("gv0", 5), ("gv1", 5), ("o0", 4), ("o1", 4), ("r0", 4), ("r1", 4),
               ("out0", 4), ("out1", 4), ("out2", 4), ("out3", 4)):
    PAIRS[_u] = (sum(v[1] for v in PAIRS.values()), _k)
TOK_BANKS = 6

BASE = 16512
KB = 1024
AT_SMALL, AT_HT, AT_RING, AT_OUT = BASE, BASE + 13 * KB, BASE + 93 * KB, BASE + 141 * KB

BANK = 512
EV_C0 = 15
ML_T0 = 4
GLA_SCALE = float(GK_W // NH) ** -0.5
LN_HD = 0.5 * float(np.log(HD))

ADA_AHEAD = 2
ACT_SCALED = 4
EU = 12
ROUNDS = CAP // 8
EH = 4


def build(nc, I, out):
    ctx = ExitStack()
    with ctx:
        def at(name, offset, shape, dt=F32):
            return nc.alloc_sbuf_tensor_at(name, shape, dt, offset=offset)

        def sem(name):
            return ctx.enter_context(nc.semaphore(name))

        xn2_dram = nc.dram_tensor("xn2_dram", [SEQ, D], F32).ap()
        acc_dram = nc.dram_tensor("acc_dram", [SEQ, D], F32).ap()

        psum = ctx.enter_context(nc.psum_tensor("psum", [P, 8 * BANK], F32))

        off = [AT_SMALL]

        def small(name, shape, dt=F32):
            t = at(name, off[0], shape, dt)
            off[0] += (int(np.prod(shape[1:])) * 4 + 31) // 32 * 32
            assert off[0] <= AT_HT, off[0] - AT_SMALL
            return t

        sm = small("sm", [P, NSMALL])
        ident = small("ident", [P, P])
        gate_rows = small("gate_rows", [P, ALL])
        mask_add = small("mask_add", [P, 2, P])
        modc = small("modc", [P, 6 * KC, 2])
        amix = small("amix", [P, 2, KC])
        cst = small("cst", [P, 3, TA, 2 * NH])
        ssq = small("ssq", [P, 16])
        rstd = small("rstd", [P, 16])
        decm = small("decm", [P, 2, NH])
        den = small("den", [P, 2, NH])
        gcol = small("gcol", [P, 5, 4, TA])
        hstat = small("hstat", [P, TL * NH])
        mprev = small("mprev", [P, TA])
        sel_s = small("sel_s", [P, 2 * NH])
        one_s = small("one_s", [P, 2])
        zero_r = small("zero_r", [P, P])
        ln_hd = small("ln_hd", [P, 1])

        def col(name):
            a, b = COLS[name]
            return sm[:, a:b]

        h_hi = at("h_hi", AT_HT, [P, KC, ALL], F32R)
        h_lo = at("h_lo", AT_HT + 40 * KB, [P, KC, ALL], F32R)
        raw = [at(f"raw{s}", AT_RING + 8 * KB * s, [P, KC, UW]) for s in range(2)]
        w_hi = [at(f"w_hi{s}", AT_RING + (32 - 16 * s) * KB, [P, KC, UW], F32R) for s in range(2)]
        w_lo = [at(f"w_lo{s}", AT_RING + (40 - 16 * s) * KB, [P, KC, UW], F32R) for s in range(2)]
        xs = at("xs", AT_OUT, [P, TA, D])
        ada_raw = [at(f"ada_raw{n}", AT_HT + 8 * KB * n, [P, KC, UW]) for n in range(8)]
        h32 = at("h32", AT_OUT + 40 * KB, [P, 2, ALL])
        c_st = at("c_st", AT_OUT + 58 * KB, [P, KC, P], F32R)
        c32 = at("c32", AT_OUT + 62 * KB, [P, 2, KC, 2])
        mod_rows = at("mod_rows", AT_OUT + 63 * KB, [P, 2, UW])
        ada_lo = [at(f"ada_lo{n}", AT_HT + 8 * KB * n, [P, KC, UW], F32R) for n in range(8)]
        pos_c = at("pos_c", AT_HT + 64 * KB, [P, D // 2])
        pos_r = at("pos_r", AT_HT + 66 * KB, [P, D // 2])
        grid_sel = at("grid_sel", AT_HT + 68 * KB, [P, TL, 2, GRID_W])
        kT = at("kT", AT_OUT, [P, NH, ALL])
        qT = at("qT", AT_OUT + 20 * KB, [P, NH, SEQ])
        rows32 = at("rows32", AT_OUT + 20 * KB, [P, 2, ALL])
        rows_na = at("rows_na", AT_OUT + 36 * KB, [P, 2, ALL], F32R)
        v_ext = at("v_ext", AT_OUT + 46 * KB, [P, TA, NH, HD + 1])
        row_f = at("row_f", AT_OUT + 46 * KB, [P, ALL])
        row_b = at("row_b", AT_OUT + 51 * KB, [P, ALL])
        row_m = at("row_m", AT_OUT + 56 * KB, [P, ALL])
        row_a = at("row_a", AT_OUT + 61 * KB, [P, ALL])

        def ml(name, n):
            return [at(f"{name}{d}", AT_RING + 2 * KB * (2 * n + d), [P, NH, P]) for d in range(2)]

        ml_w, ml_sw, ml_qs, ml_kh, ml_ks = ml("ml_w", 0), ml("ml_sw", 1), ml("ml_qs", 2), ml("ml_kh", 3), ml("ml_ks", 4)
        ml_c = at("ml_c", AT_RING + 20 * KB, [P, 2, NH, HD + 1])
        h_ml = at("h_ml", AT_RING + 32 * KB, [P, TL, ML_W])
        sel_r = at("sel_r", AT_RING + 28 * KB, [P, 2 * NH, P], F32R)
        h_sq = at("h_sq", AT_OUT + 34 * KB, [P, TL, ML_W])
        y_ml = at("y_ml", AT_OUT, [P, TL, ML_W])
        ht_f = at("ht_f", AT_HT, [P, 2 * KC, ALL])
        gk = at("gk", AT_OUT + 16 * KB, [P, 2, ALL])
        gq = at("gq", AT_OUT + 26 * KB, [P, 2, SEQ])
        gv = at("gv", AT_OUT + 34 * KB, [P, TA, GV_W])
        b_ctx = at("b_ctx", AT_OUT + 54 * KB, [P, 4, CTX])
        l_ctx, l_lat = ht_f[:, KC + 4:2 * KC, CTX + 512:2 * CTX + 512], ht_f[:, 4:KC, CTX:ALL]
        g_s = at("g_s", AT_OUT + 58 * KB, [P, 2, 2, 2 * HD])
        g_ps = at("g_ps", AT_OUT + 62 * KB, [P, 2, 2, 2 * HD])

        def stage(j):
            return ht_f[:, KC + j, CTX + 512:ALL]

        qz = [stage(d).rearrange("p (i h t) -> p i h t", i=2, h=2) for d in range(2)]
        g_a = [stage(2 + d).rearrange("p (h t) -> p h t", h=NH) for d in range(2)]
        kx = [stage(4 + d)[:, 0:2 * P].rearrange("p (i t) -> p i t", i=2) for d in range(2)]
        k_tok = [stage(4 + d)[:, 2 * P:4 * P].rearrange("p (i t) -> p i t", i=2) for d in range(2)]
        e_q = [stage(6 + d)[:, 0:2 * P].rearrange("p (i t) -> p i t", i=2) for d in range(2)]
        e_k = [stage(6 + d)[:, 2 * P:4 * P].rearrange("p (i t) -> p i t", i=2) for d in range(2)]

        def og(t):
            return ht_f[:, KC + t, CTX:CTX + GV_W]

        def gla_bank(d, j, n):
            return psum[:, BANK * (4 * d + j):BANK * (4 * d + j) + n]

        bc_ps = psum[:, 0:2 * BANK].rearrange("p (h q t) -> p h q t", h=NH, q=2)
        st_ps = psum[:, 2 * BANK:3 * BANK].rearrange("p (h t) -> p h t", h=NH)
        kt_ps = psum[:, 3 * BANK:4 * BANK].rearrange("p (h t) -> p h t", h=NH)

        def two_banks(b):
            v = psum[:, b * BANK:(b + 2) * BANK].rearrange("p (b n) -> p b n", b=2)
            return v[:, :, 0:2 * (HD + 1)].rearrange("p b (j e) -> p b j e", j=2)

        kv_ps, num_ps = two_banks(4), two_banks(6)
        modps = psum[:, 7 * BANK:7 * BANK + 12 * KC].rearrange("p (j r) -> p j r", r=2)

        s_small, s_ctx, s_pos = sem("s_small"), sem("s_ctx"), sem("s_pos")
        s_x = [sem(f"s_x{j}") for j in range(4)]
        ada_full = [sem(f"ada_full{n}") for n in range(8)]
        grid_ok, pos_mm, scaled = sem("grid_ok"), sem("pos_mm"), sem("scaled")
        raw_full = [sem("raw_full0"), sem("raw_full1")]
        hi_ready, lo_ready = sem("hi_ready"), sem("lo_ready")
        konst, ones_set = sem("konst"), sem("ones_set")
        dve_seq, act_seq = sem("dve_seq"), sem("act_seq")
        sem_out = sem("sem_out")
        c_silu, c_ready = sem("c_silu"), sem("c_ready")
        ada_rows, ada_evac, ada_cols = sem("ada_rows"), sem("ada_evac"), sem("ada_cols")
        mod1_ready = sem("mod1_ready")
        ssq_done, std_done, xn_ready = sem("ssq_done"), sem("std_done"), sem("xn_ready")
        xt_ready, h32_ready, h_ready, hhi_ready = sem("xt_ready"), sem("h32_ready"), sem("h_ready"), sem("hhi_ready")
        tile_mm, g_free, conv_mid, conv_free, conv_act = (sem("tile_mm"), sem("g_free"), sem("conv_mid"),
                                                          sem("conv_free"), sem("conv_act"))
        tok_mm, tok_act, tok_dve = sem("tok_mm"), sem("tok_act"), sem("tok_dve")
        row_act, row_dve, stat_mm, stat_ready = sem("row_act"), sem("row_dve"), sem("stat_mm"), sem("stat_ready")

        def split_bufs(n):
            if n < 8:
                return (w_hi + w_lo)[n % 4], ada_lo[n]
            return w_hi[n % 2], w_lo[n % 2]

        def wait_used(eng, n):
            kind, j = STREAM[n]
            if kind == "ada" and n < 8:
                eng.wait_ge(ada_rows, n + 1)
            elif n <= AT["in", "q1"]:
                eng.wait_ge(tile_mm, 2 * (n - 8) + 2)
            elif kind == "ada":
                eng.wait_ge(ada_rows, j + 1)
            elif kind == "in" and IN_UNITS[j] in ("gk", "gq"):
                eng.wait_ge(tile_mm, 12 if IN_UNITS[j] == "gk" else 14)
            else:
                name = IN_UNITS[j] if kind == "in" else f"out{j}"
                eng.wait_ge(tok_mm, PAIRS[name][0] + PAIRS[name][1])

        def pair_out(eng, p):
            if p < PAIRS["o0"][0]:
                eng.wait_ge(tok_dve if p % 2 else tok_act, p // 2 + 1 if p % 2 == 0 else (p + 1) // 2)
            elif p < PAIRS["r0"][0]:
                eng.wait_ge(tok_dve, 10 + p - PAIRS["o0"][0] + 1)
            elif p < PAIRS["out0"][0]:
                eng.wait_ge(tok_act, 10 + p - PAIRS["r0"][0] + 1)
            else:
                eng.wait_ge(tok_dve, 18 + p - PAIRS["out0"][0] + 1)

        def tok_ps(p, r):
            return psum[:, BANK * (p % TOK_BANKS) + UW * r:BANK * (p % TOK_BANKS) + UW * (r + 1)]

        def tokv(p, r):
            return tok_ps(p, r).rearrange("p (h n) -> p h n", n=HD)

        ml_zero_d = ada_full[3]
        kst_ready, bc_mm, st_mm, kt_mm = sem("kst_ready"), sem("bc_mm"), sem("st_mm"), sem("kt_mm")
        d_ready, w_ready, sw_ready, bc_read = sem("d_ready"), sem("w_ready"), sem("sw_ready"), sem("bc_read")
        kh_ready, kv_mm, num_mm, c_done = sem("kh_ready"), sem("kv_mm"), sem("num_mm"), sem("c_done")
        h_done, den_seq, ml_zero, ml_norm = sem("h_done"), sem("den_seq"), sem("ml_zero"), sem("ml_norm")

        def at_least(eng, s, v):
            if not isinstance(v, int) or v > 0:
                eng.wait_ge(s, v)

        def scan_steps(eng, front, back):
            def args(t):
                i, d = t // 2, t % 2
                if t < ML_T0:
                    return t, None, d, (i if d == 0 else TC - 1 - i)
                return t, t - ML_T0, d, (i if d == 0 else TC + TA - 1 - i)

            peel, last = ML_T0 + 2, 2 * TA
            front(*args(0))
            for t in range(peel):
                front(*args(t + 1))
                back(*args(t))
            with eng.Fori(TC + 1, TA - 1) as i:
                t = 2 * i
                mirrored = i * -1 + (TC + TA - 1)
                front(t + 1, t + 1 - ML_T0, 1, mirrored)
                back(t, t - ML_T0, 0, i)
                front(t + 2, t + 2 - ML_T0, 0, i + 1)
                back(t + 1, t + 1 - ML_T0, 1, mirrored)
            front(*args(last - 1))
            back(*args(last - 2))
            back(*args(last - 1))

        def scan_stages(eng, first, middle, last):
            def args(t):
                i, d = t // 2, t % 2
                if t < ML_T0:
                    return t, None, d, (i if d == 0 else TC - 1 - i)
                return t, t - ML_T0, d, (i if d == 0 else TC + TA - 1 - i)

            for t in range(ML_T0 + 2):
                first(*args(t))
                if t >= 2:
                    last(*args(t - 2))
                middle(*args(t))
            with eng.Fori(TC + 1, TA) as i:
                mirrored = i * -1 + (TC + TA - 1)
                t = 2 * i
                first(t, t - ML_T0, 0, i)
                last(t - 2, t - 2 - ML_T0, 0, i - 1)
                middle(t, t - ML_T0, 0, i)
                first(t + 1, t + 1 - ML_T0, 1, mirrored)
                last(t - 1, t - 1 - ML_T0, 1, mirrored + 1)
                middle(t + 1, t + 1 - ML_T0, 1, mirrored)
            last(*args(2 * TA - 2))
            last(*args(2 * TA - 1))

        def chunk_cols(c):
            return ds(P * c, P)

        zero_g = sem("zero_g")
        z_abs = ada_full[0]
        z_out, la_tmp, la_seq, b_ready, cols_dve, cols_act = (sem("z_out"), sem("la_tmp"), sem("la_seq"),
                                                              sem("b_ready"), sem("cols_dve"), sem("cols_act"))
        kx_ready = ada_full[1]
        e_ready, gx_ready, gst_mm, gkt_mm = sem("e_ready"), sem("gx_ready"), sem("gst_mm"), sem("gkt_mm")
        gkh_ready, a_ready, gkv_mm, go_mm = sem("gkh_ready"), sem("a_ready"), sem("gkv_mm"), sem("go_mm")
        ps_ready, kvs_ready, s_done, og_done = sem("ps_ready"), sem("kvs_ready"), sem("s_done"), sem("og_done")
        c_again, mask_exp = sem("c_again"), sem("mask_exp")
        sig_done = sem("sig_done")

        y_gla = at("y_gla", AT_OUT + 16 * KB, [P, TL, GV_W])
        yt_hi = at("yt_hi", AT_HT, [P, KC, SEQ], F32R)
        yt_lo = at("yt_lo", AT_HT + 32 * KB, [P, KC, SEQ], F32R)
        rowb = at("rowb", AT_HT + 64 * KB, [P, 3, D])
        diag = at("diag", AT_HT + 76 * KB, [P, KC, P])
        y_out = at("y_out", AT_OUT + 32 * KB, [P, TL, D])
        x_res = at("x_res", AT_OUT, [P, TL, D])
        pos_r2 = at("pos_r2", AT_RING, [P, TL, D // 2])
        pos_c2 = at("pos_c2", AT_OUT + 64 * KB, [P, D // 2])
        h2 = y_out
        h2t = [at(f"h2t{j}", AT_RING + 4 * KB * j, [P, KC, P]) for j in range(2)]
        lg_t = at("lg_t", AT_HT + 76 * KB, [P, SEQ])
        zeros = at("zeros", AT_HT + 64 * KB, [P, D])
        diag2 = at("diag2", AT_HT + 68 * KB, [P, KC, P])
        e_lg = gate_rows[:, 0:P].rearrange("p (t e) -> p t e", t=TL)
        left = [at(f"left{g}", AT_OUT + (32 + 4 * g) * KB, [P, SEQ]) for g in range(ROUNDS // 4)]
        vals = mask_add[:, 0, 0:2 * ROUNDS].rearrange("p (g j) -> p g j", j=8)
        idx_f = mask_add[:, 1, 0:2 * ROUNDS]
        idx_u = at("idx_u", AT_OUT + 66 * KB + 192, [P, ROUNDS // 4, 8], U32)
        e_raw = [at(f"e_raw{u}", (AT_RING if u < 6 else AT_HT + 32 * KB) + 8 * KB * (u % 6), [P, 2 * D]) for u in range(EU)]
        e_lo = [at(f"e_lo{u}", (AT_RING if u < 6 else AT_HT + 32 * KB) + 8 * KB * (u % 6), [P, 2 * D], F32R) for u in range(EU)]
        e_hi = [at(f"e_hi{s}", AT_HT + 8 * KB * s, [P, 2 * D], F32R) for s in range(EH)]
        x_tok = at("x_tok", AT_OUT + 32 * KB, [P, D])
        xt_hi = at("xt_hi", AT_OUT + 36 * KB, [P, KC, CAP], F32R)
        xt_lo = at("xt_lo", AT_OUT + 40 * KB, [P, KC, CAP], F32R)
        hid = at("hid", AT_OUT + 44 * KB, [P, F])
        hd_hi = at("hd_hi", AT_OUT + 48 * KB, [P, F // P, CAP], F32R)
        hd_lo = at("hd_lo", AT_OUT + 52 * KB, [P, F // P, CAP], F32R)
        y_exp = at("y_exp", AT_OUT + 56 * KB, [P, D])
        row_g2 = at("row_g2", AT_OUT + 60 * KB, [P, D])
        gates = at("gates", AT_OUT + 66 * KB, [P, N_EXP])
        tokens = at("tokens", AT_OUT + 66 * KB + 64, [P, N_EXP], U32)
        tok_g = at("tok_g", AT_OUT + 66 * KB + 128, [P, 1], U32)
        tok_s = at("tok_s", AT_OUT + 66 * KB + 160, [P, 1], U32)
        acc = at("acc", AT_HT, [P, TL, D])
        ones_m = zero_r
        vec_c = cst[:, 0, 0:4, :]

        gla_sq, yt_mm, yt_hi_ok, yt_lo_ok = sem("gla_sq"), sem("yt_mm"), sem("yt_hi_ok"), sem("yt_lo_ok")
        diag_ready, row_mm, rowb_ready = sem("diag_ready"), sem("row_mm"), sem("rowb_ready")
        s_xr, s_pr, pos_added = sem("s_xr"), sem("s_pr"), sem("pos_added")
        y_ssq, y_mean, y_std, x1_ready = sem("y_ssq"), sem("y_mean"), sem("y_std"), sem("x1_ready")
        x_ssq, x_mean, x_std, lg_copied, lg_tok = (sem("x_ssq"), sem("x_mean"), sem("x_std"), sem("lg_copied"),
                                                   sem("lg_tok"))
        h2_mid, h2_ready, h2t_mm, h2t_ready, lg_mm = (sem("h2_mid"), sem("h2_ready"), sem("h2t_mm"), sem("h2t_ready"),
                                                      sem("lg_mm"))
        h2_stored, acc_zeroed, zeros_set = sem("h2_stored"), sem("acc_zeroed"), sem("zeros_set")
        soft, aff_mm, topk, sel_mm, route_ready = sem("soft"), sem("aff_mm"), sem("topk"), sem("sel_mm"), sem("route_ready")
        e_full = [sem(f"e_full{u}") for u in range(EU)]
        e_hi_ok, e_lo_ok, w_used = sem("e_hi_ok"), sem("e_lo_ok"), sem("w_used")
        gathered, xt_mm, xt_hi_ok, xt_ok = sem("gathered"), sem("xt_mm"), sem("xt_hi_ok"), sem("xt_ok")
        tok_0_ok, tok_g_ok, tok_s_ok = sem("tok_0_ok"), sem("tok_g_ok"), sem("tok_s_ok")
        sg_ok, hid_ok, hd_mm, hd_hi_ok, hd_ok = sem("sg_ok"), sem("hid_ok"), sem("hd_mm"), sem("hd_hi_ok"), sem("hd_ok")
        y_free, y_taken, scattered = sem("y_free"), sem("y_taken"), sem("scattered")
        h2_ready_2 = ada_full[5]

        def h2_complete(eng, t):
            if t < TL - 2:
                eng.wait_ge(h2_ready, t + 1)
            else:
                eng.wait_ge(h2_ready_2, 16 + t - (TL - 2) + 1)

        o_ready_2 = ada_full[4]
        left_zero = ada_full[2]
        acc_full = e_full[0:4]
        a_ssq, o_mid, o_ready = sem("a_ssq"), sem("o_mid"), sem("o_ready")

        def e_ps(b):
            return psum[:, b * BANK:(b + 2) * BANK]

        def quarter(b, q):
            o = BANK * (b + q % 2) + UW * (q // 2)
            return psum[:, o:o + UW]

        block = ctx.enter_context(nc.Block())

        def t_lat(s):
            return psum[:, 2048 * s:2048 * s + SEQ]

        def t_ctx(s):
            return psum[:, 2048 * s + SEQ:2048 * s + ALL]

        ada_ps = psum[:, 3 * BANK:3 * BANK + UW]

        def unit_src(kind, j):
            if kind == "ada":
                return I["w_ada"].rearrange("(k p) n -> p k n", p=P)[:, :, UW * j:UW * (j + 1)]
            return I["w_in_units" if kind == "in" else "w_out_units"][j].rearrange("p (k n) -> p k n", k=KC)

        @block.sync
        def _(sp):
            sp.dma_start(sm[:], I["small"]).then_inc(s_small, 16)
            sp.dma_start(pos_r[0:SEQ // GRID_W, :], I["pos_row"]).then_inc(s_pos, 16)
            for half in range(2):
                sp.dma_start(pos_c[64 * half:64 * half + 64, :], I["pos_col"]).then_inc(s_pos, 16)

            def load_ada(n):
                sp.dma_start(ada_raw[n][:], unit_src("ada", n)).then_inc(ada_full[n], 16)

            for n in range(ADA_AHEAD):
                load_ada(n)
            sp.dma_start(xs[:, 0:TC, :], I["ctx"].rearrange("(t p) d -> p t d", p=P)).then_inc(s_ctx, 16)
            for j in range(4):
                sp.dma_start(xs[:, TC + 2 * j:TC + 2 * j + 2, :],
                             I["x"][2 * P * j:2 * P * (j + 1), :].rearrange("(t p) d -> p t d", p=P)).then_inc(s_x[j], 16)
            for n in range(ADA_AHEAD, 8):
                load_ada(n)

            def load_unit(n):
                if n >= 10:
                    sp.wait_ge(hi_ready, n - 1)
                    sp.wait_ge(lo_ready, n - 1)
                sp.dma_start(raw[n % 2][:], unit_src(*STREAM[n])).then_inc(raw_full[n % 2], 16)

            for n in range(8, EV_C0):
                load_unit(n)
            sp.wait_ge(h_done, 2 * TL)
            sp.wait_ge(c_done, 2 * TA)
            for n in range(EV_C0, AT["out", 0]):
                load_unit(n)
            for n in range(AT["out", 0], len(STREAM)):
                load_unit(n)
            sp.wait_ge(og_done, 2 * TL)
            for half in range(2):
                sp.dma_start(pos_c2[64 * half:64 * half + 64, :], I["pos_col"]).then_inc(s_pr, 16)
            sp.wait_ge(yt_mm, KC)
            sp.dma_start(x_res[:], I["x"].rearrange("(t p) d -> p t d", p=P)).then_inc(s_xr, 16)
            sp.wait_ge(hi_ready, len(STREAM))
            sp.wait_ge(lo_ready, len(STREAM))
            for half in range(2):
                sp.dma_start(pos_r2[64 * half:64 * half + 64, :, :],
                             I["pos_row"].rearrange("(t h) n -> h t n", h=2)[half].partition_broadcast(64)).then_inc(s_pr, 16)

            def expert_src(e, u):
                if 4 <= u < 8:
                    c = slice(UW * (u - 4), UW * (u - 3))
                    return I["w_e_up"][ds(e, 1), :, c].rearrange("o (k p) n -> p (o k) n", p=P)
                w = I["w_e_gate"] if u < 4 else I["w_e_down"]
                r = 2 * P * (u % 4)
                return w[ds(e, 1), r:r + 2 * P, :].rearrange("o (k p) n -> p (o k) n", p=P)

            def load_expert_unit(e, u):
                dst = e_raw[u][:].rearrange("p (k n) -> p k n", k=KC if 4 <= u < 8 else 2)
                sp.dma_start(dst, expert_src(e, u)).then_inc(e_full[u], 16)

            for t in range(TL):
                h2_complete(sp, t)
                sp.dma_start(xn2_dram[P * t:P * (t + 1), :], h2[:, t, :]).then_inc(h2_stored, 16)
            sp.wait_ge(zeros_set, 1)
            sp.dma_start(acc_dram.rearrange("(t p) d -> p t d", p=P), zeros[:].unsqueeze(1).to_broadcast([P, TL, D])).then_inc(acc_zeroed, 16)
            sp.wait_ge(pos_added, 2)
            sp.wait_ge(tok_mm, 52)
            sp.wait_ge(lg_mm, TL)
            for u in range(10):
                load_expert_unit(0, u)
            sp.wait_ge(acc_zeroed, 16)
            sp.wait_ge(row_mm, 4)
            sp.wait_ge(lg_tok, 1)
            for u in range(10, EU):
                load_expert_unit(0, u)
            with sp.Fori(0, N_EXP - 1) as e:
                for u in range(EU):
                    sp.wait_ge(w_used, EU * e + u + 1 + EH)
                    load_expert_unit(e + 1, u)
            sp.wait_ge(scattered, 16 * N_EXP)
            sp.wait_ge(w_used, EU * N_EXP + EH)
            for j in range(4):
                sp.dma_start(acc[:, 2 * j:2 * j + 2, :],
                             acc_dram[2 * P * j:2 * P * (j + 1), :].rearrange("(t p) d -> p t d", p=P)).then_inc(acc_full[j], 16)
            for t in range(TL):
                if t % 2 == 0:
                    sp.wait_ge(o_ready, t // 2 + 1)
                else:
                    sp.wait_ge(o_ready_2, 16 + t // 2 + 1)
                sp.dma_start(out[P * t:P * (t + 1), :], x_res[:, t, :]).then_inc(sem_out, 16)
            sp.wait_ge(sem_out, 16 * TL)

        @block.gpsimd
        def _(pool):
            pool.memset(ident[:], 0.0).then_inc(konst, 1)
            pool.memset(mask_add[:], 0.0).then_inc(konst, 1)
            pool.memset(sel_s[:], 0.0).then_inc(konst, 1)
            pool.memset(one_s[:], 0.0).then_inc(konst, 1)
            pool.wait_ge(konst, 4)
            pool.affine_select(out=ident[:], in_=ident[:], compare_op=ALU.not_equal, fill=1.0, base=0,
                               pattern=[[-1, P]], channel_multiplier=1).then_inc(konst, 1)
            pool.affine_select(out=mask_add[:, 0, :], in_=mask_add[:, 0, :], compare_op=ALU.is_ge, fill=-1e30,
                               base=0, pattern=[[1, P]], channel_multiplier=-1).then_inc(konst, 1)
            pool.affine_select(out=mask_add[:, 1, :], in_=mask_add[:, 1, :], compare_op=ALU.is_ge, fill=-1e30,
                               base=0, pattern=[[-1, P]], channel_multiplier=1).then_inc(konst, 1)
            for d in range(2):
                v = sel_s[:, NH * d:NH * d + NH]
                pool.affine_select(out=v, in_=v, compare_op=ALU.not_equal, fill=1.0, base=-32 * d,
                                   pattern=[[-1, NH]], channel_multiplier=1).then_inc(konst, 1)
            pool.memset(grid_sel[:], 0.0).then_inc(grid_ok, 1)
            pool.wait_ge(grid_ok, 1)
            v = grid_sel[:].rearrange("p t h w -> p (t h) w")
            pool.affine_select(out=v, in_=v, compare_op=ALU.not_equal, fill=1.0, base=0,
                               pattern=[[-1, 2 * TL], [0, GRID_W]], channel_multiplier=1).then_inc(grid_ok, 1)
            v = one_s[:, :]
            pool.affine_select(out=v, in_=v, compare_op=ALU.not_equal, fill=1.0, base=0,
                               pattern=[[-1, 2]], channel_multiplier=1).then_inc(konst, 1)
            pool.wait_ge(konst, 10)
            pool.affine_select(out=v, in_=v, compare_op=ALU.not_equal, fill=1.0, base=-2,
                               pattern=[[-1, 2]], channel_multiplier=1).then_inc(konst, 1)

            pool.wait_ge(stat_ready, 1)
            pool.wait_ge(tok_mm, 10)
            pool.wait_ge(konst, 11)
            pool.memset(sel_r[:].bitcast(F32), 0.0).then_inc(ml_zero, 1)
            for half in range(2):
                pool.wait_ge(ml_zero, 1 + 2 * half)
                for d in range(2):
                    v = sel_r[:, NH * d:NH * d + NH, :]
                    pool.affine_select(out=v, in_=v, compare_op=ALU.not_equal, fill=1.0, base=-32 * d - 64 * half,
                                       pattern=[[-1, NH], [0, P]], channel_multiplier=1).then_inc(ml_zero, 1)
            pool.wait_ge(conv_act, 8)

            def stage_k(t, l, d, c):
                at_least(pool, kt_mm, t - 1)
                pool.tensor_copy(ml_ks[d][:], kT[:, :, chunk_cols(c)]).then_inc(kst_ready, 1)

            scan_steps(pool, stage_k, lambda t, l, d, c: None)
            pool.wait_ge(z_out, 4)
            pool.memset(g_s[:], 0.0)
            pool.memset(ht_f[:, KC:2 * KC, CTX:CTX + GV_W], 0.0)
            pool.memset(ht_f[:, KC:KC + 2, CTX + 512:ALL], 0.0).then_inc(zero_g, 1)
            pool.wait_ge(s_xr, 16)
            pool.wait_ge(s_pr, 64)
            pool.tensor_tensor(x_res[:, :, D // 2:D], x_res[:, :, D // 2:D],
                               pos_c2[:].unsqueeze(1).to_broadcast([P, TL, D // 2]), ALU.add).then_inc(pos_added, 1)
            pool.tensor_tensor(x_res[:, :, 0:D // 2], x_res[:, :, 0:D // 2], pos_r2[:], ALU.add).then_inc(pos_added, 1)
            for t in range(TL - 2):
                pool.wait_ge(h2_mid, t + 1)
                pool.wait_ge(rowb_ready, 3)
                pool.tensor_tensor(h2[:, t, :], h2[:, t, :], rowb[:, 2, :], ALU.add).then_inc(h2_ready, 1)
            pool.memset(zeros[:], 0.0).then_inc(zeros_set, 1)
            pool.wait_ge(h2_stored, 16 * TL)
            pool.wait_ge(h2t_mm, TL)
            for tile in left[:-1]:
                pool.memset(tile[:], 0.0)
            pool.memset(left[-1][:], 0.0).then_inc(left_zero, 1)
            def gather(e, copied, n):
                pool.tensor_copy(tok_g[:], tokens[:, ds(e, 1)]).then_inc(copied, 1)
                pool.wait_ge(h2_stored, 16 * TL)
                pool.wait_ge(copied, n)
                pool.indirect_dma_start(x_tok[:], None, xn2_dram, bass.IndirectOffsetOnAxis(ap=tok_g[:, 0:1], axis=0)).then_inc(gathered, 16)

            def scatter(e):
                pool.wait_ge(y_free, e + 2)
                pool.tensor_copy(tok_s[:], tokens[:, ds(e, 1)]).then_inc(tok_s_ok, 1)
                pool.wait_ge(acc_zeroed, 16)
                pool.wait_ge(tok_s_ok, e + 1)
                pool.indirect_dma_start(acc_dram, bass.IndirectOffsetOnAxis(ap=tok_s[:, 0:1], axis=0), y_exp[:], None,
                                        compute_op=ALU.add).then_inc(scattered, 16)
                pool.wait_ge(scattered, 16 * e + 16)
                pool.nop().then_inc(y_taken, 1)

            pool.wait_ge(route_ready, 1)
            gather(0, tok_0_ok, 1)
            pool.nop().then_inc(y_taken, 1)
            with pool.Fori(1, N_EXP) as e:
                pool.wait_ge(xt_mm, e)
                gather(e, tok_g_ok, e)
                scatter(e - 1)
            scatter(N_EXP - 1)
            for t in range(1, TL, 2):
                pool.wait_ge(o_mid, t + 1)
                pool.tensor_tensor(x_res[:, t, :], x_res[:, t, :], acc[:, t, :], ALU.add).then_inc(o_ready_2, 1)

        @block.scalar
        def _(act):
            n_act = [0]

            def act_link(ins):
                n_act[0] += 1
                ins.then_inc(act_seq, 1)
                act.wait_ge(act_seq, n_act[0])

            def split_hi(n):
                if n < 8:
                    act.wait_ge(ada_full[n], 16)
                    src = ada_raw[n]
                else:
                    act.wait_ge(raw_full[n % 2], 16 * (n // 2 - 3))
                    src = raw[n % 2]
                if n >= (2 if n >= 8 else 4):
                    wait_used(act, n - (2 if n >= 8 else 4))
                act.activation(split_bufs(n)[0][:], src[:], ACT.Copy).then_inc(hi_ready, 1)

            act.wait_ge(s_small, 16)
            cc = col("c").rearrange("p (k r) -> p k r", k=KC)
            act.activation(c32[:, 0, :, :], cc, ACT.Silu).then_inc(c_silu, 1)
            for n in range(ADA_AHEAD):
                split_hi(n)
            for t in range(TA):
                if t < TC:
                    act.wait_ge(s_ctx, 16)
                else:
                    act.wait_ge(xn_ready, t - TC + 1)
                if t >= 2:
                    act.wait_ge(ssq_done, t - 1)
                act.activation(h32[:, t % 2, 0:D], xs[:, t, :], ACT.Square, accum_out=ssq[:, t:t + 1]).then_inc(ssq_done, 1)
            act.wait_ge(ssq_done, TA + 1)
            act.activation(rstd[:, 0:TA], ssq[:, 0:TA], ACT.Sqrt).then_inc(std_done, 1)

            def ada_evac_rows(n):
                act.wait_ge(ada_rows, n + 1)
                if n >= 2:
                    act.wait_ge(ada_cols, n - 1)
                act.activation(mod_rows[:, n % 2, :], ada_ps, ACT.Copy).then_inc(ada_evac, 1)

            for n in range(ADA_AHEAD, 3):
                split_hi(n)
            for n in range(3, 8):
                split_hi(n)
                ada_evac_rows(n - 3)
                if n == 3:
                    act.wait_ge(scaled, 1)
                    for t in range(TA - ACT_SCALED, TA):
                        act.activation(xs[:, t, :], xs[:, t, :], ACT.Copy, scale=rstd[:, t:t + 1]).then_inc(scaled, 1)
            for n in range(5, 8):
                ada_evac_rows(n)
            act.wait_ge(mod1_ready, 1)
            for k in range(KC):
                act.wait_ge(xt_ready, k + 1)
                s = k % 2
                if k >= 2:
                    act.wait_ge(h_ready, k - 1)
                act.activation(h32[:, s, 0:CTX], t_ctx(s), ACT.Identity, bias=modc[:, k, 1:2],
                               scale=amix[:, 1, k:k + 1])
                act.activation(h32[:, s, CTX:ALL], t_lat(s), ACT.Identity, bias=modc[:, k, 0:1],
                               scale=amix[:, 0, k:k + 1]).then_inc(h32_ready, 1)
                if k == 2:
                    split_hi(8)

            def conv_first(i, part, h, has_ctx):
                dst, j = (kT, NH + h) if part else (qT, h)
                act.wait_ge(tile_mm, i + 1)
                w = col("conv")[:, 2 * NH + j:2 * NH + j + 1]
                s = i % 2
                if part:
                    act.activation(dst[:, h, 0:CTX], t_ctx(s), ACT.Copy, scale=w)
                    act.activation(dst[:, h, CTX:ALL], t_lat(s), ACT.Copy, scale=w).then_inc(conv_mid, 1)
                else:
                    act.activation(dst[:, h, :], t_lat(s), ACT.Copy, scale=w).then_inc(conv_mid, 1)

            def conv_silu(i, part, h):
                act.wait_ge(conv_free, i - 1)
                v = (kT if part else qT)[:, h, :]
                act.activation(v, v, ACT.Silu).then_inc(conv_act, 1)

            split_hi(9)
            for t in range(2):
                act.wait_ge(tile_mm, t + 1)
                dst = gate_rows if t == 0 else row_f
                act.activation(dst[:, 0:CTX], t_ctx(t), ACT.Identity, bias=col("b_gates")[:, t:t + 1])
                act.activation(dst[:, CTX:ALL], t_lat(t), ACT.Identity, bias=col("b_gates")[:, t:t + 1]).then_inc(g_free, 1)
            split_hi(10)
            act.wait_ge(g_free, 2)
            act_link(act.activation(row_a[:], row_f[:], ACT.Abs))
            act_link(act.activation(row_a[:], row_a[:], ACT.Exp, scale=-1.0))
            act.activation(row_a[:], row_a[:], ACT.Ln, bias=1.0).then_inc(row_act, 1)
            conv_first(2, 1, 0, True)
            conv_first(3, 1, 1, True)
            act.wait_ge(row_dve, 1)
            act.activation(rows32[:, 1, :], rows32[:, 1, :], ACT.Exp).then_inc(row_act, 1)
            act.activation(row_f[:], row_f[:], ACT.Exp).then_inc(row_act, 1)
            act.activation(row_m[:], row_m[:], ACT.Exp, scale=-1.0, bias=ln_hd[:, 0:1]).then_inc(row_act, 1)
            split_hi(11)
            conv_silu(2, 1, 0)
            conv_silu(3, 1, 1)
            conv_first(4, 1, 2, True)
            conv_first(5, 1, 3, True)
            split_hi(12)
            conv_silu(4, 1, 2)
            conv_silu(5, 1, 3)
            act.wait_ge(row_dve, 2)
            conv_first(6, 0, 0, False)
            conv_first(7, 0, 1, False)
            split_hi(13)
            conv_silu(6, 0, 0)
            conv_silu(7, 0, 1)
            conv_first(8, 0, 2, False)
            conv_first(9, 0, 3, False)
            split_hi(14)
            conv_silu(8, 0, 2)
            conv_silu(9, 0, 3)
            act.wait_ge(stat_ready, 1)
            for u in range(2):
                for j in range(5):
                    p = 5 * u + j
                    if p % 2 == 0:
                        act.wait_ge(tok_mm, p + 1)
                        for r in range(2):
                            i = act.activation(v_ext[:, 2 * j + r, 2 * u:2 * u + 2, 0:HD], tokv(p, r), ACT.Copy)
                        i.then_inc(tok_act, 1)
            def ml_front(t, l, d, c):
                act.wait_ge(kt_mm, t + 1)
                at_least(act, kv_mm, t - 1)
                for h in range(NH):
                    i = act.activation(ml_kh[d][:, h, :], kt_ps[:, h, :], ACT.Copy,
                                       scale=cst[:, 1, ds(c, 1), NH * d + h])
                i.then_inc(kh_ready, 1)
                if l is not None:
                    act.wait_ge(d_ready, l + 1)
                    act.activation(ml_w[d][:], ml_w[d][:], ACT.Exp).then_inc(w_ready, 1)

            scan_steps(act, ml_front, lambda t, l, d, c: None)
            act.wait_ge(h_done, 2 * TL)
            act.activation(h_sq[:], h_ml[:], ACT.Square).then_inc(ml_norm, 1)
            act.wait_ge(c_done, 2 * TA)
            split_hi(15)
            act.wait_ge(ml_norm, 2)
            act.activation(hstat[:], hstat[:], ACT.Sqrt).then_inc(ml_norm, 1)
            act.wait_ge(num_mm, 2 * TL)
            act.activation(c32[:, 0, :, :], cc, ACT.Silu).then_inc(c_again, 1)

            def small_ada(n):
                kind, j = STREAM[n]
                if kind == "ada":
                    act.wait_ge(ada_rows, j + 1)
                    act.wait_ge(ada_cols, j - 1)
                    act.activation(mod_rows[:, j % 2, :], psum[:, 6 * BANK:6 * BANK + UW], ACT.Copy).then_inc(ada_evac, 1)

            act.wait_ge(ml_norm, 4)
            split_hi(16)
            for i in range(10, 14):
                act.wait_ge(tile_mm, i + 1)
                if i < 12:
                    act.activation(gk[:, i - 10, 0:CTX], t_ctx(i % 2), ACT.Copy)
                    act.activation(gk[:, i - 10, CTX:ALL], t_lat(i % 2), ACT.Copy).then_inc(g_free, 1)
                else:
                    act.activation(gq[:, i - 12, :], t_lat(i % 2), ACT.Copy, scale=GLA_SCALE).then_inc(g_free, 1)
                if i == 11:
                    split_hi(17)
            for n in range(17, AT["out", 0]):
                if n + 1 < AT["out", 0]:
                    split_hi(n + 1)
                kind, j = STREAM[n]
                if kind == "ada":
                    small_ada(n)
                    continue
                name = IN_UNITS[j]
                p0, pairs = PAIRS[name]
                u = int(name[-1])
                for q in range(pairs):
                    p = p0 + q
                    if name[:2] == "gv" and p % 2:
                        continue
                    act.wait_ge(tok_mm, p + 1)
                    src = psum[:, BANK * (p % TOK_BANKS):BANK * (p % TOK_BANKS + 1)].rearrange("p (r n) -> p r n", r=2)
                    if name[:2] == "gv":
                        act.activation(gv[:, 2 * q:2 * q + 2, UW * u:UW * (u + 1)], src, ACT.Copy).then_inc(tok_act, 1)
                    elif name[0] == "o":
                        act.activation(src, src, ACT.Sigmoid).then_inc(sig_done, 1)
                    else:
                        act.activation(ht_f[:, KC * u + 2 * q:KC * u + 2 * q + 2, 0:UW], src, ACT.Silu).then_inc(tok_act, 1)
            for i in range(4):
                act.wait_ge(tile_mm, 15 + i)
                act.activation(l_ctx[:, i, :], t_ctx(i % 2), ACT.Abs, bias=col("b_gla")[:, i:i + 1])
                act.activation(l_lat[:, i, :], t_lat(i % 2), ACT.Abs, bias=col("b_gla")[:, i:i + 1]).then_inc(z_abs, 1)
            act.wait_ge(z_abs, 16 + 4)
            act.activation(l_ctx, l_ctx, ACT.Exp, scale=-1.0)
            act.activation(l_lat, l_lat, ACT.Exp, scale=-1.0).then_inc(la_seq, 1)
            act.wait_ge(la_seq, 1)
            act.activation(l_ctx, l_ctx, ACT.Ln, bias=1.0)
            for i in range(4):
                act.activation(l_lat[:, i, :], l_lat[:, i, :], ACT.Ln, bias=1.0).then_inc(la_tmp, 1)
            act.activation(mask_add[:], mask_add[:], ACT.Exp).then_inc(mask_exp, 1)
            act.wait_ge(cols_dve, 1)
            act.activation(gcol[:, 2:5, :, :], gcol[:, 2:5, :, :], ACT.Exp, scale=1.0 / TAU).then_inc(cols_act, 1)
            act.wait_ge(cols_act, 1)
            act.wait_ge(zero_g, 1)

            def b_of(dp, l, c):
                return b_ctx[:, dp, chunk_cols(c)] if l is None else ht_f[:, dp, chunk_cols(c)]

            def gla_front(t, l, d, c):
                act.wait_ge(kx_ready, 16 + t - 1)
                if l is not None:
                    at_least(act, gx_ready, l - 1)
                for i in range(2):
                    dp = 2 * d + i
                    x = act.activation(e_k[d][:, i, :], b_of(dp, l, c), ACT.Exp, scale=-1.0 / TAU, bias=gcol[:, 1, dp, ds(c, 1)])
                    if l is not None:
                        x = act.activation(e_q[d][:, i, :], b_of(dp, l, c), ACT.Exp, scale=1.0 / TAU, bias=gcol[:, 0, dp, ds(c, 1)])
                x.then_inc(e_ready, 1)

            def gla_middle(t, l, d, c):
                if l is not None:
                    at_least(act, s_done, t - 1)
                    at_least(act, go_mm, l - 1)
                    for i in range(2):
                        x = act.activation(g_ps[:, d, i, :], g_s[:, d, i, :], ACT.Copy, scale=gcol[:, 2, 2 * d + i, ds(c, 1)])
                    x.then_inc(ps_ready, 1)
                act.wait_ge(gkt_mm, t + 1)
                at_least(act, gkv_mm, t - 1)
                act.activation(k_tok[d], gla_bank(d, 1, 2 * P).rearrange("p (i t) -> p i t", i=2), ACT.Copy).then_inc(gkh_ready, 1)

            def gla_back(t, l, d, c):
                act.wait_ge(gkv_mm, t + 1)
                for i in range(2):
                    v = gla_bank(d, 2, 4 * HD)[:, 2 * HD * i:2 * HD * (i + 1)]
                    x = act.activation(v, v, ACT.Copy, scale=gcol[:, 4, 2 * d + i, ds(c, 1)])
                x.then_inc(kvs_ready, 1)

            scan_stages(act, gla_front, gla_middle, gla_back)
            act.wait_ge(og_done, 2 * TL)
            act.wait_ge(s_done, 2 * TA)
            for half in range(2):
                t4 = slice(4 * half, 4 * half + 4)
                act.activation(y_gla[:, t4, :], ht_f[:, KC:2 * KC, CTX:CTX + GV_W][:, t4, :], ACT.Square).then_inc(gla_sq, 1)
            split_hi(AT["out", 0])
            act.wait_ge(gla_sq, 3)
            act.activation(hstat[:], hstat[:], ACT.Sqrt).then_inc(gla_sq, 1)
            split_hi(AT["out", 1])
            act.wait_ge(gla_sq, 4 + NH)
            for k in range(KC):
                act.wait_ge(yt_mm, k + 1)
                act.activation(yt_hi[:, k, :], t_lat(k % 2), ACT.Copy, scale=col("g_heads")[:, k:k + 1]).then_inc(yt_hi_ok, 1)

            def y_squares(q):
                p = PAIRS["out0"][0] + q
                act.wait_ge(tok_mm, p + 1)
                for j in range(2):
                    n, t = 2 * q + j, 2 * (q % 4) + j
                    at_least(act, y_ssq, n - 3)
                    act.activation(gate_rows[:, UW * (n % 4):UW * (n % 4 + 1)], tok_ps(p, j), ACT.Square,
                                   accum_out=hstat[:, 4 * t + q // 4:4 * t + q // 4 + 1]).then_inc(y_ssq, 1)

            def y_root(j):
                act.wait_ge(y_mean, j + 1)
                act.activation(rstd[:, 2 * j:2 * j + 2], ssq[:, 2 * j:2 * j + 2], ACT.Sqrt).then_inc(y_std, 1)

            def x_squares(j):
                for t in (2 * j, 2 * j + 1):
                    act.wait_ge(x1_ready, t + 1)
                    act.activation(y_out[:, t, :], x_res[:, t, :], ACT.Square,
                                   accum_out=ssq[:, TL + t:TL + t + 1]).then_inc(x_ssq, 1)

            def x_root(j):
                act.wait_ge(x_mean, j + 1)
                a = TL + 2 * j
                act.activation(rstd[:, a:a + 2], ssq[:, a:a + 2], ACT.Sqrt).then_inc(x_std, 1)

            def h2t_part(t):
                act.wait_ge(h2t_mm, t + 1)
                at_least(act, lg_mm, t - 1)
                act.activation(h2t[t % 2][:], e_ps(6).rearrange("p (k n) -> p k n", k=KC), ACT.Copy).then_inc(h2t_ready, 1)

            for u in range(3):
                if u == 0:
                    act.wait_ge(row_mm, 1)
                    act.activation(rowb[:, 0, :], e_ps(6), ACT.Copy).then_inc(rowb_ready, 1)
                for q in range(4):
                    y_squares(4 * u + q)
                if u < 2:
                    split_hi(AT["out", u + 2])
                    act.wait_ge(row_mm, u + 2)
                    act.activation(rowb[:, u + 1, :], e_ps(6), ACT.Copy).then_inc(rowb_ready, 1)
            act.wait_ge(pos_added, 2)
            y_squares(12)
            y_root(0)
            for j in range(4):
                if j < 3:
                    y_squares(13 + j)
                if j >= 2:
                    h2t_part(2 * j - 4)
                x_squares(j)
                if j < 3:
                    y_root(j + 1)
                if j >= 2:
                    h2t_part(2 * j - 3)
                x_root(j)
            for t in range(4, TL):
                h2t_part(t)
            act.wait_ge(soft, 1)
            act.activation(e_lg, e_lg, ACT.Exp).then_inc(soft, 1)

            def e_split_hi(e, u):
                act.wait_ge(e_full[u], 16 * e + 16)
                act.wait_ge(w_used, EU * e + u + 1)
                act.activation(e_hi[u % EH][:], e_raw[u][:], ACT.Copy).then_inc(e_hi_ok, 1)

            def xt_hi_part(e):
                act.wait_ge(xt_mm, e + 1)
                act.activation(xt_hi[:].rearrange("p k n -> p (k n)"), e_ps(6), ACT.Copy).then_inc(xt_hi_ok, 1)

            def hd_hi_part(e, q):
                act.wait_ge(hd_mm, 4 * e + q + 1)
                act.activation(hd_hi[:, 2 * q:2 * q + 2, :], quarter(0, q).rearrange("p (k n) -> p k n", k=2), ACT.Copy).then_inc(hd_hi_ok, 1)

            def e_split_his(e, units):
                for u in units:
                    e_split_hi(e, u)

            def expert_act(e, last):
                act.wait_ge(w_used, EU * e + 4 + EH)
                act.activation(hid[:], e_ps(0), ACT.Silu).then_inc(sg_ok, 1)
                e_split_his(e, (7, 8))
                hd_hi_part(e, 0)
                e_split_hi(e, 9)
                hd_hi_part(e, 1)
                e_split_hi(e, 10)
                hd_hi_part(e, 2)
                if not last:
                    xt_hi_part(e + 1)
                hd_hi_part(e, 3)
                e_split_hi(e, 11)
                if not last:
                    e_split_his(e + 1, range(3))
                act.wait_ge(w_used, EU * e + EU + EH)
                act.wait_ge(y_taken, e + 1)
                act.activation(y_exp[:], e_ps(4), ACT.Copy, scale=gates[:, ds(e, 1)]).then_inc(y_free, 1)
                if not last:
                    e_split_his(e + 1, range(3, 7))

            act.wait_ge(h2_stored, 16 * TL)
            act.wait_ge(row_mm, 4)
            act.activation(row_g2[:], e_ps(6), ACT.Copy).then_inc(rowb_ready, 1)
            act.nop().then_inc(y_free, 1)
            e_split_his(0, range(EH))
            act.wait_ge(route_ready, 1)
            xt_hi_part(0)
            e_split_his(0, range(EH, 7))
            with act.Fori(0, N_EXP - 1) as e:
                expert_act(e, False)
            expert_act(N_EXP - 1, True)
            for j in range(4):
                act.wait_ge(acc_full[j], 16 * N_EXP + 16)
                for t in (2 * j, 2 * j + 1):
                    at_least(act, a_ssq, 4 * (j - 1) + 4)
                    act.activation(e_ps(4 + 2 * (t % 2)), acc[:, t, :], ACT.Square, accum_out=ssq[:, t:t + 1]).then_inc(a_ssq, 1)
                act.wait_ge(a_ssq, 4 * j + 3)
                act.activation(rstd[:, 2 * j:2 * j + 2], ssq[:, 2 * j:2 * j + 2], ACT.Sqrt).then_inc(a_ssq, 1)

        @block.vector
        def _(dve):
            n_dve = [0]

            def link(ins):
                n_dve[0] += 1
                ins.then_inc(dve_seq, 1)
                dve.wait_ge(dve_seq, n_dve[0])

            def split_lo(n):
                dve.wait_ge(hi_ready, n + 1)
                hi, lo = split_bufs(n)
                dve.tensor_tensor(lo[:], (ada_raw[n] if n < 8 else raw[n % 2])[:], hi[:],
                                  ALU.subtract).then_inc(lo_ready, 1)

            link(dve.memset(c_st[:].bitcast(F32), 0.0))
            link(dve.memset(zero_r[:], 0.0))
            dve.wait_ge(c_silu, 1)
            link(dve.tensor_copy(c_st[:, :, 0:2], c32[:, 0, :, :]))
            dve.tensor_tensor(c_st[:, :, 2:4], c32[:, 0, :, :], c_st[:, :, 0:2], ALU.subtract).then_inc(c_ready, 1)
            for n in range(ADA_AHEAD):
                split_lo(n)
            for t in range(TL):
                dve.wait_ge(s_x[t // 2], 16)
                dve.wait_ge(s_pos, 48)
                dve.wait_ge(pos_mm, t + 1)
                v = xs[:, TC + t, :]
                dve.tensor_tensor(v[:, 0:D // 2], v[:, 0:D // 2], psum[:, BANK * (t % 2):BANK * (t % 2 + 1)], ALU.add)
                dve.tensor_tensor(v[:, D // 2:D], v[:, D // 2:D], pos_c[:], ALU.add).then_inc(xn_ready, 1)
            dve.memset(ln_hd[:], LN_HD).then_inc(ones_set, 1)
            dve.wait_ge(ssq_done, TA)
            dve.tensor_scalar(ssq[:, 0:TA], ssq[:, 0:TA], 1.0 / D, EPS, ALU.mult, ALU.add).then_inc(ssq_done, 1)
            dve.wait_ge(std_done, 1)
            dve.reciprocal(rstd[:, 0:TA], rstd[:, 0:TA]).then_inc(scaled, 1)
            dve.wait_ge(scaled, 1)
            for t in range(TA - ACT_SCALED):
                dve.tensor_scalar(xs[:, t, :], xs[:, t, :], rstd[:, t:t + 1], None, ALU.mult).then_inc(scaled, 1)
            for n in range(ADA_AHEAD, 8):
                split_lo(n)
            dve.wait_ge(ada_cols, 8)
            b = col("b_ada")[:, 0:2 * KC].unsqueeze(2).to_broadcast([P, 2 * KC, 2])
            link(dve.tensor_tensor(modc[:, 0:2 * KC, :], modps[:, 0:2 * KC, :], b, ALU.add))
            for r in range(2):
                i = dve.scalar_tensor_tensor(amix[:, r, :], modc[:, KC:2 * KC, r], 1.0, col("g_mix_pre"), ALU.add, ALU.mult)
            i.then_inc(mod1_ready, 1)
            for k in range(KC):
                dve.wait_ge(h32_ready, k + 1)
                dve.tensor_copy(h_hi[:, k, :], h32[:, k % 2, :]).then_inc(hhi_ready, 1)
                dve.wait_ge(hhi_ready, k + 1)
                dve.tensor_tensor(h_lo[:, k, :], h32[:, k % 2, :], h_hi[:, k, :], ALU.subtract).then_inc(h_ready, 1)
                if k == 3:
                    split_lo(8)
            split_lo(9)
            link(dve.memset(row_b[:], 0.0))
            link(dve.memset(row_m[:], 0.0))
            split_lo(10)

            dve.wait_ge(row_act, 1)
            link(dve.scalar_tensor_tensor(row_f[:], row_f[:], 0.0, row_a[:], ALU.min, ALU.subtract))
            for c in range(TA):
                a, z = P * c, P * (c + 1)
                dve.tensor_tensor_scan(row_b[0:NH, a:z], row_f[0:NH, a:z], zero_r[0:NH, :], 0.0, ALU.add, ALU.add)
                rb = row_b[32:32 + NH, a:z][:, ::-1]
                dve.tensor_tensor_scan(rb, row_f[32:32 + NH, a:z][:, ::-1], zero_r[32:32 + NH, :], 0.0, ALU.add, ALU.add)
            dve.tensor_tensor_scan(row_m[0:NH, :], row_f[0:NH, :], gate_rows[0:NH, :], 0.0, ALU.add, ALU.max)
            link(dve.tensor_tensor_scan(row_m[32:32 + NH, 0:CTX][:, ::-1], row_f[32:32 + NH, 0:CTX][:, ::-1],
                                        gate_rows[32:32 + NH, 0:CTX][:, ::-1], 0.0, ALU.add, ALU.max))
            link(dve.tensor_tensor_scan(row_m[32:32 + NH, CTX:ALL][:, ::-1], row_f[32:32 + NH, CTX:ALL][:, ::-1],
                                        gate_rows[32:32 + NH, CTX:ALL][:, ::-1], row_m[32:32 + NH, 0:1], ALU.add, ALU.max))
            link(dve.tensor_tensor(rows32[:, 0, :], row_b[:], row_m[:], ALU.subtract))
            link(dve.memset(mprev[:], 0.0))
            dve.tensor_copy(mprev[0:NH, 1:TA], row_m[0:NH, P - 1:ALL - 1:P])
            dve.tensor_copy(mprev[32:32 + NH, TC:TA - 1], row_m[32:32 + NH, CTX + P:ALL:P])
            dve.tensor_copy(mprev[32:32 + NH, TA - 1:TA], row_m[32:32 + NH, 0:1])
            link(dve.tensor_copy(mprev[32:32 + NH, 0:1], row_m[32:32 + NH, P:P + 1]))
            r3 = lambda v: v.rearrange("p (c t) -> p c t", t=P)
            dve.tensor_tensor(r3(rows32[:, 1, :]), r3(rows32[:, 0, :]), mprev[:].unsqueeze(2).to_broadcast([P, TA, P]), ALU.add)
            link(dve.tensor_tensor(row_a[:], gate_rows[:], row_b[:], ALU.subtract))
            link(dve.memset(row_f[:], 0.0))
            for d in range(2):
                q = slice(32 * d, 32 * d + NH)
                end = r3(rows32[q, 0, :])[:, :, (P - 1) * (1 - d):(P - 1) * (1 - d) + 1]
                i = dve.tensor_tensor(r3(row_f[q, :]), r3(row_a[q, :]), end.to_broadcast([NH, TA, P]), ALU.add)
            i.then_inc(row_dve, 1)

            def conv_taps(i, part, h):
                dst, j = (kT, NH + h) if part else (qT, h)
                wts = [col("conv")[:, 2 * NH * t + j:2 * NH * t + j + 1] for t in (0, 2)]
                dve.wait_ge(conv_mid, i - 1)
                s = i % 2
                segs = [(t_lat(s), dst[:, h, CTX:ALL] if part else dst[:, h, :], SEQ)]
                if part:
                    segs.append((t_ctx(s), dst[:, h, 0:CTX], CTX))
                for src, o, n in segs:
                    last = dve.scalar_tensor_tensor(o[:, 1:n], src[:, 0:n - 1], wts[0], o[:, 1:n], ALU.mult, ALU.add)
                link(last)
                for src, o, n in segs:
                    last = dve.scalar_tensor_tensor(o[:, 0:n - 1], src[:, 1:n], wts[1], o[:, 0:n - 1], ALU.mult, ALU.add)
                last.then_inc(conv_free, 1)

            conv_taps(2, 1, 0)
            conv_taps(3, 1, 1)
            dve.wait_ge(row_act, 2)
            link(dve.tensor_copy(rows_na[0:64, :, :], rows32[0:64, :, :]))
            dve.tensor_tensor(rows_na[64:P, :, :], rows32[0:64, :, :], rows_na[0:64, :, :], ALU.subtract).then_inc(row_dve, 1)
            split_lo(11)
            conv_taps(4, 1, 2)
            conv_taps(5, 1, 3)
            split_lo(12)
            conv_taps(6, 0, 0)
            conv_taps(7, 0, 1)
            split_lo(13)
            conv_taps(8, 0, 2)
            conv_taps(9, 0, 3)
            dve.wait_ge(stat_mm, 1)
            dve.tensor_copy(cst[:].rearrange("p q c s -> p (q c s)"), psum[:, 7 * BANK:7 * BANK + 3 * TA * 2 * NH]).then_inc(stat_ready, 1)
            split_lo(14)
            dve.memset(v_ext[:, :, :, HD:HD + 1], 1.0).then_inc(ones_set, 1)
            for u in range(2):
                for j in range(5):
                    p = 5 * u + j
                    if p % 2 == 1:
                        dve.wait_ge(tok_mm, p + 1)
                        for r in range(2):
                            i = dve.tensor_copy(v_ext[:, 2 * j + r, 2 * u:2 * u + 2, 0:HD], tokv(p, r))
                        i.then_inc(tok_dve, 1)
            dve.wait_ge(tok_mm, 10)
            dve.memset(ml_c[:], 0.0).then_inc(ml_zero_d, 1)
            dve.memset(h_ml[:], 0.0).then_inc(ml_zero_d, 1)
            dve.wait_ge(ml_zero_d, 16 + 2)

            def ml_front(t, l, d, c):
                dve.wait_ge(bc_mm, t + 1)
                at_least(dve, c_done, t - 1)
                if l is None:
                    dve.tensor_copy(decm[:, d, :], bc_ps[:, :, 1, (P - 1) * (1 - d)]).then_inc(bc_read, 1)
                    return
                dve.tensor_copy(decm[:, d, :], bc_ps[:, :, 1, (P - 1) * (1 - d)])
                at_least(dve, sw_ready, l - 1)
                for h in range(NH):
                    i = dve.scalar_tensor_tensor(ml_w[d][:, h, :], mask_add[:, d, :], cst[:, 0, ds(c, 1), NH * d + h],
                                                 bc_ps[:, h, 0, :], ALU.add, ALU.add)
                i.then_inc(d_ready, 1)
                at_least(dve, num_mm, l - 1)
                dve.tensor_tensor(ml_qs[d][:], qT[:, :, ds(P * (c - TC), P)], bc_ps[:, :, 1, :], ALU.mult).then_inc(bc_read, 1)
                dve.wait_ge(w_ready, l + 1)
                dve.wait_ge(st_mm, l + 1)
                dve.tensor_tensor(ml_sw[d][:], st_ps[:], ml_w[d][:], ALU.mult).then_inc(sw_ready, 1)

            def ml_back(t, l, d, c):
                dve.wait_ge(kv_mm, t + 1)
                dve.wait_ge(bc_read, t + 1)
                if l is not None:
                    dve.wait_ge(num_mm, l + 1)
                at_least(dve, c_done, t)
                def state(heads):
                    for h in heads:
                        i = dve.scalar_tensor_tensor(ml_c[:, d, h, :], ml_c[:, d, h, :], decm[:, d, h:h + 1],
                                                     kv_ps[:, h // 2, h % 2, :], ALU.mult, ALU.add)
                    return i

                if l is None:
                    state(range(NH)).then_inc(c_done, 1)
                    return
                dn = den[:, d, :].rearrange("p (b j) -> p b j", b=2)
                fl = cst[:, 2, ds(c, 1), NH * d:NH * d + NH].rearrange("p o (b j) -> p (o b) j", b=2)
                dve.tensor_tensor(dn, num_ps[:, :, :, HD], fl, ALU.max).then_inc(den_seq, 1)
                state((0, 1))
                dve.wait_ge(den_seq, 3 * l + 1)
                dve.scalar_tensor_tensor(dn, num_ps[:, :, :, HD], -1.0, dn, ALU.mult, ALU.max).then_inc(den_seq, 1)
                state((2,))
                dve.wait_ge(den_seq, 3 * l + 2)
                dve.reciprocal(den[:, d, :], den[:, d, :]).then_inc(den_seq, 1)
                state((3,)).then_inc(c_done, 1)
                dve.wait_ge(den_seq, 3 * l + 3)
                at_least(dve, h_done, l)
                for h in range(NH):
                    o = h_ml[:, ds(c - TC, 1), HD * h:HD * (h + 1)].rearrange("p o n -> p (o n)")
                    i = dve.scalar_tensor_tensor(o, num_ps[:, h // 2, h % 2, 0:HD], den[:, d, h:h + 1], o, ALU.mult, ALU.add)
                i.then_inc(h_done, 1)

            dve.wait_ge(ml_zero, 5)
            scan_steps(dve, ml_front, ml_back)
            dve.wait_ge(ml_norm, 1)
            link(dve.tensor_reduce(hstat[:], h_sq[:].rearrange("p t (h n) -> p (t h) n", h=NH), AX.X, ALU.add))
            dve.tensor_scalar(hstat[:], hstat[:], 1.0 / HD, EPS, ALU.mult, ALU.add).then_inc(ml_norm, 1)
            split_lo(15)
            dve.wait_ge(ml_norm, 3)
            link(dve.reciprocal(hstat[:], hstat[:]))
            v4 = lambda v: v.rearrange("p t (h n) -> p (t h) n", h=NH)
            dve.tensor_tensor(v4(y_ml[:]), v4(h_ml[:]), hstat[:].unsqueeze(2).to_broadcast([P, TL * NH, HD]),
                              ALU.mult).then_inc(ml_norm, 1)
            dve.wait_ge(c_again, 1)
            link(dve.memset(c_st[:].bitcast(F32), 0.0))
            link(dve.tensor_copy(c_st[:, :, 0:2], c32[:, 0, :, :]))
            dve.tensor_tensor(c_st[:, :, 2:4], c32[:, 0, :, :], c_st[:, :, 0:2], ALU.subtract).then_inc(c_ready, 1)
            dve.wait_ge(ml_norm, 4)
            split_lo(16)
            split_lo(17)
            for n in range(17, AT["out", 0]):
                if n + 1 < AT["out", 0]:
                    split_lo(n + 1)
                kind, j = STREAM[n]
                if kind == "ada" or IN_UNITS[j][0] == "r":
                    continue
                name = IN_UNITS[j]
                p0, pairs = PAIRS[name]
                u = int(name[-1])
                for q in range(pairs):
                    p = p0 + q
                    src = psum[:, BANK * (p % TOK_BANKS):BANK * (p % TOK_BANKS + 1)].rearrange("p (r n) -> p r n", r=2)
                    if name[:2] == "gv":
                        if p % 2:
                            dve.wait_ge(tok_mm, p + 1)
                            dve.tensor_copy(gv[:, 2 * q:2 * q + 2, UW * u:UW * (u + 1)], src).then_inc(tok_dve, 1)
                    else:
                        dve.wait_ge(sig_done, p - PAIRS["o0"][0] + 1)
                        y = y_ml[:, 2 * q:2 * q + 2, UW * u:UW * (u + 1)]
                        dve.tensor_tensor(y, y, src, ALU.mult).then_inc(tok_dve, 1)
            dve.wait_ge(ada_cols, 24)
            b2 = col("b_ada")[:, 2 * KC:].unsqueeze(2).to_broadcast([P, 4 * KC, 2])
            link(dve.tensor_tensor(modc[:, 2 * KC:, :], modps[:, 2 * KC:, :], b2, ALU.add))
            for i in range(4):
                dve.wait_ge(z_abs, 16 + i + 1)
                bias = col("b_gla")[:, i:i + 1]
                dve.tensor_scalar(b_ctx[:, i, :], t_ctx(i % 2), bias, 0.0, ALU.add, ALU.min)
                dve.tensor_scalar(ht_f[:, i, CTX:ALL], t_lat(i % 2), bias, 0.0, ALU.add, ALU.min).then_inc(z_out, 1)
            dve.wait_ge(z_out, 4)
            for i in range(4):
                dve.wait_ge(la_tmp, i + 1)
                dve.tensor_tensor(b_ctx[:, i, :], b_ctx[:, i, :], l_ctx[:, i, :], ALU.subtract)
                link(dve.tensor_tensor(ht_f[:, i, CTX:ALL], ht_f[:, i, CTX:ALL], l_lat[:, i, :], ALU.subtract))
                for c in range(TA):
                    v = b_ctx[:, i, P * c:P * (c + 1)] if c < TC else ht_f[:, i, P * c:P * (c + 1)]
                    if i >= 2:
                        v = v[:, ::-1]
                    x = dve.tensor_tensor_scan(v, v, zero_r[:], 0.0, ALU.add, ALU.add)
                link(x)
                for q, pos in ((2, P // 2 - 1 if i < 2 else P // 2), (3, P - 1 if i < 2 else 0)):
                    dve.tensor_copy(gcol[:, q, i, 0:TC], b_ctx[:, i, pos::P])
                    x = dve.tensor_copy(gcol[:, q, i, TC:TA], ht_f[:, i, CTX + pos::P])
                x.then_inc(b_ready, 1)
            dve.wait_ge(b_ready, 4)
            dve.tensor_scalar(gcol[:, 0, :, :], gcol[:, 2, :, :], -1.0 / TAU, None, ALU.mult)
            dve.tensor_scalar(gcol[:, 1, :, :], gcol[:, 2, :, :], 1.0 / TAU, None, ALU.mult)
            dve.tensor_tensor(gcol[:, 4, :, :], gcol[:, 3, :, :], gcol[:, 2, :, :], ALU.subtract).then_inc(cols_dve, 1)

            def gla_front(t, l, d, c):
                dve.wait_ge(e_ready, t + 1)
                at_least(dve, gkt_mm, t - 1)
                dve.tensor_tensor(kx[d], gk[:, :, chunk_cols(c)], e_k[d], ALU.mult).then_inc(kx_ready, 1)
                if l is not None:
                    at_least(dve, go_mm, l - 1)
                    for h in range(2):
                        q = slice(64 * h, 64 * h + 64)
                        x = dve.tensor_tensor(qz[d][q, :, h, :], gq[q, :, ds(P * (c - TC), P)], e_q[d][q, :, :], ALU.mult)
                    x.then_inc(gx_ready, 1)

            def gla_middle(t, l, d, c):
                if l is not None:
                    dve.wait_ge(gst_mm, l + 1)
                    dve.tensor_tensor(g_a[d], gla_bank(d, 0, 512).rearrange("p (h t) -> p h t", h=NH),
                                      mask_add[:, d, :].unsqueeze(1).to_broadcast([P, NH, P]), ALU.mult).then_inc(a_ready, 1)

            def gla_back(t, l, d, c):
                dve.wait_ge(kvs_ready, t + 1)
                if l is not None:
                    dve.wait_ge(ps_ready, l + 1)
                at_least(dve, s_done, t - 1)
                for i in range(2):
                    x = dve.scalar_tensor_tensor(g_s[:, d, i, :], g_s[:, d, i, :], gcol[:, 3, 2 * d + i, ds(c, 1)],
                                                 gla_bank(d, 2, 4 * HD)[:, 2 * HD * i:2 * HD * (i + 1)], ALU.mult, ALU.add)
                x.then_inc(s_done, 1)
                if l is not None:
                    dve.wait_ge(go_mm, l + 1)
                    at_least(dve, og_done, l)
                    o = ht_f[:, ds(KC + c - TC, 1), CTX:CTX + GV_W]
                    dve.tensor_tensor(o, o, gla_bank(d, 3, 512).unsqueeze(1), ALU.add).then_inc(og_done, 1)

            dve.wait_ge(mask_exp, 1)
            dve.wait_ge(cols_act, 1)
            dve.wait_ge(zero_g, 1)
            scan_stages(dve, gla_front, gla_middle, gla_back)
            v4g = lambda v: v.rearrange("p t (h n) -> p (t h) n", h=NH)
            for half in range(2):
                dve.wait_ge(gla_sq, half + 1)
                i = dve.tensor_reduce(hstat[:, 16 * half:16 * half + 16], v4g(y_gla[:, 4 * half:4 * half + 4, :]), AX.X, ALU.add)
            link(i)
            dve.tensor_scalar(hstat[:], hstat[:], 1.0 / HD, EPS, ALU.mult, ALU.add).then_inc(gla_sq, 1)
            for u in range(2):
                o = ht_f[:, KC:2 * KC, CTX + UW * u:CTX + UW * (u + 1)]
                i = dve.tensor_tensor(o, o, ht_f[:, KC * u:KC * (u + 1), 0:UW], ALU.mult)
            link(i)
            dve.wait_ge(gla_sq, 4)
            link(dve.reciprocal(hstat[:], hstat[:]))
            for h in range(NH):
                dve.tensor_tensor(y_gla[:, :, HD * h:HD * (h + 1)], ht_f[:, KC:2 * KC, CTX + HD * h:CTX + HD * (h + 1)],
                                  hstat[:, h::NH].unsqueeze(2).to_broadcast([P, TL, HD]), ALU.mult).then_inc(gla_sq, 1)
            dve.memset(ones_m[:], 1.0)
            part = lambda j: modc[:, KC * j:KC * (j + 1), 0]
            dve.tensor_tensor(vec_c[:, 0, :], part(2), col("g_mix_post"), ALU.mult)
            dve.scalar_tensor_tensor(vec_c[:, 1, :], part(4), 1.0, col("g_ffn_pre"), ALU.add, ALU.mult)
            dve.tensor_copy(vec_c[:, 2, :], part(3))
            link(dve.tensor_tensor(vec_c[:, 3, :], part(5), col("g_ffn_post"), ALU.mult))

            def make_diag(dst, q):
                dve.tensor_tensor(dst[:], ident[:].unsqueeze(1).to_broadcast([P, KC, P]),
                                  vec_c[:, q, :].unsqueeze(2).to_broadcast([P, KC, P]), ALU.mult).then_inc(diag_ready, 1)

            dve.wait_ge(gla_sq, 4 + NH)
            make_diag(diag, 0)
            for k in range(KC):
                dve.wait_ge(yt_hi_ok, k + 1)
                dve.scalar_tensor_tensor(yt_lo[:, k, :], t_lat(k % 2), col("g_heads")[:, k:k + 1], yt_hi[:, k, :],
                                         ALU.mult, ALU.subtract).then_inc(yt_lo_ok, 1)
                if k == 2:
                    split_lo(AT["out", 0])
            split_lo(AT["out", 1])
            def y_part(q):
                p, u, j = PAIRS["out0"][0] + q, q // 4, q % 4
                dve.wait_ge(y_ssq, 2 * q + 2)
                dve.tensor_tensor(y_out[:, 2 * j:2 * j + 2, UW * u:UW * (u + 1)],
                                  psum[:, BANK * (p % TOK_BANKS):BANK * (p % TOK_BANKS + 1)].rearrange("p (r n) -> p r n", r=2),
                                  rowb[:, 0, UW * u:UW * (u + 1)].unsqueeze(1).to_broadcast([P, 2, UW]),
                                  ALU.mult).then_inc(tok_dve, 1)

            def y_stat(j):
                v = ssq[:, 2 * j:2 * j + 2]
                link(dve.tensor_reduce(v, hstat[:, 8 * j:8 * j + 8].rearrange("p (t u) -> p t u", u=4), AX.X, ALU.add))
                dve.tensor_scalar(v, v, 1.0 / D, EPS, ALU.mult, ALU.add).then_inc(y_mean, 1)

            def x_part(j):
                v = rstd[:, 2 * j:2 * j + 2]
                dve.wait_ge(y_std, j + 1)
                link(dve.reciprocal(v, v))
                dve.wait_ge(tok_dve, 18 + 12 + j + 1)
                for t in (2 * j, 2 * j + 1):
                    dve.scalar_tensor_tensor(x_res[:, t, :], y_out[:, t, :], rstd[:, t:t + 1], x_res[:, t, :],
                                             ALU.mult, ALU.add).then_inc(x1_ready, 1)

            def x_stat(j):
                v = ssq[:, TL + 2 * j:TL + 2 * j + 2]
                dve.wait_ge(x_ssq, 2 * j + 2)
                dve.tensor_scalar(v, v, 1.0 / D, EPS, ALU.mult, ALU.add).then_inc(x_mean, 1)

            def h2_part(j):
                v = rstd[:, TL + 2 * j:TL + 2 * j + 2]
                dve.wait_ge(x_std, j + 1)
                link(dve.reciprocal(v, v))
                for t in (2 * j, 2 * j + 1):
                    dve.scalar_tensor_tensor(h2[:, t, :], x_res[:, t, :], rstd[:, TL + t:TL + t + 1], rowb[:, 1, :],
                                             ALU.mult, ALU.mult).then_inc(h2_mid, 1)

            dve.wait_ge(rowb_ready, 1)
            for u in range(3):
                for q in range(4):
                    y_part(4 * u + q)
                if u < 2:
                    dve.wait_ge(row_mm, u + 1)
                    make_diag(diag, u + 1)
                    split_lo(AT["out", u + 2])
            dve.wait_ge(rowb_ready, 3)
            dve.wait_ge(pos_added, 2)
            y_part(12)
            y_stat(0)
            x_part(0)
            for j in range(4):
                if j < 3:
                    y_part(13 + j)
                    y_stat(j + 1)
                x_stat(j)
                if j < 3:
                    x_part(j + 1)
                h2_part(j)
            for t in range(TL - 2, TL):
                dve.wait_ge(h2_mid, t + 1)
                dve.tensor_tensor(h2[:, t, :], h2[:, t, :], rowb[:, 2, :], ALU.add).then_inc(h2_ready_2, 1)
            make_diag(diag2, 3)
            link(dve.memset(vals, 0.0))
            dve.wait_ge(lg_mm, TL)
            dve.tensor_copy(lg_t[0:N_EXP, :], psum[0:N_EXP, 4 * BANK:4 * BANK + SEQ]).then_inc(lg_copied, 1)
            dve.wait_ge(lg_tok, 1)
            lg = psum[:, 2 * BANK:2 * BANK + TL * N_EXP].rearrange("p (t e) -> p t e", t=TL)
            wide = lambda v: v.unsqueeze(2).to_broadcast([P, TL, N_EXP])
            link(dve.tensor_reduce(ssq[:, 0:TL], lg, AX.X, ALU.max))
            dve.tensor_tensor(e_lg, lg, wide(ssq[:, 0:TL]), ALU.subtract).then_inc(soft, 1)
            dve.wait_ge(soft, 2)
            link(dve.tensor_reduce(ssq[:, 0:TL], e_lg, AX.X, ALU.add))
            link(dve.reciprocal(ssq[:, 0:TL], ssq[:, 0:TL]))
            dve.tensor_tensor(e_lg, e_lg, wide(ssq[:, 0:TL]), ALU.mult).then_inc(soft, 1)
            def of_round(r):
                q = 32 * (r % 4)
                return left[r // 4][q:q + N_EXP, :], vals[q:q + N_EXP, r // 4, :]

            dve.wait_ge(aff_mm, 1)
            dve.wait_ge(left_zero, 16 + 1)
            dve.tensor_copy(of_round(0)[0], psum[0:N_EXP, 0:SEQ]).then_inc(topk, 1)
            for r in range(ROUNDS):
                rest, best = of_round(r)
                dve.wait_ge(topk, 2 * r + 1)
                dve.max(best, rest).then_inc(topk, 1)
                if r < ROUNDS - 1:
                    dve.wait_ge(topk, 2 * r + 2)
                    dve.match_replace(of_round(r + 1)[0], best, rest, -1.0).then_inc(topk, 1)
            dve.wait_ge(topk, 2 * ROUNDS)
            for g in range(ROUNDS // 4):
                i = dve.max_index(idx_u[:, g, :], vals[:, g, :], left[g][:])
            link(i)
            dve.tensor_copy(idx_f, idx_u[:].rearrange("p g j -> p (g j)")).then_inc(topk, 1)
            dve.wait_ge(sel_mm, 1)
            for q in range(4):
                to, cols_q = slice(32 * q, 32 * (q + 1)), slice(32 * q, 32 * q + N_EXP)
                dve.tensor_copy(gates[to, :], psum[0:2 * ROUNDS, cols_q])
                i = dve.tensor_copy(tokens[to, :], psum[0:2 * ROUNDS, P + 32 * q:P + 32 * q + N_EXP])
            i.then_inc(route_ready, 1)

            def e_split_lo(e, u):
                dve.wait_ge(e_hi_ok, EU * e + u + 1)
                dve.tensor_tensor(e_lo[u][:], e_raw[u][:], e_hi[u % EH][:], ALU.subtract).then_inc(e_lo_ok, 1)

            def xt_lo_part(e):
                dve.wait_ge(xt_hi_ok, e + 1)
                dve.tensor_tensor(xt_lo[:].rearrange("p k n -> p (k n)"), e_ps(6), xt_hi[:].rearrange("p k n -> p (k n)"),
                                  ALU.subtract).then_inc(xt_ok, 1)

            def hid_part(e, q):
                if q == 0:
                    dve.wait_ge(sg_ok, e + 1)
                dve.wait_ge(w_used, EU * e + 4 + q + 1 + EH)
                h = hid[:, UW * q:UW * (q + 1)]
                dve.tensor_tensor(h, h, quarter(2, q), ALU.mult).then_inc(hid_ok, 1)

            def hd_lo_part(e, q):
                dve.wait_ge(hd_hi_ok, 4 * e + q + 1)
                dve.tensor_tensor(hd_lo[:, 2 * q:2 * q + 2, :], quarter(0, q).rearrange("p (k n) -> p k n", k=2),
                                  hd_hi[:, 2 * q:2 * q + 2, :], ALU.subtract).then_inc(hd_ok, 1)

            def e_split_los(e, units):
                for u in units:
                    e_split_lo(e, u)

            def expert_dve(e, last):
                hid_part(e, 0)
                e_split_lo(e, 7)
                hid_part(e, 1)
                e_split_lo(e, 8)
                hd_lo_part(e, 0)
                hid_part(e, 2)
                e_split_lo(e, 9)
                hd_lo_part(e, 1)
                hid_part(e, 3)
                e_split_lo(e, 10)
                hd_lo_part(e, 2)
                if not last:
                    xt_lo_part(e + 1)
                hd_lo_part(e, 3)
                e_split_lo(e, 11)
                if not last:
                    e_split_los(e + 1, range(7))

            e_split_los(0, range(3))
            xt_lo_part(0)
            e_split_los(0, range(3, 7))
            with dve.Fori(0, N_EXP - 1) as e:
                expert_dve(e, False)
            expert_dve(N_EXP - 1, True)
            for j in range(4):
                pr = slice(2 * j, 2 * j + 2)
                dve.wait_ge(a_ssq, 4 * j + 2)
                dve.tensor_scalar(ssq[:, pr], ssq[:, pr], 1.0 / D, EPS, ALU.mult, ALU.add).then_inc(a_ssq, 1)
                dve.wait_ge(a_ssq, 4 * j + 4)
                link(dve.reciprocal(rstd[:, pr], rstd[:, pr]))
                for t in (2 * j, 2 * j + 1):
                    dve.scalar_tensor_tensor(acc[:, t, :], acc[:, t, :], rstd[:, t:t + 1], row_g2[:], ALU.mult, ALU.mult).then_inc(o_mid, 1)
                t = 2 * j
                dve.wait_ge(o_mid, t + 1)
                dve.tensor_tensor(x_res[:, t, :], x_res[:, t, :], acc[:, t, :], ALU.add).then_inc(o_ready, 1)

        @block.tensor
        def _(pe):
            def unit_ready(n):
                pe.wait_ge(hi_ready, n + 1)
                pe.wait_ge(lo_ready, n + 1)

            pe.wait_ge(c_ready, 1)

            def ada_to_cols(n):
                pe.wait_ge(ada_evac, n + 1)
                for j in range(2):
                    i = pe.matmul(modps[:, 2 * n + j, :], mod_rows[:, n % 2, P * j:P * (j + 1)], one_s[:],
                                  start=True, stop=True)
                i.then_inc(ada_cols, 1)

            def ada_unit(n):
                unit_ready(n)
                if n:
                    pe.wait_ge(ada_evac, n)
                hi, lo = split_bufs(n)
                for k in range(KC):
                    pe.matmul(ada_ps, c_st[:, k, :], hi[:, k, :], start=k == 0, stop=False)
                for k in range(KC):
                    i = pe.matmul(ada_ps, c_st[:, k, :], lo[:, k, :], start=False, stop=k == KC - 1)
                i.then_inc(ada_rows, 1)

            def x_block(k):
                s = k % 2
                if k >= 2:
                    pe.wait_ge(h32_ready, k - 1)
                for t in range(TA):
                    o = t_ctx(s)[:, P * t:P * (t + 1)] if t < TC else t_lat(s)[:, P * (t - TC):P * (t - TC + 1)]
                    i = pe.transpose(o, xs[:, t, P * k:P * (k + 1)], ident[:])
                i.then_inc(xt_ready, 1)

            pe.wait_ge(konst, 11)
            ada_unit(0)
            pe.wait_ge(grid_ok, 2)
            pe.wait_ge(s_pos, 48)
            rows = slice(0, SEQ // GRID_W)
            for t in range(TL):
                if t >= 2:
                    pe.wait_ge(xn_ready, t - 1)
                pe.matmul(psum[:, BANK * (t % 2):BANK * (t % 2 + 1)], grid_sel[rows, t, :, :], pos_r[rows, :],
                          start=True, stop=True).then_inc(pos_mm, 1)
            for n in range(1, 8):
                ada_unit(n)
                ada_to_cols(n - 1)
                if n == 5:
                    pe.wait_ge(scaled, 1 + TA)
                    x_block(0)
                    x_block(1)
            ada_to_cols(7)
            for k in range(2, KC):
                x_block(k)
            pe.wait_ge(h32_ready, KC - 1)

            def t_tile(i, n, j, has_ctx):
                s, m = i % 2, n % 2
                c = slice(P * j, P * (j + 1))
                for k in range(KC):
                    if i == 0:
                        pe.wait_ge(h_ready, k + 1)
                    for w, h in ((w_hi, h_hi), (w_hi, h_lo), (w_lo, h_hi)):
                        a, z = k == 0 and w is w_hi and h is h_hi, k == KC - 1 and w is w_lo
                        for q in range(2):
                            last = pe.matmul(t_lat(s)[:, BANK * q:BANK * (q + 1)], w[m][:, k, c],
                                             h[:, k, CTX + BANK * q:CTX + BANK * (q + 1)], start=a, stop=z)
                        if has_ctx:
                            last = pe.matmul(t_ctx(s), w[m][:, k, c], h[:, k, 0:CTX], start=a, stop=z)
                return last

            def t_unit(n, i0, has_ctx, free):
                unit_ready(n)
                for j in range(2):
                    if free is not None:
                        pe.wait_ge(free, i0 + j - 1 - (2 if free is conv_free else 0))
                    last = t_tile(i0 + j, n, j, has_ctx)
                    if j == 0:
                        last.then_inc(tile_mm, 1)
                last.then_inc(tile_mm, 1)

            t_unit(8, 0, True, None)
            t_unit(9, 2, True, g_free)
            t_unit(10, 4, True, conv_free)
            t_unit(11, 6, False, conv_free)
            t_unit(12, 8, False, conv_free)
            pe.wait_ge(row_act, 4)
            for q, src in enumerate((row_a, row_f, row_m)):
                for c in range(TA):
                    o = 7 * BANK + (q * TA + c) * 2 * NH
                    last = pe.matmul(psum[:, o:o + 2 * NH], src[:, P * c:P * (c + 1)], sel_s[:], start=True, stop=True)
            last.then_inc(stat_mm, 1)

            def tok_unit(name, n, x_hi, x_lo, t0):
                unit_ready(n)
                p0, pairs = PAIRS[name]
                for j in range(pairs):
                    p = p0 + j
                    if p >= TOK_BANKS:
                        pair_out(pe, p - TOK_BANKS)
                    for r in range(2):
                        c = slice(P * (t0 + 2 * j + r), P * (t0 + 2 * j + r + 1))
                        o = tok_ps(p, r)
                        for k in range(KC):
                            pe.matmul(o, x_hi[:, k, c], w_hi[n % 2][:, k, :], start=k == 0, stop=False)
                            pe.matmul(o, x_lo[:, k, c], w_hi[n % 2][:, k, :], start=False, stop=False)
                            last = pe.matmul(o, x_hi[:, k, c], w_lo[n % 2][:, k, :], start=False, stop=k == KC - 1)
                    last.then_inc(tok_mm, 1)

            pe.wait_ge(conv_free, 8)
            pe.wait_ge(stat_ready, 1)
            tok_unit("v0", 13, h_hi, h_lo, 0)
            tok_unit("v1", 14, h_hi, h_lo, 0)
            def ml_front(t, l, d, c):
                pe.wait_ge(kst_ready, t + 1)
                at_least(pe, bc_read, t)
                for h in range(NH):
                    i = pe.matmul(bc_ps[:, h, :, :], sel_r[:, NH * d + h, :], rows_na[:, :, chunk_cols(c)], start=True, stop=True)
                i.then_inc(bc_mm, 1)
                if l is not None:
                    at_least(pe, sw_ready, l)
                    for h in range(NH):
                        i = pe.matmul(st_ps[:, h, :], ml_ks[d][:, h, :], qT[:, h, ds(P * (c - TC), P)], start=True, stop=True)
                    i.then_inc(st_mm, 1)
                at_least(pe, kh_ready, t)
                for h in range(NH):
                    i = pe.transpose(kt_ps[:, h, :], ml_ks[d][:, h, :], ident[:])
                i.then_inc(kt_mm, 1)

            def ml_back(t, l, d, c):
                pe.wait_ge(kh_ready, t + 1)
                at_least(pe, c_done, t)
                vc = lambda h: v_ext[:, ds(c, 1), h, :]
                for h in range(NH):
                    i = pe.matmul(kv_ps[:, h // 2, h % 2, :], ml_kh[d][:, h, :], vc(h), start=True, stop=True)
                i.then_inc(kv_mm, 1)
                if l is None:
                    return
                pe.wait_ge(sw_ready, l + 1)
                at_least(pe, h_done, l)
                for h in range(NH):
                    o = num_ps[:, h // 2, h % 2, :]
                    pe.matmul(o, ml_sw[d][:, h, :], vc(h), start=True, stop=False)
                    i = pe.matmul(o, ml_qs[d][:, h, :], ml_c[:, d, h, :], start=False, stop=True)
                i.then_inc(num_mm, 1)

            pe.wait_ge(ml_zero, 5)
            pe.wait_ge(row_dve, 2)
            pe.wait_ge(ml_zero_d, 16 + 2)
            pe.wait_ge(conv_act, 8)
            pe.wait_ge(tok_act, 5)
            pe.wait_ge(tok_dve, 5)
            pe.wait_ge(ones_set, 2)
            scan_steps(pe, ml_front, ml_back)
            pe.wait_ge(h_done, 2 * TL)
            pe.wait_ge(c_done, 2 * TA)
            t_unit(15, 10, True, None)
            unit_ready(16)
            for i in (12, 13):
                pe.wait_ge(g_free, i - 9)
                t_tile(i, 16, i - 12, False).then_inc(tile_mm, 1)
            pe.wait_ge(g_free, 6)
            pe.wait_ge(c_ready, 2)
            for n in range(17, AT["out", 0]):
                kind, j = STREAM[n]
                if kind == "in":
                    name = IN_UNITS[j]
                    tok_unit(name, n, h_hi, h_lo, 0 if name[:2] == "gv" else TC)
                    continue
                unit_ready(n)
                pe.wait_ge(ada_evac, j)
                o = psum[:, 6 * BANK:6 * BANK + UW]
                for k in range(KC):
                    pe.matmul(o, c_st[:, k, :], w_hi[n % 2][:, k, :], start=k == 0, stop=False)
                for k in range(KC):
                    i = pe.matmul(o, c_st[:, k, :], w_lo[n % 2][:, k, :], start=False, stop=k == KC - 1)
                i.then_inc(ada_rows, 1)
                if j > 8:
                    ada_to_cols(j - 1)
            ada_to_cols(23)
            pair_out(pe, PAIRS["r1"][0] + 3)
            for i in range(4):
                if i >= 2:
                    pe.wait_ge(z_out, i - 1)
                w = col("w_gla2")[:, P * i:P * (i + 1)]
                for q in range(2):
                    pe.matmul(t_lat(i % 2)[:, BANK * q:BANK * (q + 1)], w, gate_rows[:, CTX + BANK * q:CTX + BANK * (q + 1)],
                              start=True, stop=True)
                pe.matmul(t_ctx(i % 2), w, gate_rows[:, 0:CTX], start=True, stop=True).then_inc(tile_mm, 1)

            def gla_front(t, l, d, c):
                pe.wait_ge(kx_ready, 16 + t + 1)
                at_least(pe, gkh_ready, t - 1)
                for i in range(2):
                    x = pe.transpose(gla_bank(d, 1, 2 * P)[:, P * i:P * (i + 1)], kx[d][:, i, :], ident[:])
                x.then_inc(gkt_mm, 1)
                if l is not None:
                    pe.wait_ge(gx_ready, l + 1)
                    at_least(pe, a_ready, l - 1)
                    for i in range(2):
                        x = pe.matmul(gla_bank(d, 0, 512)[:, 2 * P * i:2 * P * (i + 1)], kx[d][:, i, :],
                                      qz[d][:, i, :, :], start=True, stop=True)
                    x.then_inc(gst_mm, 1)

            def gla_back(t, l, d, c):
                pe.wait_ge(gkh_ready, t + 1)
                at_least(pe, s_done, t - 1)
                for i in range(2):
                    x = pe.matmul(gla_bank(d, 2, 4 * HD)[:, 2 * HD * i:2 * HD * (i + 1)], k_tok[d][:, i, :],
                                  gv[:, ds(c, 1), 2 * HD * i:2 * HD * (i + 1)], start=True, stop=True)
                x.then_inc(gkv_mm, 1)
                if l is None:
                    return
                pe.wait_ge(a_ready, l + 1)
                pe.wait_ge(ps_ready, l + 1)
                at_least(pe, og_done, l - 1)
                for h in range(NH):
                    o = gla_bank(d, 3, 512)[:, HD * h:HD * (h + 1)]
                    pe.matmul(o, g_a[d][:, h, :], gv[:, ds(c, 1), HD * h:HD * (h + 1)], start=True, stop=False)
                    x = pe.matmul(o, qz[d][:, h // 2, h % 2, :], g_ps[:, d, h // 2, HD * (h % 2):HD * (h % 2 + 1)],
                                  start=False, stop=True)
                x.then_inc(go_mm, 1)

            pe.wait_ge(z_out, 4)
            pe.wait_ge(tok_dve, 18)
            pe.wait_ge(zero_g, 1)
            scan_steps(pe, gla_front, gla_back)
            pe.wait_ge(og_done, 2 * TL)
            pe.wait_ge(s_done, 2 * TA)
            for k in range(KC):
                if k >= KC // 2:
                    pe.wait_ge(gla_sq, 4 + k - KC // 2 + 1)
                at_least(pe, yt_lo_ok, k - 1)
                y = y_ml if k < KC // 2 else y_gla
                for t in range(TL):
                    i = pe.transpose(t_lat(k % 2)[:, P * t:P * (t + 1)], y[:, t, P * (k % 4):P * (k % 4 + 1)], ident[:])
                i.then_inc(yt_mm, 1)

            def row_product(q, d):
                pe.wait_ge(diag_ready, q + 1)
                at_least(pe, rowb_ready, q)
                for b in range(2):
                    i = pe.matmul(psum[:, (6 + b) * BANK:(7 + b) * BANK], ones_m[:], d[:, 4 * b:4 * b + 4, :], start=True, stop=True)
                i.then_inc(row_mm, 1)

            pe.wait_ge(yt_lo_ok, KC)
            w_r = col("w_router").rearrange("p (k e) -> p k e", k=KC)

            def logits(t):
                pe.wait_ge(h2t_ready, t + 1)
                for k in range(KC):
                    i = pe.matmul(psum[0:N_EXP, 4 * BANK + P * t:4 * BANK + P * (t + 1)], w_r[:, k, :], h2t[t % 2][:, k, :],
                                  start=k == 0, stop=k == KC - 1)
                i.then_inc(lg_mm, 1)

            def route(j):
                for t in (2 * j, 2 * j + 1):
                    h2_complete(pe, t)
                    at_least(pe, h2t_ready, t)
                    for k in range(KC):
                        i = pe.transpose(e_ps(6)[:, P * k:P * (k + 1)], h2[:, t, P * k:P * (k + 1)], ident[:])
                    i.then_inc(h2t_mm, 1)
                    if t:
                        logits(t - 1)

            row_product(0, diag)
            for u in range(3):
                tok_unit(f"out{u}", AT["out", u], yt_hi, yt_lo, 0)
                if u < 2:
                    row_product(u + 1, diag)
            pe.wait_ge(rowb_ready, 3)
            tok_unit("out3", AT["out", 3], yt_hi, yt_lo, 0)
            for j in range(4):
                route(j)
            logits(TL - 1)
            pe.wait_ge(lg_copied, 1)
            for t in range(TL):
                i = pe.transpose(psum[:, 2 * BANK + N_EXP * t:2 * BANK + N_EXP * (t + 1)], lg_t[0:N_EXP, P * t:P * (t + 1)],
                                 ident[0:N_EXP, 0:N_EXP])
            i.then_inc(lg_tok, 1)
            row_product(3, diag2)
            pe.wait_ge(soft, 3)
            for t in range(TL):
                i = pe.transpose(psum[0:N_EXP, P * t:P * (t + 1)], e_lg[:, t, :], ident[:])
            i.then_inc(aff_mm, 1)
            pe.nop().then_inc(w_used, EH)
            pe.wait_ge(topk, 2 * ROUNDS + 1)
            pe.transpose(psum[0:2 * ROUNDS, 0:P], vals.rearrange("p g j -> p (g j)"), ident[:])
            pe.transpose(psum[0:2 * ROUNDS, P:2 * P], idx_f, ident[:]).then_inc(sel_mm, 1)

            def e_unit(e, u, x_hi, x_lo, o):
                pe.wait_ge(e_lo_ok, EU * e + u + 1)
                hi, lo = e_hi[u % EH], e_lo[u]
                if 4 <= u < 8:
                    for k in range(KC):
                        c = slice(UW * k, UW * (k + 1))
                        pe.matmul(o, x_hi[:, k, :], hi[:, c], start=k == 0, stop=False)
                        pe.matmul(o, x_lo[:, k, :], hi[:, c], start=False, stop=False)
                        i = pe.matmul(o, x_hi[:, k, :], lo[:, c], start=False, stop=k == KC - 1)
                else:
                    for j in range(2):
                        k = 2 * (u % 4) + j
                        for x, w in ((x_hi, hi), (x_hi, lo), (x_lo, hi)):
                            a, z = k == 0 and x is x_hi and w is hi, k == KC - 1 and x is x_lo
                            for b in range(2):
                                i = pe.matmul(o[:, BANK * b:BANK * (b + 1)], x[:, k, :], w[:, D * j + BANK * b:D * j + BANK * (b + 1)],
                                              start=a, stop=z)
                i.then_inc(w_used, 1)

            def x_transposes(e):
                pe.wait_ge(gathered, 16 * e + 16)
                for k in range(KC):
                    i = pe.transpose(e_ps(6)[:, P * k:P * (k + 1)], x_tok[:, P * k:P * (k + 1)], ident[:])
                i.then_inc(xt_mm, 1)

            def hid_transposes(e, q):
                pe.wait_ge(hid_ok, 4 * e + q + 1)
                for j in range(2):
                    c = UW * q + P * j
                    i = pe.transpose(quarter(0, q)[:, P * j:P * (j + 1)], hid[:, c:c + P], ident[:])
                i.then_inc(hd_mm, 1)

            def expert_pe(e, last):
                pe.wait_ge(xt_ok, e + 1)
                for u in range(4):
                    e_unit(e, u, xt_hi, xt_lo, e_ps(0))
                for q in range(4):
                    e_unit(e, 4 + q, xt_hi, xt_lo, quarter(2, q))
                    if q:
                        hid_transposes(e, q - 1)
                if not last:
                    x_transposes(e + 1)
                hid_transposes(e, 3)
                pe.wait_ge(y_free, e + 1)
                for u in range(8, EU):
                    pe.wait_ge(hd_ok, 4 * e + u - 8 + 1)
                    e_unit(e, u, hd_hi, hd_lo, e_ps(4))

            pe.wait_ge(rowb_ready, 4)
            pe.wait_ge(route_ready, 1)
            x_transposes(0)
            with pe.Fori(0, N_EXP - 1) as e:
                expert_pe(e, False)
            expert_pe(N_EXP - 1, True)


def small_array(a):
    def cols(v):
        return v.reshape(-1, P).T

    c2 = np.stack([a["c"][0], a["c_ctx"]], -1).reshape(KC, P, 2).transpose(1, 0, 2).reshape(P, -1)
    bg = np.zeros((P, 2), np.float32)
    g = a["b_ml_gates"][0].reshape(4, NH)
    for kind in range(2):
        bg[0:NH, kind], bg[32:32 + NH, kind] = g[kind], g[2 + kind]
    w2 = np.zeros((P, 2 * GK_W), np.float32)
    for d in range(2):
        w2[64 + RANK * d:64 + RANK * (d + 1), GK_W * d:GK_W * (d + 1)] = a["w_gla_a2"][0, d]
    parts = {
        "c": c2, "b_ada": cols(a["b_ada"][0]), "g_mix_pre": cols(a["g_mix_pre"][0]),
        "g_mix_post": cols(a["g_mix_post"][0]), "g_ffn_pre": cols(a["g_ffn_pre"][0]),
        "g_ffn_post": cols(a["g_ffn_post"][0]),
        "g_heads": cols(np.concatenate([a["g_ml_norm"][0], a["g_gla_norm"][0]])),
        "conv": a["conv_qk"][0].reshape(3 * 2 * NH, P).T, "b_gates": bg, "b_gla": cols(a["b_gla_a"][0].reshape(-1)),
        "w_gla2": w2,
        "w_router": a["w_router"][0].reshape(KC, P, N_EXP).transpose(1, 0, 2).reshape(P, -1),
    }
    return np.ascontiguousarray(np.concatenate([parts[n] for n in COLS], 1))


def unit_arrays(a):
    w = a["w_in"][0]
    g = np.zeros((D, UW), np.float32)
    for d in range(2):
        for kind in range(2):
            o = OFF_G + NH * (2 * d + kind)
            g[:, P * kind + 32 * d:P * kind + 32 * d + NH] = w[:, o:o + NH]
    g[:, 64:64 + 2 * RANK] = w[:, OFF_A:OFF_A + 2 * RANK]
    starts = [OFF_K, OFF_K + UW, OFF_Q, OFF_Q + UW, OFF_V, OFF_V + UW, OFF_GK, OFF_GQ, OFF_GV, OFF_GV + UW,
              OFF_O, OFF_O + UW, OFF_R, OFF_R + UW]
    units = [g] + [w[:, o:o + UW] for o in starts]
    pack = lambda u: u.reshape(KC, P, UW).transpose(1, 0, 2).reshape(P, KC * UW)
    wo = a["w_out"][0]
    return (np.ascontiguousarray(np.stack([pack(u) for u in units])),
            np.ascontiguousarray(np.stack([pack(wo[:, UW * j:UW * (j + 1)]) for j in range(D // UW)])))


def pos_tables():
    quarter = D // 4
    freq = np.power(np.float32(POS_BASE), -np.arange(quarter, dtype=np.float32) / np.float32(quarter)).astype(np.float32)
    r = np.arange(SEQ // GRID_W, dtype=np.float32)[:, None] * freq
    c = np.arange(GRID_W, dtype=np.float32)[:, None] * freq
    return (np.concatenate([np.sin(r), np.cos(r)], -1).astype(np.float32),
            np.concatenate([np.sin(c), np.cos(c)], -1).astype(np.float32))


def arrays_of(inputs):
    a = {k: np.asarray(v) for k, v in inputs.items()}
    w_in_units, w_out_units = unit_arrays(a)
    pos_row, pos_col = pos_tables()
    return {
        "x": np.ascontiguousarray(a["x"][0]), "ctx": np.ascontiguousarray(a["ctx"][0]),
        "small": small_array(a), "w_ada": np.ascontiguousarray(a["w_ada"][0]),
        "w_in_units": w_in_units, "w_out_units": w_out_units, "pos_row": pos_row, "pos_col": pos_col,
        "w_e_gate": np.ascontiguousarray(a["w_e_gate"][0]), "w_e_up": np.ascontiguousarray(a["w_e_up"][0]),
        "w_e_down": np.ascontiguousarray(a["w_e_down"][0]),
    }


def kernel(**inputs):
    import concourse.bacc as bacc
    from concourse.bass_utils import run_bass_kernel_spmd

    nc = bacc.Bacc("TRN2", target_bir_lowering=False, num_devices=1)
    arrays = arrays_of(inputs)
    I = {n: nc.dram_tensor(n, a.shape, mybir.dt.from_np(a.dtype), kind="ExternalInput").ap() for n, a in arrays.items()}
    out = nc.dram_tensor("out", [SEQ, D], F32, kind="ExternalOutput").ap()
    build(nc, I, out)
    r = run_bass_kernel_spmd(nc, [arrays], core_ids=[0])
    return r.results[0]["out"].reshape(1, SEQ, D)
```
